# Optimizing a Trainium2 kernel written in Bass

```python
import math, functools
import jax, jax.numpy as jnp
from jax import lax
import numpy as np

D_MODEL = 1024
BATCH = 1
SEQ = 128
DEPTH = 2
DEC_BATCH = 1
DEC_SEQ = 256
PAST_LEN = 128

GRID_W = 64
CHUNK = 128
Q_BLOCK = 128
EPS = 1e-6
ALPHA = (2 * DEPTH) ** 0.25
BETA = (8 * DEPTH) ** -0.25
W_A = D_MODEL // 2
DK_A = 64
DV_A = 64
H_A = W_A // DV_A
HD_B = 64
H_B = (D_MODEL // 2) // HD_B
KV_B = H_B // 4
ROPE_THETA = 10000.0
D_INNER = 2 * D_MODEL
HD_C = 64
H_C = D_INNER // HD_C
NG_C = 4
HPG_C = H_C // NG_C
D_STATE = 128
CONV_W = 3
CONV_CH = D_INNER + 2 * NG_C * D_STATE
D_FF = 2816
N_EXPERTS = 8
TOP_K = 2
D_FF_E = 1408
MIX_SIZES = (W_A, W_A, W_A, W_A, 4 * H_A, H_B * HD_B, KV_B * HD_B, KV_B * HD_B)
SSD_SIZES = (D_INNER, CONV_CH, 2 * H_C)

kernel_name = 'hybrid_mlstm_gqa_ssd_moe_diffusion_step'

def split_cols(x, sizes):
    idx = np.cumsum(sizes)[:-1].tolist()
    return jnp.split(x, idx, axis=-1)

def flip(a):
    return jnp.flip(a, axis=1)

def to_chunks(a):
    b, s = a.shape[:2]
    return a.reshape(b, s // CHUNK, CHUNK, *a.shape[2:]).swapaxes(0, 1)

def from_chunks(a):
    nc, b, l = a.shape[:3]
    return a.swapaxes(0, 1).reshape(b, nc * l, *a.shape[3:])

def layer_norm(x, g, b):
    xf = x.astype(jnp.float32)
    mu = xf.mean(-1, keepdims=True)
    var = jnp.mean(jnp.square(xf - mu), -1, keepdims=True)
    return ((xf - mu) * lax.rsqrt(var + EPS) * g.astype(jnp.float32) + b.astype(jnp.float32)).astype(x.dtype)

def rms_norm(x, g):
    xf = x.astype(jnp.float32)
    return (xf * lax.rsqrt(jnp.mean(jnp.square(xf), -1, keepdims=True) + EPS) * g.astype(jnp.float32)).astype(x.dtype)

def ada_mods(cvec, w, b):
    m = jax.nn.silu(cvec) @ w + b
    return [t[:, None, :] for t in jnp.split(m, 6, axis=-1)]

def axial_rope(x, row, col):
    half = x.shape[-1] // 2
    nf = half // 2
    inv = ROPE_THETA ** (-jnp.arange(nf, dtype=jnp.float32) / nf)

    def rot(xh, p):
        ang = p.astype(jnp.float32)[:, None] * inv
        cos, sin = jnp.cos(ang)[None, :, None, :], jnp.sin(ang)[None, :, None, :]
        x1, x2 = xh[..., :nf], xh[..., nf:]
        return jnp.concatenate([x1 * cos - x2 * sin, x2 * cos + x1 * sin], axis=-1)

    xf = x.astype(jnp.float32)
    return jnp.concatenate([rot(xf[..., :half], row), rot(xf[..., half:], col)], axis=-1).astype(x.dtype)

def block_attention(q, k, v):
    bsz, s_len = q.shape[:2]
    qb = q.reshape(bsz, s_len // Q_BLOCK, Q_BLOCK, *q.shape[2:]).swapaxes(0, 1)
    scale = HD_B ** -0.5

    def one(qblk):
        s = jnp.einsum('bqhgd,bkhd->bhgqk', qblk, k).astype(jnp.float32) * scale
        p = jax.nn.softmax(s, axis=-1).astype(v.dtype)
        return jnp.einsum('bhgqk,bkhd->bqhgd', p, v)

    o = lax.map(one, qb)
    return o.swapaxes(0, 1).reshape(bsz, s_len, -1)

def mlstm_scan(q, k, v, li, lf, c0, n0, m0):
    tril = jnp.tril(jnp.ones((CHUNK, CHUNK), bool))

    def step(carry, inp):
        c, n, m = carry
        qc, kc, vc, lic, lfc = inp
        b = jnp.cumsum(lfc, axis=1)
        a = b + m[:, None]
        dmat = jnp.where(tril[None, :, :, None], b[:, :, None] - b[:, None] + lic[:, None], -jnp.inf)
        mt = jnp.maximum(a, dmat.max(axis=2))
        w_in = jnp.exp(dmat - mt[:, :, None])
        w_st = jnp.exp(a - mt)
        sc = jnp.einsum('bthd,bshd->btsh', qc, kc) * w_in
        num = jnp.einsum('btsh,bshv->bthv', sc, vc) + w_st[..., None] * jnp.einsum('bhdv,bthd->bthv', c, qc)
        den = sc.sum(2) + w_st * jnp.einsum('bhd,bthd->bth', n, qc)
        h = num / jnp.maximum(jnp.abs(den), jnp.exp(-mt))[..., None]
        bl = b[:, -1]
        ls = bl[:, None] - b + lic
        m_new = jnp.maximum(bl + m, ls.max(1))
        ws = jnp.exp(ls - m_new[:, None])
        decay = jnp.exp(bl + m - m_new)
        c_new = decay[..., None, None] * c + jnp.einsum('bsh,bshd,bshv->bhdv', ws, kc, vc)
        n_new = decay[..., None] * n + jnp.einsum('bsh,bshd->bhd', ws, kc)
        return (c_new, n_new, m_new), h

    (c, n, m), h = lax.scan(step, (c0, n0, m0), (to_chunks(q), to_chunks(k), to_chunks(v), to_chunks(li), to_chunks(lf)))
    return from_chunks(h), c, n, m

def ssd_scan(x, dt, a_coef, bm, cm, s0):
    tril = jnp.tril(jnp.ones((CHUNK, CHUNK), bool))

    def step(s, inp):
        xc, dtc, bc, cc = inp
        cum = jnp.cumsum(dtc * a_coef, axis=1)
        seg = jnp.where(tril[None, :, :, None, None], cum[:, :, None] - cum[:, None], -jnp.inf)
        cb = jnp.einsum('btgn,bsgn->btsg', cc, bc)
        w = cb[..., None] * jnp.exp(seg) * dtc[:, None]
        y = jnp.einsum('btsgr,bsgrp->btgrp', w, xc) + jnp.einsum('bgrpn,btgn->btgrp', s, cc) * jnp.exp(cum)[..., None]
        ws = jnp.exp(cum[:, -1:] - cum) * dtc
        s_new = jnp.exp(cum[:, -1])[..., None, None] * s + jnp.einsum('bsgr,bsgrp,bsgn->bgrpn', ws, xc, bc)
        return s_new, y

    s, y = lax.scan(step, s0, (to_chunks(x), to_chunks(dt), to_chunks(bm), to_chunks(cm)))
    return from_chunks(y), s

def depthwise_conv_centred(x, w):
    return lax.conv_general_dilated(x, w[:, None, :], window_strides=(1,), padding=[(CONV_W // 2, CONV_W // 2)],
                                    dimension_numbers=('NWC', 'WIO', 'NWC'), feature_group_count=x.shape[-1])

def mlstm_attn_mixer(u, w_in, b_gates, norm_g, q_g, k_g, w_out, pos, ctx):
    f32 = jnp.float32
    bsz, s_len, _ = u.shape
    qm, km, vm, om, gates, qa, ka, va = split_cols(u @ w_in, MIX_SIZES)
    qm = qm.reshape(bsz, s_len, H_A, DK_A).astype(f32) * DK_A ** -0.5
    km = km.reshape(bsz, s_len, H_A, DK_A).astype(f32)
    vm = vm.reshape(bsz, s_len, H_A, DV_A).astype(f32)
    gates = gates.reshape(bsz, s_len, 4, H_A).astype(f32) + b_gates.astype(f32)
    li_f, lf_f = gates[:, :, 0], jax.nn.log_sigmoid(gates[:, :, 1])
    li_b, lf_b = gates[:, :, 2], jax.nn.log_sigmoid(gates[:, :, 3])
    if ctx is None:
        c0 = jnp.zeros((bsz, 2, H_A, DK_A, DV_A), f32)
        n0 = jnp.zeros((bsz, 2, H_A, DK_A), f32)
        m0 = jnp.zeros((bsz, 2, H_A), f32)
    else:
        c0, n0, m0 = (t.astype(f32) for t in ctx[2:])
    h_f, c_f, n_f, m_f = mlstm_scan(qm, km, vm, li_f, lf_f, c0[:, 0], n0[:, 0], m0[:, 0])
    h_b, c_b, n_b, m_b = mlstm_scan(flip(qm), flip(km), flip(vm), flip(li_b), flip(lf_b), c0[:, 1], n0[:, 1], m0[:, 1])
    h = h_f + flip(h_b)
    mu = h.mean(-1, keepdims=True)
    var = jnp.mean(jnp.square(h - mu), -1, keepdims=True)
    h = ((h - mu) * lax.rsqrt(var + EPS)).reshape(bsz, s_len, W_A)
    h = h * norm_g.astype(f32) * jax.nn.sigmoid(om.astype(f32))
    qa = rms_norm(qa.reshape(bsz, s_len, H_B, HD_B), q_g)
    ka = rms_norm(ka.reshape(bsz, s_len, KV_B, HD_B), k_g)
    va = va.reshape(bsz, s_len, KV_B, HD_B)
    if ctx is None:
        k_all, v_all = ka, va
    else:
        row, col = pos
        qa = axial_rope(qa, row, col)
        k_all = jnp.concatenate([ctx[0], axial_rope(ka, row, col)], axis=1)
        v_all = jnp.concatenate([ctx[1], va], axis=1)
    o = block_attention(qa.reshape(bsz, s_len, KV_B, H_B // KV_B, HD_B), k_all, v_all)
    y = jnp.concatenate([h.astype(u.dtype), o], axis=-1) @ w_out
    if ctx is None:
        dt = u.dtype
        state = (ka, va, jnp.stack([c_f, c_b], 1).astype(dt), jnp.stack([n_f, n_b], 1).astype(dt),
                 jnp.stack([m_f, m_b], 1).astype(dt))
    else:
        state = None
    return y, state

def ssd_mixer(u, w_in, conv_w, conv_b, dt_bias, a_log, d_skip, norm_g, w_out, s_init):
    f32 = jnp.float32
    bsz, s_len, _ = u.shape
    z, xbc, dt = split_cols(u @ w_in, SSD_SIZES)
    xbc = jax.nn.silu(depthwise_conv_centred(xbc, conv_w) + conv_b)
    xs, bm, cm = split_cols(xbc.astype(f32), (D_INNER, NG_C * D_STATE, NG_C * D_STATE))
    xs = xs.reshape(bsz, s_len, NG_C, HPG_C, HD_C)
    bm = bm.reshape(bsz, s_len, NG_C, D_STATE)
    cm = cm.reshape(bsz, s_len, NG_C, D_STATE)
    dt = jax.nn.softplus(dt.astype(f32).reshape(bsz, s_len, 2, H_C) + dt_bias.astype(f32))
    dt = dt.reshape(bsz, s_len, 2, NG_C, HPG_C)
    a_coef = -jnp.exp(a_log.astype(f32)).reshape(2, NG_C, HPG_C)
    if s_init is None:
        s0 = jnp.zeros((bsz, 2, NG_C, HPG_C, HD_C, D_STATE), f32)
    else:
        s0 = s_init.astype(f32).reshape(bsz, 2, NG_C, HPG_C, HD_C, D_STATE)
    y_f, s_f = ssd_scan(xs, dt[:, :, 0], a_coef[0], bm, cm, s0[:, 0])
    y_b, s_b = ssd_scan(flip(xs), flip(dt[:, :, 1]), a_coef[1], flip(bm), flip(cm), s0[:, 1])
    y = y_f + flip(y_b) + d_skip.astype(f32).reshape(NG_C, HPG_C)[..., None] * xs
    y = y.reshape(bsz, s_len, D_INNER) * jax.nn.silu(z.astype(f32))
    yg = y.reshape(bsz, s_len, NG_C, D_INNER // NG_C)
    yg = yg * lax.rsqrt(jnp.mean(jnp.square(yg), -1, keepdims=True) + EPS)
    y = yg.reshape(bsz, s_len, D_INNER) * norm_g.astype(f32)
    out = y.astype(u.dtype) @ w_out
    if s_init is None:
        state = jnp.stack([s_f, s_b], 1).reshape(bsz, 2, H_C, HD_C, D_STATE).astype(u.dtype)
    else:
        state = None
    return out, state

def swiglu(u, w1, w3, w2):
    return (jax.nn.silu(u @ w1) * (u @ w3)) @ w2

def moe_swiglu(u, router_w, router_b, w1, w3, w2):
    bsz, s_len, d = u.shape
    t = u.reshape(-1, d)
    logits = (t @ router_w).astype(jnp.float32) + router_b.astype(jnp.float32)
    top_v, top_i = lax.top_k(logits, TOP_K)
    probs = jax.nn.softmax(top_v, axis=-1)
    gate = jnp.einsum('tk,tke->te', probs, jax.nn.one_hot(top_i, N_EXPERTS, dtype=jnp.float32)).astype(u.dtype)
    out = jnp.zeros_like(t)
    for e in range(N_EXPERTS):
        out = out + gate[:, e:e + 1] * swiglu(t, w1[e], w3[e], w2[e])
    return out.reshape(bsz, s_len, d)

def post_norm_layer(x, mods, mixer, channel, ln):
    sh1, sc1, g1, sh2, sc2, g2 = mods
    y, state = mixer(x * (1 + sc1) + sh1)
    x = layer_norm(ALPHA * x + g1 * y, ln[0], ln[1])
    x = layer_norm(ALPHA * x + g2 * channel(x * (1 + sc2) + sh2), ln[2], ln[3])
    return x, state

def setup_inputs(seed: int = 0) -> dict:
    key = jax.random.key(seed)
    ks = iter(jax.random.split(key, 64))

    def nrm(shape, scale):
        return jax.random.normal(next(ks), shape, jnp.float32) * scale

    def ones_n(n):
        return 1.0 + nrm((n,), 0.02)

    def small(n):
        return nrm((n,), 0.02)

    d = D_MODEL
    w_mix_in = sum(MIX_SIZES)
    w_mix_out = W_A + H_B * HD_B
    w_ssd_in = sum(SSD_SIZES)
    fgate = jnp.linspace(3.0, 6.0, H_A)
    gate_b = jnp.stack([nrm((H_A,), 0.1), fgate + nrm((H_A,), 0.1), nrm((H_A,), 0.1), fgate + nrm((H_A,), 0.1)])
    dt0 = jnp.exp(jax.random.uniform(next(ks), (2, H_C), jnp.float32, math.log(1e-3), math.log(1e-1)))
    dt_bias = dt0 + jnp.log(-jnp.expm1(-dt0))
    a_log = jnp.log(jax.random.uniform(next(ks), (2, H_C), jnp.float32, 1.0, 16.0))
    return {
        'x_prompt': nrm((BATCH, SEQ, d), 1.0),
        'x_sample': nrm((DEC_BATCH, DEC_SEQ, d), 1.0),
        'cache_k_l0': nrm((DEC_BATCH, PAST_LEN, KV_B, HD_B), 1.0),
        'cache_v_l0': nrm((DEC_BATCH, PAST_LEN, KV_B, HD_B), 1.0),
        'state_mlstm_c_l0': nrm((DEC_BATCH, 2, H_A, DK_A, DV_A), 0.5),
        'state_mlstm_n_l0': nrm((DEC_BATCH, 2, H_A, DK_A), 1.0),
        'state_mlstm_m_l0': nrm((DEC_BATCH, 2, H_A), 1.0),
        'state_ssd_l1': nrm((DEC_BATCH, 2, H_C, HD_C, D_STATE), 0.1),
        'c': nrm((DEC_BATCH, d), 1.0),
        'c_ctx': nrm((d,), 1.0),
        'ada_w_l0': nrm((d, 6 * d), d ** -0.5),
        'ada_b_l0': small(6 * d),
        'mix_w_in_l0': nrm((d, w_mix_in), d ** -0.5),
        'mlstm_gate_b_l0': gate_b,
        'mlstm_norm_g_l0': ones_n(W_A),
        'q_norm_g_l0': ones_n(HD_B),
        'k_norm_g_l0': ones_n(HD_B),
        'mix_w_out_l0': nrm((w_mix_out, d), BETA * w_mix_out ** -0.5),
        'ln1_g_l0': ones_n(d),
        'ln1_b_l0': small(d),
        'ln2_g_l0': ones_n(d),
        'ln2_b_l0': small(d),
        'ffn_w1_l0': nrm((d, D_FF), d ** -0.5),
        'ffn_w3_l0': nrm((d, D_FF), d ** -0.5),
        'ffn_w2_l0': nrm((D_FF, d), BETA * D_FF ** -0.5),
        'ada_w_l1': nrm((d, 6 * d), d ** -0.5),
        'ada_b_l1': small(6 * d),
        'ssd_w_in_l1': nrm((d, w_ssd_in), d ** -0.5),
        'ssd_conv_w_l1': nrm((CONV_W, CONV_CH), CONV_W ** -0.5),
        'ssd_conv_b_l1': small(CONV_CH),
        'ssd_dt_bias_l1': dt_bias,
        'ssd_a_log_l1': a_log,
        'ssd_d_l1': ones_n(H_C),
        'ssd_norm_g_l1': ones_n(D_INNER),
        'ssd_w_out_l1': nrm((D_INNER, d), BETA * D_INNER ** -0.5),
        'ln1_g_l1': ones_n(d),
        'ln1_b_l1': small(d),
        'ln2_g_l1': ones_n(d),
        'ln2_b_l1': small(d),
        'router_w_l1': nrm((d, N_EXPERTS), d ** -0.5),
        'router_b_l1': nrm((N_EXPERTS,), 0.01),
        'moe_w1_l1': nrm((N_EXPERTS, d, D_FF_E), d ** -0.5),
        'moe_w3_l1': nrm((N_EXPERTS, d, D_FF_E), d ** -0.5),
        'moe_w2_l1': nrm((N_EXPERTS, D_FF_E, d), BETA * D_FF_E ** -0.5),
    }

def reference(x_prompt, x_sample, cache_k_l0, cache_v_l0, state_mlstm_c_l0, state_mlstm_n_l0, state_mlstm_m_l0,
              state_ssd_l1, c, c_ctx, ada_w_l0, ada_b_l0, mix_w_in_l0, mlstm_gate_b_l0, mlstm_norm_g_l0,
              q_norm_g_l0, k_norm_g_l0, mix_w_out_l0, ln1_g_l0, ln1_b_l0, ln2_g_l0, ln2_b_l0, ffn_w1_l0,
              ffn_w3_l0, ffn_w2_l0, ada_w_l1, ada_b_l1, ssd_w_in_l1, ssd_conv_w_l1, ssd_conv_b_l1,
              ssd_dt_bias_l1, ssd_a_log_l1, ssd_d_l1, ssd_norm_g_l1, ssd_w_out_l1, ln1_g_l1, ln1_b_l1,
              ln2_g_l1, ln2_b_l1, router_w_l1, router_b_l1, moe_w1_l1, moe_w3_l1, moe_w2_l1):
    even_params = [(ada_w_l0, ada_b_l0, mix_w_in_l0, mlstm_gate_b_l0, mlstm_norm_g_l0, q_norm_g_l0, k_norm_g_l0,
                    mix_w_out_l0, (ln1_g_l0, ln1_b_l0, ln2_g_l0, ln2_b_l0), (ffn_w1_l0, ffn_w3_l0, ffn_w2_l0))]
    odd_params = [(ada_w_l1, ada_b_l1, ssd_w_in_l1, ssd_conv_w_l1, ssd_conv_b_l1, ssd_dt_bias_l1, ssd_a_log_l1,
                   ssd_d_l1, ssd_norm_g_l1, ssd_w_out_l1, (ln1_g_l1, ln1_b_l1, ln2_g_l1, ln2_b_l1),
                   (router_w_l1, router_b_l1, moe_w1_l1, moe_w3_l1, moe_w2_l1))]
    caches = [(cache_k_l0, cache_v_l0, state_mlstm_c_l0, state_mlstm_n_l0, state_mlstm_m_l0), state_ssd_l1]

    rows = x_sample.shape[1] // GRID_W
    row = jnp.repeat(jnp.arange(rows), GRID_W)
    col = jnp.tile(jnp.arange(GRID_W), rows)
    ctx_vec = c_ctx[None, :]

    y_p, y_s = x_prompt, x_sample
    new_states = []
    for layer in range(DEPTH):
        if layer % 2 == 0:
            aw, ab, w_in, gb, mhg, qg, kg, w_out, ln, ffn = even_params[layer // 2]
            common = dict(w_in=w_in, b_gates=gb, norm_g=mhg, q_g=qg, k_g=kg, w_out=w_out)
            mixer_p = functools.partial(mlstm_attn_mixer, pos=None, ctx=None, **common)
            mixer_s = functools.partial(mlstm_attn_mixer, pos=(row, col), ctx=caches[layer], **common)
            channel = functools.partial(swiglu, w1=ffn[0], w3=ffn[1], w2=ffn[2])
        else:
            aw, ab, w_in, cw, cb, dtb, alog, dsk, ng, w_out, ln, moe = odd_params[layer // 2]
            common = dict(w_in=w_in, conv_w=cw, conv_b=cb, dt_bias=dtb, a_log=alog, d_skip=dsk, norm_g=ng,
                          w_out=w_out)
            mixer_p = functools.partial(ssd_mixer, s_init=None, **common)
            mixer_s = functools.partial(ssd_mixer, s_init=caches[layer], **common)
            channel = functools.partial(moe_swiglu, router_w=moe[0], router_b=moe[1], w1=moe[2], w3=moe[3],
                                        w2=moe[4])
        y_p, state = post_norm_layer(y_p, ada_mods(ctx_vec, aw, ab), mixer_p, channel, ln)
        new_states.append(state)
        y_s, _ = post_norm_layer(y_s, ada_mods(c, aw, ab), mixer_s, channel, ln)

    new_k_l0, new_v_l0, new_mlstm_c_l0, new_mlstm_n_l0, new_mlstm_m_l0 = new_states[0]
    new_ssd_l1 = new_states[1]
    return (y_p, y_s, new_k_l0, new_v_l0, new_mlstm_c_l0, new_mlstm_n_l0, new_mlstm_m_l0, new_ssd_l1)


_drawn_inputs = setup_inputs


def setup_inputs(seed=0):
    import zlib

    import numpy as np

    out = dict(_drawn_inputs(seed))
    spreads = {}
    factors = {'cache_k_l0': 6.393,
     'cache_v_l0': 4.661,
     'state_mlstm_c_l0': 6.815,
     'state_mlstm_n_l0': 8.0,
     'state_mlstm_m_l0': 8.0,
     'mlstm_norm_g_l0': 25.152,
     'q_norm_g_l0': 23.242,
     'k_norm_g_l0': 35.32,
     'ssd_d_l1': 135.853,
     'ssd_norm_g_l1': 19.209,
     'ln2_b_l1': 2.893,
     'router_b_l1': 15.04,
     'state_ssd_l1': 7.523}
    for name, (base, spread) in spreads.items():
        noise = np.random.default_rng([zlib.crc32(name.encode()), seed]).standard_normal(out[name].shape)
        drawn = base * np.exp(spread * noise) if base else spread * noise
        out[name] = __import__('jax').numpy.asarray(drawn.astype(out[name].dtype))
    for name, factor in factors.items():
        out[name] = (out[name] * factor).astype(out[name].dtype)
    return out
```

```python
from contextlib import ExitStack

import numpy as np
import concourse.bass as bass
from concourse import mybir

F32 = mybir.dt.float32
BF16 = mybir.dt.bfloat16
I32 = mybir.dt.int32
ALU = mybir.AluOpType
ACT = mybir.ActivationFunctionType
X = mybir.AxisListType.X

P = 128
D = 1024
KB = D // P
TP, TS = 128, 256
T = TP + TS
C = T // P
ALPHA = 4 ** 0.25
EPS = 1e-6
HD = 64
HA = 8
VA = HD + 1
H_ATT, KV = 8, 2
HC, NG, HPG, NS = 32, 4, 8, 128
FF, FE, NE = 2816, 1408, 8
FFB, FEB = FF // P, FE // P
XBCB = 24
SCALE = HD ** -0.5
GROUPS = ((0, 0, TP), (1, TP, T))

SLOT = 2816
RING = 4
MOE_SLOTS = 12
TOKW = 288
TOKN = 2304
ITEMS = 13
OVER = ITEMS - NE

QA, KA, VAT, KM, VM, OM = 0, 512, 640, 768, 1280, 1792

CI = {}
_at = 0
for _n, _w in (("ident", 128), ("ropec", 128), ("ropes", 128),
               ("iota", 128), ("tri", 128), ("tie", 64), ("selp", 128), ("pm", 4), ("jrow", 16),
               ("erow", 16), ("irow", OVER)):
    CI[_n] = (_at, _at + _w)
    _at += _w
NCONST = _at

PV = {}
_at = 0
for _n, _w in (("adab0", 48), ("adab1", 48), ("ln", 64), ("convw", 72), ("convb", 24), ("ssdn", 16)):
    PV[_n] = (_at, _at + _w)
    _at += _w
NPV = _at

ADA, ADA_PE = 24, 4
ADA_DVE = ADA - ADA_PE

STAGES = (
    ("ada0a", ADA_PE, 2048, 1), ("gate", 1, 256, 1), ("qm", 2, 2048, 2), ("tok", 8, 8 * TOKW, 1),
    ("mixo", 4, 2048, 2), ("up", 22, 2048, 1), ("down", 8, 2816, 1),
    ("dt", 1, 512, 1), ("xbc", 12, 2048, 2), ("z", 8, 2048, 1),
    ("ssdo", 8, 2048, 1),
)
FIRST, _t = {}, 0
for _n, _k, _w, _s in STAGES:
    FIRST[_n] = _t
    _t += _k


def ds(start, size):
    return bass.ds(start, size)


def wide(ap, axis, n):
    u = ap.unsqueeze(axis)
    shape = list(u.shape)
    shape[axis] = n
    return u.broadcast_to(shape)


def build(nc, i, o):
    ctx = ExitStack()
    with ctx:
        def sb(name, shape, dt=F32):
            return ctx.enter_context(nc.sbuf_tensor(name, shape, dt))

        arena = sb("arena", [P, MOE_SLOTS * SLOT])
        spare = sb("spare", [P, 3900])
        cons = sb("cons", [P, NCONST])
        pvec = sb("pvec", [P, NPV])
        mods = sb("mods", [P, 192])
        xT = sb("xT", [P, KB, T])
        uT = sb("uT", [P, KB, T])
        zT = sb("zT", [P, KB, T])
        sqT = sb("sqT", [P, KB, T])
        onesm = sb("onesm", [P, P])
        onesf = sb("onesf", [P, P])
        maskb16 = sb("maskb16", [P, 2, P], BF16)
        identb16 = sb("identb16", [P, P], BF16)
        small = sb("small", [P, 640])
        ps = ctx.enter_context(nc.psum_tensor("ps", [P, 8, 512], F32))

        ident = cons[:, CI["ident"][0]:CI["ident"][1]]

        def con(name, rows=P):
            return cons[0:rows, CI[name][0]:CI[name][1]]

        def pv(name, j):
            return pvec[:, PV[name][0] + j:PV[name][0] + j + 1]

        def mod(layer, which, b, grp):
            c = layer * 96 + (which * KB + b) * 2 + grp
            return mods[:, c:c + 1]

        def slot(s):
            return arena[:, s * SLOT:(s + 1) * SLOT]

        class Region:
            def __init__(self, ap, at=0):
                self.ap, self.at, self.end = ap, at, ap.shape[1]

            def take(self, n, rows=P):
                assert self.at + n <= self.end, (self.at, n, self.end)
                self.at += n
                return self.ap[0:rows, self.at - n:self.at]

        wa = Region(arena[:, :], RING * SLOT)
        sa = Region(spare[:, :])
        tok0 = wa.take(C * TOKN).rearrange("p (c n) -> p c n", c=C)
        qmT = wa.take(4 * T).rearrange("p (j t) -> p j t", j=4)
        ada_at0 = wa.at
        qkr = wa.take(C * 640).rearrange("p (c n) -> p c n", c=C)
        vaug = wa.take(C * HA * VA).rearrange("p (c h v) -> p c h v", c=C, h=HA)
        kmT = wa.take(4 * T).rearrange("p (j t) -> p j t", j=4)
        qaT = wa.take(4 * T).rearrange("p (j t) -> p j t", j=4)
        kaT = wa.take(4 * P)
        vcache = wa.take(P)
        cst = wa.take(4 * 4 * VA).rearrange("p (w e j v) -> p w e j v", w=2, e=2, j=4)
        cnew = wa.take(2 * 4 * VA).rearrange("p (e j v) -> p e j v", e=2, j=4)
        ewt = wa.take(2 * T).rearrange("p (e t) -> p e t", e=2)
        pwt = wa.take(4 * T).rearrange("p (b e t) -> p b e t", b=2, e=2)
        rope1 = sa.take(C * 640).rearrange("p (c n) -> p c n", c=C)
        rope2 = sa.take(C * 640).rearrange("p (c n) -> p c n", c=C)
        sa.at = 0
        pexp = sa.take(2 * 896).rearrange("p (b n) -> p b n", b=2)
        pexpT = sa.take(2 * 896).rearrange("p (b n) -> p b n", b=2)
        sa.at = 0
        kw = sa.take(4 * 512).rearrange("p (u h d) -> p u h d", u=4, h=HA)
        sa.at = 0
        num = sa.take(HA * 6 * VA).rearrange("p (h u v) -> p h u v", h=HA, u=6)
        itmp = sa.take(4 * VA).rearrange("p (u v) -> p u v", u=4)
        qkg = wa.take(640)
        normg = wa.take(512)
        hsum = wa.take(C * HA * HD).rearrange("p (h c d) -> p h c d", h=HA, c=C)
        ga = Region(zT[:, :, :].rearrange("p a b -> p (a b)"))
        gates32 = ga.take(T, 32)
        gli = ga.take(2 * T, HA).rearrange("p (e t) -> p e t", e=2)
        glf = ga.take(2 * T, HA).rearrange("p (e t) -> p e t", e=2)
        gtmp = ga.take(2 * T, HA).rearrange("p (e t) -> p e t", e=2)
        gb = Region(sqT[:, :, :].rearrange("p a b -> p (a b)"))
        gb1 = gb.take(2 * T, HA).rearrange("p (e t) -> p e t", e=2)
        rows = gb.take(4 * 2 * T - 2 * T, HA)
        rows = rows.rearrange("p (q e t) -> p q e t", q=3, e=2)
        gmax = glf
        hcat = uT[:, :, :].rearrange("p a b -> p (a b)").rearrange("p (c n) -> p c n", c=C)
        hT0 = arena[:, RING * SLOT:RING * SLOT + KB * T].rearrange("p (b t) -> p b t", b=KB)
        sm = Region(small[:, :])
        cvec = sm.take(2 * KB).rearrange("p (k v) -> p k v", k=KB)
        cact = sm.take(2 * KB).rearrange("p (k v) -> p k v", k=KB)
        gbias = sm.take(1, 32)
        mrow = sm.take(2, HA)
        mprev = sm.take(6, HA).rearrange("p (e c) -> p e c", e=2)
        mlast = sm.take(6, HA).rearrange("p (e c) -> p e c", e=2)
        mnew = sm.take(6, HA).rearrange("p (e c) -> p e c", e=2)
        decay = sm.take(6, HA).rearrange("p (e c) -> p e c", e=2)
        dspread = sm.take(8, HA).rearrange("p (e j) -> p e j", e=2)
        dcol = sm.take(8).rearrange("p (e j) -> p e j", e=2)
        cols = sm.take(4 * 6 * HA).rearrange("p (q u h) -> p q u h", q=4, u=6)
        rstat = sm.take(30)
        rstat2 = sm.take(30)
        negmax = sm.take(6).rearrange("p (b u) -> p b u", b=2)
        rsum = sm.take(24).rearrange("p (h u) -> p h u", h=H_ATT)
        rrec = sm.take(24).rearrange("p (h u) -> p h u", h=H_ATT)
        den = sm.take(48)
        den2 = sm.take(48)
        hmean = sm.take(24).rearrange("p (h c) -> p h c", h=HA)
        hvar = sm.take(24).rearrange("p (h c) -> p h c", h=HA)
        epsc = sm.take(1)
        hsq = qkr.rearrange("p c n -> p (c n)")[:, 0:HA * C * HD].rearrange("p (h c d) -> p h c d", h=HA, c=C)
        knew_v = wa.take(P)
        stdr = sb("stdr", [P, T])
        masks = stdr[:, 0:2 * P].rearrange("p (e t) -> p e t", e=2)

        ffh = arena[:, RING * SLOT:RING * SLOT + FFB * T].rearrange("p (f t) -> p f t", f=FFB)
        silu2 = arena[:, RING * SLOT + FFB * T:RING * SLOT + (FFB + 2) * T].rearrange("p (b t) -> p b t", b=2)

        ada_free = RING * SLOT + (FFB + 2) * T
        adaw = [[arena[:, at + 2048 * b:at + 2048 * (b + 1)] for b in range(2)] for at in (ada_at0, ada_free)]
        crow = [spare[:, 0:2 * D], arena[:, ada_free + 4096:ada_free + 4096 + 2 * D]]
        junk = [spare[:, 2 * D:3 * D], arena[:, ada_free + 4096 + 2 * D:ada_free + 4096 + 3 * D]]

        wb = Region(arena[:, :], RING * SLOT)
        bcT = wb.take(2 * NG * T).rearrange("p (n t) -> p n t", n=2 * NG)
        btok = wb.take(C * 512).rearrange("p (c n) -> p c n", c=C)
        xg_flat = wb.take(NG * C * 512)
        xg = xg_flat.rearrange("p (g c n) -> p g c n", g=NG, c=C)
        yT = xg_flat.rearrange("p (k t) -> p k t", t=T)
        zg = wb.take(2 * C * 512).rearrange("p (b c n) -> p b c n", b=2, c=C)
        xdt_at = wb.at
        xdt = wb.take(2 * C * 512).rearrange("p (e c n) -> p e c n", e=2, c=C)
        xdt_end, wb.at = wb.at, xdt_at
        PAD = T + 3
        raw = wb.take(2 * PAD).rearrange("p (b t) -> p b t", b=2)
        conv = wb.take(2 * PAD).rearrange("p (b t) -> p b t", b=2)
        xfeat = wb.take(2 * T).rearrange("p (b t) -> p b t", b=2)
        wb.at = xdt_end
        cb = wb.take(T)
        edec = wb.take(2 * T).rearrange("p (e t) -> p e t", e=2)
        wdec = wb.take(4 * T).rearrange("p (b e t) -> p b e t", b=2, e=2)
        sec = wb.take(2 * 512).rearrange("p (e n) -> p e n", e=2)
        yacc = wb.take(C * 512).rearrange("p (c n) -> p c n", c=C)
        sc_ = Region(spare[:, :])
        sini = sc_.take(2 * 512).rearrange("p (e n) -> p e n", e=2)
        snew = sc_.take(2 * 4 * P).rearrange("p (e j n) -> p e j n", e=2, j=4)
        dtc = sc_.take(6 * HC).rearrange("p (u h) -> p u h", u=6)
        cumc = sc_.take(6 * HC).rearrange("p (u h) -> p u h", u=6)
        ncumc = sc_.take(6 * HC).rearrange("p (u h) -> p u h", u=6)
        ecumc = sc_.take(6 * HC).rearrange("p (u h) -> p u h", u=6)
        wsc = sc_.take(6 * HC).rearrange("p (u h) -> p u h", u=6)
        dskip = sc_.take(HC)
        inter1 = sc_.take(512)
        elast = sm.take(2 * HC).rearrange("p (e h) -> p e h", e=2)
        dtb = sm.take(2, HC)
        acoef = sm.take(2, HC)
        gss = sm.take(C)
        gsd = sm.take(C)
        ra = Region(zT[:, :, :].rearrange("p a b -> p (a b)"))
        rx, rz, ru, rd = (ra.take(2 * T, HC).rearrange("p (e t) -> p e t", e=2) for _ in range(4))
        rb = Region(sqT[:, :, :].rearrange("p a b -> p (a b)"))
        rdt, rda, rcum = (rb.take(2 * T, HC).rearrange("p (e t) -> p e t", e=2) for _ in range(3))
        ra.at = 0
        xw = ra.take(4 * 512).rearrange("p (u n) -> p u n", u=4)
        ysq = ra.take(512)

        utok = sqT[:, :, :].rearrange("p a b -> p (a b)").rearrange("p (c n) -> p c n", c=C)
        rc = Region(zT[:, :, :].rearrange("p a b -> p (a b)"))
        xe = rc.take(D).rearrange("p (k s) -> p k s", k=KB)
        ye = rc.take(D)
        disp = rc.take(C * P).rearrange("p (c s) -> p c s", c=C)
        comb = rc.take(T)
        gdisp = stdr[:, :].rearrange("p (c s) -> p c s", c=C)
        acc = uT
        re_ = Region(spare[:, :])
        he = re_.take(FE)
        sige = re_.take(2 * (FE // 4)).rearrange("p (b n) -> p b n", b=2)
        heT = re_.take(FEB * P).rearrange("p (f s) -> p f s", f=FEB)
        posi = re_.take(C * ITEMS).rearrange("p (c i) -> p c i", c=C)
        gatei = re_.take(C * ITEMS).rearrange("p (c i) -> p c i", c=C)
        listf = re_.take(16)
        routw = re_.take(KB * NE).rearrange("p (k e) -> p k e", k=KB)
        routb = re_.take(NE)
        rt = Region(spare[:, :])
        logit, sel, ppos, gate, rank, expl = (rt.take(C * NE).rearrange("p (c e) -> p c e", c=C) for _ in range(6))
        vmax, gsum = rt.take(C), rt.take(C)
        cnt = rt.take(NE)
        cmp1, cmp2 = (rt.take(C * NE * NE) for _ in range(2))
        have, order = rt.take(16), rt.take(16)
        hot = rt.take(OVER * 16)
        pp2, gg2 = (rt.take(C * 16) for _ in range(2))
        big = rt.take(C * OVER * 16)
        jover, eover = rt.take(OVER), rt.take(OVER)
        lists = sb("lists", [1, 16], I32)

        sems = {}

        def S(name):
            if name not in sems:
                sems[name] = ctx.enter_context(nc.semaphore(name))
            return sems[name]

        ready = [S(f"slot_ready{s}") for s in range(RING)]
        ready += [S(f"slot_ready{s}") for s in range(RING, MOE_SLOTS)]
        TILES = FIRST["ssdo"] + 8
        moe_base = [16 * sum(t % RING == s for t in range(TILES)) if s < RING else 0 for s in range(MOE_SLOTS)]

        def tile_done(t):
            for name, n, _, per in STAGES:
                if t < FIRST[name] + n:
                    k = t - FIRST[name]
                    if name == "ada0a":
                        return S("ada_mm"), k + 1
                    return S({"mixo": "y_mm", "down": "y_mm", "ssdo": "y_mm"}.get(name, name + "_mm")), \
                        {"mixo": 0, "down": KB, "ssdo": 2 * KB}.get(name, 0) + per * (k + 1)

        def tile_ready(t):
            return ready[t % RING], 16 * (t // RING + 1)

        class Serial:
            def __init__(self, eng, sem):
                self.eng, self.sem, self.n = eng, sem, 0

            def __call__(self, ins):
                self.n += 1
                ins.then_inc(self.sem, 1)
                self.eng.wait_ge(self.sem, self.n)

            def done(self, ins, sem, count):
                ins.then_inc(sem, 1)
                self.eng.wait_ge(sem, count)

            def ready(self, ins, sem, count):
                ins.then_inc(sem, 1)
                self.eng.wait_ge(sem, count)

        block = ctx.enter_context(nc.Block())

        @block.sync
        def _(sp):
            sp.dma_start(cons[:, :], i["consts"]).then_inc(S("consts_in"), 16)
            sp.dma_start(pvec[:, :], i["pvec"]).then_inc(S("consts_in"), 16)
            sp.dma_start(masks, i["masks"]).then_inc(S("consts_in"), 16)
            sp.dma_start(cvec, i["cvec"]).then_inc(S("consts_in"), 16)

            def load(name, width, t, k):
                g = FIRST[name] + t
                sp.dma_start(slot(g % RING)[:, 0:width], i["w_" + name][k]).then_inc(ready[g % RING], 16)

            def stream(name):
                _, n, width, per = [x for x in STAGES if x[0] == name][0]
                first = FIRST[name]
                head = min(n, RING)
                for t in range(head):
                    if first + t >= RING:
                        sp.wait_ge(*tile_done(first + t - RING))
                    load(name, width, t, t)
                loops = (n - head) // RING
                if loops:
                    with sp.Fori(0, loops) as it:
                        for j in range(RING):
                            sem, count = tile_done(first + j)
                            sp.wait_ge(sem, it * (RING * per) + count)
                            load(name, width, head + j, it * RING + head + j)
                for t in range(head + loops * RING, n):
                    sp.wait_ge(*tile_done(first + t - RING))
                    load(name, width, t, t)

            sp.dma_start(xT[:, :, :], i["xT"]).then_inc(S("x_in"), 16)
            for name, *_ in STAGES:
                stream(name)

            def load_expert(e, s):
                sp.dma_start(slot(s), i["w_moe"][e, s] if isinstance(e, int) else
                             i["w_moe"][ds(e, 1), s].rearrange("a p n -> (a p) n")).then_inc(ready[s], 16)

            def expert_tile_free(it, s):
                if s < 8:
                    sp.wait_ge(S("mup_mm"), it * 4 + (s // 2 - 3))
                else:
                    sp.wait_ge(S("my_mm"), it * 4 + (s - 8 - 3))

            last = FIRST["ssdo"] + 8
            for s in range(MOE_SLOTS):
                if s < RING:
                    t = max(t for t in range(last) if t % RING == s)
                    sp.wait_ge(*tile_done(t))
                else:
                    sp.wait_ge(S("y_mm"), 3 * KB)
                load_expert(0, s)
            with sp.Fori(1, NE) as it:
                for s in range(MOE_SLOTS):
                    expert_tile_free(it, s)
                    load_expert(it, s)
            sp.wait_ge(S("routed"), 1)
            n_items = sp.value_load(lists[0:1, ITEMS:ITEMS + 1], min_val=NE, max_val=ITEMS)
            with sp.If(n_items > NE):
                with sp.Fori(NE, n_items) as it:
                    e = sp.value_load(lists[0:1, ds(it, 1)], min_val=0, max_val=NE - 1)
                    for s in range(MOE_SLOTS):
                        expert_tile_free(it, s)
                        load_expert(e, s)
            sp.wait_ge(S("x_ready"), 4 * KB)
            sp.dma_start(o["yT"], xT[:, :, :]).then_inc(S("stored"), 16)
            sp.wait_ge(S("stored"), 16)
            sp.wait_ge(S("ctx_stored"), 16 * 4)
            sp.wait_ge(S("ssd_stored"), 16 * NG)

        @block.gpsimd
        def _(gp):
            step = Serial(gp, S("pool_step"))

            def ada_tile(layer, n, b):
                src = i[f"w_adav{layer}"]
                gp.dma_start(adaw[layer][b], src[n] if isinstance(n, int) else
                             src[ds(n, 1)].rearrange("a p n -> (a p) n")).then_inc(S(f"ada_in{b}"), 16)

            def ada_tiles(layer, n):
                base = (0, ADA_DVE)[layer]
                with gp.Fori(0, n // 2 - 1) as it:
                    for b in range(2):
                        gp.wait_ge(S("ada_used"), it * 2 + (base + b + 1))
                        ada_tile(layer, it * 2 + (b + 2), b)

            gp.dma_start(crow[0], i["cond"].partition_broadcast(P)).then_inc(S("cond_in"), 16)
            for b in range(2):
                ada_tile(0, b, b)
            gp.dma_start(gbias, i["gate_b"]).then_inc(S("misc_in"), 16)
            gp.dma_start(kaT[:, P:2 * P], i["cache_kT"]).then_inc(S("misc_in"), 16)
            gp.dma_start(vcache, i["cache_v"]).then_inc(S("misc_in"), 16)
            gp.dma_start(cst[:, 0, :, :, :], i["c0n0"]).then_inc(S("misc_in"), 16)
            gp.dma_start(mrow, i["m0"]).then_inc(S("misc_in"), 16)
            gp.dma_start(qkg, i["qk_g"].partition_broadcast(P)).then_inc(S("misc_in"), 16)
            gp.dma_start(normg, i["mlstm_g"].partition_broadcast(P)).then_inc(S("misc_in"), 16)
            ada_tiles(0, ADA_DVE)

            def scale_x(n):
                gp.wait_ge(S("u_ready"), KB * (n + 1))
                step.done(nc.gpsimd.tensor_scalar_mul(xT[:, :, :], xT[:, :, :], ALPHA), S("ax_ready"), n + 1)

            scale_x(0)
            gp.wait_ge(S("qk_ready"), 1)
            gp.dma_start(o["new_k"], knew_v).then_inc(S("ctx_stored"), 16)
            gp.dma_start(o["new_v"], tok0[:, 0, VAT:VAT + P]).then_inc(S("ctx_stored"), 16)
            gp.wait_ge(S("exp_in"), 1)
            gp.dma_start(o["new_m"], mnew).then_inc(S("ctx_stored"), 16)
            gp.wait_ge(S("state_ready"), 1)
            gp.dma_start(o["new_cn"], cnew).then_inc(S("ctx_stored"), 16)
            gp.wait_ge(S("z_ready"), 1)
            gp.dma_start(crow[1], i["cond"].partition_broadcast(P)).then_inc(S("cond_in"), 16)
            for b in range(2):
                ada_tile(1, b, b)
            scale_x(1)
            ada_tiles(1, ADA)
            gp.dma_start(dtb, i["dt_bias"]).then_inc(S("misc1_in"), 16)
            gp.dma_start(acoef, i["a_log"]).then_inc(S("misc1_in"), 16)
            gp.wait_ge(S("z_ready"), 2 * KB)
            gp.dma_start(routw, i["router_w"]).then_inc(S("misc1_in"), 16)
            gp.dma_start(routb, i["router_b"].partition_broadcast(P)).then_inc(S("misc1_in"), 16)
            gp.dma_start(dskip, i["d_skip"].partition_broadcast(P)).then_inc(S("misc1_in"), 16)
            scale_x(2)
            step.done(nc.gpsimd.memset(raw, 0.0), S("raw_zero"), 1)
            for g in range(NG):
                def heads(ap):
                    return ap.rearrange("p (h d) -> p h d", d=HD)

                hs = slice(g * HPG, (g + 1) * HPG)
                gp.wait_ge(S("wexp_ready"), 1)
                if g:
                    gp.wait_ge(S("inter_mm"), 4 * g)
                    gp.wait_ge(S("inter_ready"), 4 * g)
                    gp.wait_ge(S("sec_ready"), 2 * g)
                    gp.wait_ge(S("ysum_mm"), HPG * g)
                gp.dma_start(sini, i["ssd0"][g]).then_inc(S("sini_in"), 16)
                for e in range(2):
                    for c in range(C):
                        k = nc.gpsimd.tensor_tensor(heads(xdt[:, e, c, :]), heads(xg[:, g, c, :]),
                                                    wide(dtc[:, 3 * e + c, hs], 2, HD), ALU.mult)
                        step(k)
                    step.done(nc.gpsimd.memset(listf[0:1, 14:15], 0.0), S("xdt_ready"), 2 * g + e + 1)
                for u, (c, e) in enumerate(((0, 0), (0, 1), (1, 0), (2, 1))):
                    step.done(nc.gpsimd.tensor_tensor(heads(xw[:, u, :]), heads(xdt[:, e, c, :]),
                                                      wide(wsc[:, 3 * e + c, hs], 2, HD), ALU.mult),
                              S("xw_ready"), 4 * g + u + 1)
                if g:
                    gp.wait_ge(S("yn_ready"), g)
                for c in range(C):
                    step.done(nc.gpsimd.tensor_tensor(heads(yacc[:, c, :]), heads(xg[:, g, c, :]),
                                                      wide(dskip[:, hs], 2, HD), ALU.mult),
                              S("yd_ready"), C * g + c + 1)
                gp.wait_ge(S("snew_half"), 2 * g + 2)
                gp.dma_start(o["new_ssd"][g], snew).then_inc(S("ssd_stored"), 16)
            scale_x(3)

        @block.scalar
        def _(act):
            step = Serial(act, S("act_step"))

            def layer_norm(ln):
                for q in range(4):
                    act.wait_ge(S("dev_ready"), 4 * ln + q + 1)
                    nc.scalar.activation(sqT[:, 2 * q:2 * q + 2, :], zT[:, 2 * q:2 * q + 2, :], ACT.Square) \
                        .then_inc(S("sq_ready"), 1)
                act.wait_ge(S("var_mm"), ln + 1)
                nc.scalar.activation(stdr[:, :], ps[:, 7, 0:T], ACT.Sqrt, bias=epsc).then_inc(S("std_ready"), 1)
                for b in range(KB):
                    act.wait_ge(S("norm_ready"), 4 * ln + b // 2 + 1)
                    nc.scalar.activation(xT[:, b, :], zT[:, b, :], ACT.Identity,
                                         bias=pv("ln", (2 * ln + 1) * KB + b),
                                         scale=pv("ln", 2 * ln * KB + b)).then_inc(S("x_ready"), 1)

            act.wait_ge(S("consts_in"), 64)
            nc.scalar.activation(cact, cvec, ACT.Silu).then_inc(S("cact_ready"), 1)
            act.wait_ge(S("cond_in"), 16)
            nc.scalar.activation(crow[0], crow[0], ACT.Silu).then_inc(S("cond_ready"), 1)
            act.wait_ge(S("gate_mm"), 1)
            act.wait_ge(S("misc_in"), 16 * 7)
            step.done(nc.scalar.activation(gates32, ps[0:32, 2, 0:T], ACT.Identity, bias=gbias),
                      S("gates_ready"), 1)
            for q in range(4):
                act.dma_start((gli, glf)[q % 2][:, q // 2, :], gates32[HA * q:HA * q + HA, :]) \
                    .then_inc(S("gates_moved"), 16)
            for j in range(4):
                act.wait_ge(S("qm_mm"), j + 1)
                step.done(nc.scalar.activation(qmT[:, j, :], ps[:, j % 2, 0:T], ACT.Copy, scale=SCALE),
                          S("qm_ready"), j + 1)
            act.wait_ge(S("gates_moved"), 64)
            step(nc.scalar.activation(gtmp, glf, ACT.Abs))
            step(nc.scalar.activation(gtmp, gtmp, ACT.Exp, scale=-1.0))
            step.done(nc.scalar.activation(gtmp, gtmp, ACT.Ln, bias=1.0), S("soft_log"), 1)
            act.sem_inc(S("tok_free"), 2)
            with act.Fori(0, 2) as it:
                for j in range(4):
                    act.wait_ge(S("tok_mm"), it * 4 + j + 1)
                    for c in range(C):
                        e = nc.scalar.activation(tok0[:, c, ds(it * (4 * TOKW) + j * TOKW, TOKW)],
                                                 ps[:, 3 * (j % 2) + c, 0:TOKW], ACT.Copy)
                    e.then_inc(S("tok_free"), 1)
            act.wait_ge(S("tok_free"), 10)
            act.wait_ge(S("ada_used"), ADA_DVE)
            step.done(nc.scalar.activation(rope1, tok0[:, :, 0:640], ACT.Square), S("qk_moments"), 1)
            act.wait_ge(S("qk_var"), 1)
            step.done(nc.scalar.activation(rstat2, rstat, ACT.Sqrt, bias=epsc, scale=1.0 / HD), S("qk_moments"), 2)
            act.wait_ge(S("exp_in"), 1)
            step(nc.scalar.activation(rows[:, 0:2, :, :], rows[:, 0:2, :, :], ACT.Exp, scale=-1.0))
            step(nc.scalar.activation(rows[:, 2, :, :], rows[:, 2, :, :], ACT.Exp))
            step.done(nc.scalar.activation(decay, decay, ACT.Exp), S("rows_ready"), 1)
            for c in range(C):
                act.wait_ge(S("tr_mm"), c + 1)
                nc.scalar.activation(kmT[:, :, c * P:(c + 1) * P],
                                     ps[:, 4 + c, :].rearrange("p (j t) -> p j t", j=4), ACT.Copy) \
                    .then_inc(S("kmT_ready"), 1)
            for h in range(H_ATT):
                act.wait_ge(S("max_ready"), h + 1)
                a = h % 2
                if h >= 2:
                    act.wait_ge(S("attT_mm"), h - 1)
                src = (ps[:, 2 * a, 384:512], ps[:, 2 * a, 0:384], ps[:, 2 * a + 1, 0:384])
                dst = (pexp[:, a, 0:128], pexp[:, a, 128:512], pexp[:, a, 512:896])
                for u in range(3):
                    nc.scalar.activation(dst[u], src[u], ACT.Exp, bias=negmax[:, a, u:u + 1], scale=SCALE,
                                         accum_out=rsum[:, h, u:u + 1]).then_inc(S("exp_ready"), 1)
                act.wait_ge(S("attT_mm"), h + 1)
                if h >= 2:
                    act.wait_ge(S("pv_mm"), h - 1)
                nc.scalar.activation(pexpT[:, a, 512:896], ps[:, 5, 0:384], ACT.Copy).then_inc(S("attT_act"), 1)
            act.wait_ge(S("att_ready"), 1)
            nc.scalar.activation(tok0[:, :, OM:OM + 512], tok0[:, :, OM:OM + 512], ACT.Sigmoid) \
                .then_inc(S("om_ready"), 1)
            for h in range(HA):
                for e in range(2):
                    act.wait_ge(S("bc_mm"), 2 * h + e + 1)
                    if h == 0:
                        act.wait_ge(S("cols_ready"), 1)
                        act.wait_ge(S("pv_mm"), H_ATT)
                    else:
                        act.wait_ge(S("pt_ready"), 2 * (h - 1) + e + 1)
                    for c in range(C):
                        k = nc.scalar.activation(ewt[:, e, c * P:(c + 1) * P], ps[:, 2 + e, c * P:(c + 1) * P],
                                                 ACT.Exp, bias=cols[:, 0, 3 * e + c, h:h + 1])
                    k.then_inc(S("e_ready"), 1)
            act.wait_ge(S("h_moments"), 1)
            nc.scalar.activation(hsq, hsum, ACT.Square).then_inc(S("h_moments_act"), 1)
            act.wait_ge(S("h_moments"), 2)
            nc.scalar.activation(hvar, hvar, ACT.Sqrt, bias=epsc, scale=1.0 / HD).then_inc(S("h_moments_act"), 1)
            for b in range(3, 6):
                act.wait_ge(S("hcatT_mm"), b + 1)
                nc.scalar.activation(hT0[:, 4:8, (b - 3) * P:(b - 2) * P],
                                     ps[:, b, :].rearrange("p (j t) -> p j t", j=4), ACT.Copy) \
                    .then_inc(S("hT_act"), 1)
            layer_norm(0)
            act.wait_ge(S("cond_in"), 32)
            nc.scalar.activation(crow[1], crow[1], ACT.Silu).then_inc(S("cond_ready"), 1)
            act.wait_ge(S("z_ready"), KB)
            for t in range(2):
                act.wait_ge(S("up_mm"), t + 1)
                nc.scalar.activation(silu2[:, t, :], ps[:, 2 * t, 0:T], ACT.Silu).then_inc(S("silu_ready"), 1)
            with act.Fori(0, FFB // 2 - 1) as it:
                for t in range(2):
                    act.wait_ge(S("up_mm"), it * 2 + t + 3)
                    act.wait_ge(S("h_ready"), it * 2 + t + 3)
                    nc.scalar.activation(silu2[:, t, :], ps[:, 2 * t, 0:T], ACT.Silu).then_inc(S("silu_ready"), 1)
            layer_norm(1)
            act.wait_ge(S("misc1_in"), 16 * 5)
            step(nc.scalar.activation(acoef, acoef, ACT.Exp))
            act.wait_ge(S("dt_mm"), 1)
            for e in range(2):
                step(nc.scalar.activation(rx[:, e, :], ps[0:HC, e, 0:T], ACT.Identity, bias=dtb[:, e:e + 1]))
            step(nc.scalar.activation(rz, rx, ACT.Abs))
            step.done(nc.scalar.activation(rz, rz, ACT.Exp, scale=-1.0), S("soft_log"), 2)
            act.wait_ge(S("dt_u"), 1)
            step.done(nc.scalar.activation(rdt, ru, ACT.Ln), S("soft_log"), 3)
            act.sem_inc(S("bc_free"), 2)

            def conv_in(n, j, first):
                act.wait_ge(S("xbc_mm"), n + 1)
                b = j % 2
                if not first:
                    act.wait_ge(S("conv_ready"), n - 1)
                nc.scalar.activation(raw[:, b, 1:1 + TP], ps[:, 2 + b, 0:TP], ACT.Copy)
                nc.scalar.activation(raw[:, b, 2 + TP:2 + T], ps[:, 2 + b, TP:T], ACT.Copy) \
                    .then_inc(S("bc_free"), 1)

            def conv_out(n, j, dst, sem):
                act.wait_ge(S("conv_ready"), n + 1)
                b = j % 2
                nc.scalar.activation(dst[:, 0:TP], conv[:, b, 0:TP], ACT.Silu)
                nc.scalar.activation(dst[:, TP:T], conv[:, b, TP + 1:T + 1], ACT.Silu).then_inc(sem, 1)

            act.wait_ge(S("raw_zero"), 1)
            for n in range(2):
                conv_in(n, n, True)
            with act.Fori(0, 2) as it:
                for j in range(8):
                    n = it * 8 + j
                    conv_out(n, j, xfeat[:, j % 2, :], S("xfeat_ready"))
                    conv_in(n + 2, j, False)
            for n in range(16, 24):
                conv_out(n, n, bcT[:, n - 16, :], S("bcT_ready"))
                if n + 2 < 24:
                    conv_in(n + 2, n, False)
            act.wait_ge(S("ccol_ready"), 2)
            step(nc.scalar.activation(ecumc, cumc, ACT.Exp))
            step.done(nc.scalar.activation(ncumc, cumc, ACT.Copy, scale=-1.0), S("cumc_ready"), 1)
            act.wait_ge(S("last_ready"), 1)
            step(nc.scalar.activation(elast, elast, ACT.Exp))
            step.done(nc.scalar.activation(wsc, wsc, ACT.Exp), S("wexp_ready"), 1)
            for g in range(NG):
                act.wait_ge(S("z_mm"), 2 * g + 2)
                if g >= 2:
                    act.wait_ge(S("yT_mm"), C * (g - 1))
                for c in range(C):
                    nc.scalar.activation(zg[:, g % 2, c, :], ps[:, 5 + c, :], ACT.Silu).then_inc(S("zg_ready"), 1)
                if g:
                    act.wait_ge(S("yg_ready"), g)
                    for c in range(C):
                        step(nc.scalar.activation(ysq, zg[:, (g - 1) % 2, c, :], ACT.Square,
                                                  accum_out=gss[:, c:c + 1]))
                    step.done(nc.scalar.activation(gsd, gss, ACT.Sqrt, bias=epsc, scale=1.0 / 512),
                              S("yg_std"), g)
                act.wait_ge(S("cb_mm"), g + 1)
                if g:
                    act.wait_ge(S("s_w_ready"), 2 * HPG * g)
                nc.scalar.activation(cb, ps[:, 3, 0:T], ACT.Copy).then_inc(S("cb_ready"), 1)
                for r in range(HPG):
                    h = g * HPG + r
                    for e in range(2):
                        act.wait_ge(S("s_bc_mm"), 2 * h + e + 1)
                        if h:
                            act.wait_ge(S("s_w_ready"), 2 * (h - 1) + e + 1)
                        for c in range(C):
                            k = nc.scalar.activation(edec[:, e, c * P:(c + 1) * P],
                                                     ps[:, 3 + e, c * P:(c + 1) * P], ACT.Exp,
                                                     bias=ncumc[:, 3 * e + c, h:h + 1])
                        k.then_inc(S("s_e_ready"), 1)
                    if r in (2, 4):
                        e = r // 2 - 1
                        act.wait_ge(S("out_mm"), 2 * g + e + 1)
                        if g and e == 0:
                            act.wait_ge(S("ssd_stored"), 16 * g)
                        k = nc.scalar.activation(snew[:, e, :, :],
                                                 ps[:, 5 + e, :].rearrange("p (j n) -> p j n", j=4), ACT.Copy)
                        step.done(k, S("snew_half"), 2 * g + e + 1)
            act.wait_ge(S("yg_ready"), NG)
            for c in range(C):
                step(nc.scalar.activation(ysq, zg[:, (NG - 1) % 2, c, :], ACT.Square, accum_out=gss[:, c:c + 1]))
            step.done(nc.scalar.activation(gsd, gss, ACT.Sqrt, bias=epsc, scale=1.0 / 512), S("yg_std"), NG)
            layer_norm(2)
            act.wait_ge(S("ssd_stored"), 16 * NG)
            act.wait_ge(S("sel_ready"), 2)
            step.done(nc.scalar.activation(expl, expl, ACT.Exp), S("expl_ready"), 1)
            for n in range(3):
                act.wait_ge(S("utok_mm"), 2 * n + 2)
                nc.scalar.activation(utok[:, n, 512:1024], ps[:, 3 + 2 * (n % 2), :], ACT.Copy) \
                    .then_inc(S("utok_act"), 1)
            act.wait_ge(S("routed"), 1)
            n_items = act.value_load(lists[0:1, ITEMS:ITEMS + 1], min_val=NE, max_val=ITEMS)
            with act.Fori(0, n_items) as it:
                act.wait_ge(S("xe_mm"), it * 2 + 1)
                nc.scalar.activation(xe[:, 0:4, :], ps[:, 4, :].rearrange("p (k s) -> p k s", k=4), ACT.Copy) \
                    .then_inc(S("xe_act"), 1)
                for f in range(4):
                    act.wait_ge(S("mup_mm"), it * 4 + f + 1)
                    if f >= 2:
                        act.wait_ge(S("mh_ready"), it * 4 + (f - 1))
                    nc.scalar.activation(sige[:, f % 2, :], ps[:, 2 * (f % 2), 0:FE // 4], ACT.Silu) \
                        .then_inc(S("msilu_ready"), 1)
                for n, bank, f0, f1 in ((0, 4, 0, 4), (2, 6, 8, FEB)):
                    act.wait_ge(S("mhT_mm"), it * 3 + n + 1)
                    nc.scalar.activation(heT[:, f0:f1, :],
                                         ps[:, bank, 0:(f1 - f0) * P].rearrange("p (f s) -> p f s", s=P),
                                         ACT.Copy).then_inc(S("mhT_act"), 1)
                for n in range(2):
                    act.wait_ge(S("my_mm"), it * 4 + 2 * n + 2)
                    nc.scalar.activation(ye[:, n * 512:(n + 1) * 512], ps[:, (7, 4)[n], :], ACT.Copy) \
                        .then_inc(S("ye_ready"), 1)
            layer_norm(3)

        @block.vector
        def _(v):
            step = Serial(v, S("dve_step"))
            V = nc.vector

            def ada_rows(layer, n, b, seen, used):
                v.wait_ge(S(f"ada_in{b}"), seen)
                for blk in range(2):
                    for grp in range(2):
                        c = n * 4 + (layer * 96 + 2 * blk + grp)
                        k = V.scalar_tensor_tensor(junk[layer], adaw[layer][b][:, blk * D:(blk + 1) * D], 1.0,
                                                   crow[layer][:, grp * D:(grp + 1) * D], ALU.mult, ALU.mult,
                                                   accum_out=mods[:, ds(c, 1)])
                        if (blk, grp) != (1, 1):
                            step(k)
                step.done(k, S("ada_used"), used)

            def ada_loop(layer, n0, n1, between=None):
                first, base = ((ADA_PE, 0), (0, ADA_DVE))[layer]
                at = step.n
                with v.Fori(0, (n1 - n0) // 2) as it:
                    for b in range(2):
                        step.n = it * 6 + (at + 3 * b)
                        if between:
                            between(it, b)
                        ada_rows(layer, it * 2 + (n0 + b + first), b, it * 16 + 8 * (n0 + base + 2),
                                 it * 2 + (n0 + base + b + 1))
                step.n = at + 3 * (n1 - n0)

            def modulations(layer, b0, b1, count):
                for lo, hi, src in ((b0, 2 * ADA_PE, ps[:, 5, :]), (2 * ADA_PE, b1, mods)) \
                        if layer == 0 and b0 == 0 else ((b0, b1, mods),):
                    c0, c1 = layer * 96 + 2 * lo, layer * 96 + 2 * hi
                    bias = pvec[:, PV[f"adab{layer}"][0] + lo:PV[f"adab{layer}"][0] + hi]
                    step(V.tensor_tensor(mods[:, c0:c1].rearrange("p (b g) -> p b g", g=2),
                                         src[:, c0:c1].rearrange("p (b g) -> p b g", g=2),
                                         wide(bias, 2, 2), ALU.add))
                for s in (2 * KB, 8 * KB):
                    if 2 * b0 <= s < 2 * b1:
                        s += layer * 96
                        step(V.tensor_scalar_add(mods[:, s:s + 2 * KB], mods[:, s:s + 2 * KB], 1.0))
                step.done(V.memset(epsc, EPS), S("mods_ready"), count)

            def modulate(layer, half, n):
                for b in range(KB):
                    if n:
                        v.wait_ge(S("x_ready"), KB * n + b + 1 - (KB if n else 0))
                    for _, t0, t1 in GROUPS:
                        grp = 0 if t0 == 0 else 1
                        u = V.tensor_scalar(uT[:, b, t0:t1], xT[:, b, t0:t1], mod(layer, 3 * half + 1, b, grp),
                                            mod(layer, 3 * half, b, grp), ALU.mult, ALU.add)
                        if grp == 0:
                            step(u)
                    step.done(u, S("u_ready"), KB * n + b + 1)

            def layer_norm(layer, half, ln, bank):
                v.wait_ge(S("ax_ready"), ln + 1)
                for b in range(KB):
                    v.wait_ge(S("y_mm"), KB * ln + b + 1)
                    for grp, t0, t1 in GROUPS:
                        z = V.scalar_tensor_tensor(zT[:, b, t0:t1], ps[:, bank(b), t0:t1],
                                                   mod(layer, 3 * half + 2, b, grp), xT[:, b, t0:t1],
                                                   ALU.mult, ALU.add)
                        if grp == 0:
                            step(z)
                    step.done(z, S("z_ready"), KB * ln + b + 1)
                norm_steps(ln)

            def norm_steps(ln):
                v.wait_ge(S("mean_mm"), ln + 1)
                for q in range(4):
                    step.done(V.tensor_tensor(zT[:, 2 * q:2 * q + 2, :], zT[:, 2 * q:2 * q + 2, :],
                                              wide(ps[:, 6, 0:T], 1, 2), ALU.subtract),
                              S("dev_ready"), 4 * ln + q + 1)
                v.wait_ge(S("std_ready"), ln + 1)
                step(V.reciprocal(stdr[:, :], stdr[:, :]))
                for q in range(4):
                    step.done(V.tensor_tensor(zT[:, 2 * q:2 * q + 2, :], zT[:, 2 * q:2 * q + 2, :],
                                              wide(stdr[:, :], 1, 2), ALU.mult), S("norm_ready"), 4 * ln + q + 1)

            step(V.memset(onesf[:, :], 1.0))
            step(V.memset(epsc, EPS))
            step(V.memset(onesm[:, :], 1.0 / D))
            v.wait_ge(S("consts_in"), 64)
            step(V.tensor_copy(maskb16[:, :, :], masks))
            step.done(V.tensor_copy(identb16[:, :], ident), S("b16_ready"), 1)
            v.wait_ge(S("cond_ready"), 1)
            ada_loop(0, 0, KB - ADA_PE)
            v.wait_ge(S("ada_mm"), ADA_PE)
            modulations(0, 0, 2 * KB, 1)
            v.wait_ge(S("x_in"), 16)
            modulate(0, 0, 0)
            ada_loop(0, KB - ADA_PE, KB)
            v.wait_ge(S("soft_log"), 1)
            step(V.scalar_tensor_tensor(glf, glf, 0.0, gtmp, ALU.min, ALU.subtract))

            def span(ap, e, c):
                if e == 0:
                    return ap[:, 0, c * P:(c + 1) * P]
                return ap[:, 1, (c + 1) * P - 1:(c * P - 1 if c else None):-1]

            for e in range(2):
                for c in range(C):
                    step(V.tensor_tensor_scan(span(gb1, e, c), onesf[0:HA, :], span(glf, e, c), 0.0,
                                              ALU.mult, ALU.add))
            step(V.tensor_tensor(gli, gli, gb1, ALU.subtract))

            def running_max(e, c, initial):
                step(V.tensor_tensor_scan(span(gmax, e, c), span(gli, e, c), span(gli, e, c), initial,
                                          ALU.max, ALU.max))
                last = c * P + (P - 1 if e == 0 else 0)
                step(V.tensor_copy(mlast[:, e, c:c + 1], gmax[:, e, last:last + 1]))
                step(V.tensor_tensor(mnew[:, e, c:c + 1], mlast[:, e, c:c + 1], gb1[:, e, last:last + 1], ALU.add))

            step(V.memset(mprev, 0.0))
            v.wait_ge(S("misc_in"), 16 * 7)
            for e in range(2):
                running_max(e, 0, 0.0)
                first, second = (1, 2) if e == 0 else (2, 1)
                step(V.tensor_copy(mprev[:, e, first:first + 1], mrow[:, e:e + 1]))
                running_max(e, first, mrow[:, e:e + 1])
                step(V.tensor_copy(mprev[:, e, second:second + 1], mnew[:, e, first:first + 1]))
                running_max(e, second, mnew[:, e, first:first + 1])
            step(V.tensor_scalar_mul(gtmp, gmax, -1.0))

            def chunks(ap):
                return ap.rearrange("p e (c t) -> p (e c) t", c=C)

            def per_chunk(ap):
                return wide(ap.rearrange("p e c -> p (e c)"), 2, P)

            step(V.tensor_tensor(chunks(rows[:, 0, :, :]), chunks(gmax), per_chunk(mprev), ALU.subtract))
            step(V.tensor_tensor(rows[:, 1, :, :], gmax, gb1, ALU.add))
            step(V.tensor_tensor(chunks(rows[:, 2, :, :]), chunks(gli), per_chunk(mlast), ALU.subtract))
            step.done(V.tensor_tensor(decay, mprev, mlast, ALU.subtract), S("exp_in"), 1)
            ada_loop(0, KB, ADA_DVE)
            modulations(0, 2 * KB, 6 * KB, 2)

            v.wait_ge(S("qk_moments"), 1)
            sq30 = rope1.rearrange("p c (h d) -> p (c h) d", d=HD)
            qk = tok0[:, :, 0:640]
            step.done(V.tensor_reduce(rstat, sq30, X, ALU.add), S("qk_var"), 1)
            v.wait_ge(S("qk_moments"), 2)
            step(V.reciprocal(rstat, rstat2))
            for c in range(C):
                qc = tok0[:, c, 0:640].rearrange("p (h d) -> p h d", d=HD)
                step(V.tensor_tensor(qc, qc, wide(rstat[:, 10 * c:10 * c + 10], 2, HD), ALU.mult))
            step(V.tensor_tensor(qk, qk, wide(qkg, 1, C), ALU.mult))
            step(V.tensor_copy(knew_v, tok0[:, 0, KA:KA + P]))

            def paired(ap):
                return ap.rearrange("p (j w d) -> p w j d", w=2, d=HD)

            def plain(ap):
                return ap.rearrange("p (w j d) -> p w j d", w=2, d=HD)

            step(V.tensor_copy(paired(qkr[:, 0, 0:512]), plain(tok0[:, 0, 0:512])))
            step(V.tensor_copy(qkr[:, 0, 512:640], tok0[:, 0, 512:640]))
            for c in (1, 2):
                cosr = con("ropec")[:, (c - 1) * HD:c * HD]
                sinr = con("ropes")[:, (c - 1) * HD:c * HD].rearrange("p (a b f) -> p a b f", a=2, b=2)
                step(V.tensor_tensor(rope1[:, c, :].rearrange("p (h d) -> p h d", d=HD),
                                     tok0[:, c, 0:640].rearrange("p (h d) -> p h d", d=HD),
                                     wide(cosr, 1, 10), ALU.mult))
                x4 = tok0[:, c, 0:640].rearrange("p (h a b f) -> p h a b f", a=2, b=2, f=16)
                y4 = rope2[:, c, :].rearrange("p (h a b f) -> p h a b f", a=2, b=2, f=16)
                for b in range(2):
                    step(V.tensor_tensor(y4[:, :, :, b, :], x4[:, :, :, 1 - b, :],
                                         wide(sinr[:, :, b, :], 1, 10), ALU.mult))
                step(V.tensor_tensor(paired(qkr[:, c, 0:512]), plain(rope1[:, c, 0:512]),
                                     plain(rope2[:, c, 0:512]), ALU.add))
                step(V.tensor_tensor(qkr[:, c, 512:640], rope1[:, c, 512:640], rope2[:, c, 512:640], ALU.add))
            step.done(V.memset(vaug[:, :, :, HD:VA], 1.0), S("qk_ready"), 1)
            step(V.tensor_copy(vaug[:, :, :, 0:HD].rearrange("p c h d -> p (c h) d"),
                                    tok0[:, :, VM:VM + 512].rearrange("p c (h d) -> p c h d", d=HD)
                                    .rearrange("p c h d -> p c h d")) if False else
                      V.tensor_copy(vaug[:, :, :, 0:HD], tok0[:, :, VM:VM + 512]
                                    .rearrange("p c (h d) -> p c h d", d=HD)))
            for c in range(C):
                v.wait_ge(S("qkT_mm"), c + 1)
                step(V.tensor_copy(qaT[:, :, c * P:(c + 1) * P], ps[:, c, :].rearrange("p (j t) -> p j t", j=4)))
            v.wait_ge(S("qkT_mm"), 4)
            step(V.tensor_copy(kaT[:, 0:P], ps[:, 3, 0:P]))
            step.done(V.tensor_copy(kaT[:, 2 * P:4 * P], ps[:, 3, 2 * P:4 * P]), S("qkT_ready"), 1)
            for h in range(H_ATT + 1):
                if h < H_ATT:
                    a = h % 2
                    v.wait_ge(S("att_mm"), h + 1)
                    if h >= 2:
                        v.wait_ge(S("exp_ready"), 3 * (h - 1))
                    src = (ps[:, 2 * a, 384:512], ps[:, 2 * a, 0:384], ps[:, 2 * a + 1, 0:384])
                    for u in range(3):
                        step(V.tensor_reduce(negmax[:, a, u:u + 1], src[u], X, ALU.max))
                    step.done(V.tensor_scalar_mul(negmax[:, a, :], negmax[:, a, :], -SCALE),
                              S("max_ready"), h + 1)
                    v.wait_ge(S("attT_mm"), h + 1)
                    if h >= 2:
                        v.wait_ge(S("pv_mm"), h - 1)
                    step.done(V.tensor_copy(pexpT[:, a, 0:512], ps[:, 4, :]), S("attT_dve"), h + 1)
                if h >= 1:
                    g = h - 1
                    v.wait_ge(S("pv_mm"), h)
                    step(V.reciprocal(rrec[:, g, :], rsum[:, g, :]))
                    step.done(V.tensor_tensor(hcat[:, :, 512 + g * HD:512 + (g + 1) * HD],
                                              ps[:, 6 + g % 2, 0:C * HD].rearrange("p (c d) -> p c d", c=C),
                                              wide(rrec[:, g, :], 2, HD), ALU.mult), S("att_ready"), h)
            v.wait_ge(S("cols_mm"), 1)
            step.done(V.tensor_copy(cols, ps[:, 7, 0:192].rearrange("p (q u h) -> p q u h", q=4, u=6)),
                      S("cols_ready"), 1)
            UNITS = ((0, 0), (0, 1), (1, 0), (2, 1))
            for u, (c, e) in enumerate(UNITS):
                step.done(V.tensor_tensor(kw[:, u, :, :],
                                          tok0[:, c, KM:KM + 512].rearrange("p (h d) -> p h d", d=HD),
                                          wide(cols[:, 3, 3 * e + c, :], 2, HD), ALU.mult), S("kw_ready"), u + 1)
            for e, c in ((0, 1), (1, 2)):
                step.done(V.tensor_scalar(dspread[:, e, :], con("pm", HA), decay[:, e, c:c + 1], None, ALU.mult),
                          S("dspread_ready"), e + 1)
            v.wait_ge(S("dcol_mm"), 1)
            step.done(V.tensor_copy(dcol, ps[:, 7, 192:200].rearrange("p (e j) -> p e j", e=2)), S("dspread_ready"), 3)
            for u, (c, e) in enumerate(UNITS):
                v.wait_ge(S("state_mm"), u + 1)
                if u >= 2:
                    step(V.tensor_tensor(cst[:, 1, e, :, :], cst[:, 0, e, :, :], wide(dcol[:, e, :], 2, VA),
                                         ALU.mult))
                for half in range(2):
                    part = ps[:, 2 * u + half, 0:4 * VA].rearrange("p (j w v) -> p j w v", j=2, w=2)
                    for w in range(2):
                        r = slice(HD * w, HD * w + HD)
                        j2 = slice(2 * half, 2 * half + 2)
                        if u < 2:
                            step(V.tensor_copy(cnew[r, e, j2, :], part[r, :, w, :]))
                        else:
                            step(V.tensor_tensor(cst[r, 1, e, j2, :], part[r, :, w, :], cst[r, 1, e, j2, :],
                                                 ALU.add))
                if u % 2 == 1:
                    step.done(V.memset(itmp[:, 0:1, 0:1], 0.0), S("state_ready"), u // 2 + 1)
            for h in range(HA + 1):
                if h < HA:
                    for e in range(2):
                        v.wait_ge(S("e_ready"), 2 * h + e + 1)
                        if e == 0:
                            v.wait_ge(S("sc_mm"), h + 1)
                            if h >= 2:
                                v.wait_ge(S("num_mm"), h - 1)
                        step.done(V.tensor_tensor(pwt[:, h % 2, e, :], ps[:, h % 2, 0:T], ewt[:, e, :], ALU.mult),
                                  S("pt_ready"), 2 * h + e + 1)
                if h >= 1:
                    g = h - 1
                    v.wait_ge(S("num_mm"), h)
                    inter = ps[:, 6 + g % 2, 0:4 * VA].rearrange("p (u v) -> p u v", u=4)
                    intra = ps[:, 4 + g % 2, 0:6 * VA].rearrange("p (u v) -> p u v", u=6)
                    for e in range(2):
                        step(V.tensor_tensor(itmp[:, 2 * e:2 * e + 2, :], inter[:, 2 * e:2 * e + 2, :],
                                             wide(cols[:, 1, 3 * e + 1:3 * e + 3, g], 2, VA), ALU.mult))
                        step(V.tensor_tensor(num[:, g, 3 * e + 1:3 * e + 3, :], intra[:, 3 * e + 1:3 * e + 3, :],
                                             itmp[:, 2 * e:2 * e + 2, :], ALU.add))
                        step.done(V.tensor_copy(num[:, g, 3 * e, :], intra[:, 3 * e, :]),
                                  S("num_ready"), 2 * g + e + 1)
            den3 = den.rearrange("p (h u) -> p h u", h=HA)
            step(V.tensor_copy(den3, num[:, :, :, HD]))
            step(V.scalar_tensor_tensor(den2, den, -1.0, den, ALU.mult, ALU.max))
            step(V.tensor_tensor(den2.rearrange("p (h u) -> p u h", h=HA), den2.rearrange("p (h u) -> p u h", h=HA),
                                 cols[:, 2, :, :], ALU.max))
            step(V.reciprocal(den, den2))
            numf = num.rearrange("p h u v -> p (h u) v")[:, :, 0:HD]
            step(V.tensor_tensor(numf, numf, wide(den, 2, HD), ALU.mult))
            for e in range(1):
                step(V.tensor_tensor(hsum, num[:, :, 0:3, 0:HD], num[:, :, 3:6, 0:HD], ALU.add))
            hf = hsum.rearrange("p h c d -> p (h c) d")
            hm = hmean.rearrange("p h c -> p (h c)")
            step(V.tensor_reduce(hm, hf, X, ALU.add))
            step(V.tensor_scalar_mul(hm, hm, 1.0 / HD))
            step.done(V.tensor_tensor(hf, hf, wide(hm, 2, HD), ALU.subtract), S("h_moments"), 1)
            v.wait_ge(S("h_moments_act"), 1)
            hv = hvar.rearrange("p h c -> p (h c)")
            step.done(V.tensor_reduce(hv, hsq.rearrange("p h c d -> p (h c) d"), X, ALU.add), S("h_moments"), 2)
            v.wait_ge(S("h_moments_act"), 2)
            step(V.reciprocal(hm, hv))
            step(V.tensor_tensor(hf, hf, wide(hm, 2, HD), ALU.mult))
            v.wait_ge(S("om_ready"), 1)
            step(V.tensor_tensor(tok0[:, :, OM:OM + 512], tok0[:, :, OM:OM + 512], wide(normg, 1, C), ALU.mult))
            for c in range(C):
                step.done(V.tensor_tensor(hcat[:, c, 0:512].rearrange("p (h d) -> p h d", d=HD), hsum[:, :, c, :],
                                          tok0[:, c, OM:OM + 512].rearrange("p (h d) -> p h d", d=HD), ALU.mult),
                          S("hcat_ready"), c + 1)
            for b in range(3):
                v.wait_ge(S("hcatT_mm"), b + 1)
                if b == 0:
                    v.wait_ge(S("ctx_stored"), 16 * 4)
                step.done(V.tensor_copy(hT0[:, 0:4, b * P:(b + 1) * P],
                                        ps[:, b, :].rearrange("p (j t) -> p j t", j=4)), S("hT_ready"), b + 1)
            layer_norm(0, 0, 0, lambda b: b % 4)
            modulate(0, 1, 1)
            v.sem_inc(S("h_ready"), 2)

            def hidden(it, t):
                v.wait_ge(S("silu_ready"), it * 2 + t + 1)
                V.tensor_tensor(ffh[:, ds(it * 2 + t, 1), :].rearrange("p a t -> p (a t)"), ps[:, 2 * t + 1, 0:T],
                                silu2[:, t, :], ALU.mult).then_inc(S("h_ready"), 1)

            v.wait_ge(S("cond_ready"), 2)
            ada_loop(1, 0, FFB, hidden)
            ada_loop(1, FFB, ADA)
            modulations(1, 0, 6 * KB, 3)
            v.wait_ge(S("h_ready"), FFB + 2)
            layer_norm(0, 1, 1, lambda b: b % 4)
            modulate(1, 0, 2)
            v.wait_ge(S("soft_log"), 2)
            step(V.tensor_scalar_mul(acoef, acoef, -1.0))
            step.done(V.tensor_scalar_add(ru, rz, 1.0), S("dt_u"), 1)
            step(V.tensor_scalar_add(rd, ru, -1.0))
            step(V.tensor_tensor(rd, rz, rd, ALU.subtract))
            v.wait_ge(S("soft_log"), 3)
            step(V.reciprocal(ru, ru))
            step(V.tensor_tensor(rd, rd, ru, ALU.mult))
            step(V.tensor_tensor(rdt, rdt, rd, ALU.add))
            step(V.scalar_tensor_tensor(rdt, rx, 0.0, rdt, ALU.max, ALU.add))
            for e in range(2):
                step(V.tensor_scalar(rda[:, e, :], rdt[:, e, :], acoef[:, e:e + 1], None, ALU.mult))
            for e in range(2):
                for c in range(C):
                    step(V.tensor_tensor_scan(span(rcum, e, c), onesf[0:HC, :], span(rda, e, c), 0.0,
                                              ALU.mult, ALU.add))
            step.done(V.memset(gsd[0:1, 0:1], 0.0), S("cum_ready"), 1)

            def convolve(n, j):
                b = j % 2
                v.wait_ge(S("bc_free"), n + 3)
                w0 = PV["convw"][0]
                full = slice(0, PAD - 2)

                def col(k):
                    return pvec[:, ds(n + k, 1)]

                step(V.tensor_scalar(conv[:, b, full], raw[:, b, 1:PAD - 1], col(w0 + XBCB), col(PV["convb"][0]),
                                     ALU.mult, ALU.add))
                step(V.scalar_tensor_tensor(conv[:, b, full], raw[:, b, 0:PAD - 2], col(w0), conv[:, b, full],
                                            ALU.mult, ALU.add))
                step.ready(V.scalar_tensor_tensor(conv[:, b, full], raw[:, b, 2:PAD], col(w0 + 2 * XBCB),
                                                  conv[:, b, full], ALU.mult, ALU.add), S("conv_ready"), n + 1)

            def xg_out(it, j):
                v.wait_ge(S("xT_mm"), it * 8 + (j + 1))
                g = it * 2 + j // 4
                for c in range(C):
                    k = V.tensor_copy(xg_flat[:, ds(g * (C * 512) + (c * 512 + (j % 4) * P), P)],
                                      ps[:, 4 + j % 2, c * P:(c + 1) * P])
                k.then_inc(S("xg_ready"), 1)

            convolve(0, 0)
            at = step.n
            per = 2 * 8
            with v.Fori(0, 2) as it:
                for j in range(8):
                    step.n = it * per + (at + 2 * j)
                    convolve(it * 8 + (j + 1), j + 1)
                    xg_out(it, j)
            step.n = at + 2 * per
            v.wait_ge(S("xg_ready"), 16)
            for n in range(17, 24):
                if n == 17:
                    v.wait_ge(S("xfeat_ready"), 16)
                else:
                    v.wait_ge(S("bcT_ready"), n - 17)
                convolve(n, n)
            for c in range(C):
                v.wait_ge(S("b_mm"), c + 1)
                step.done(V.tensor_copy(btok[:, c, :], ps[:, 4 + c, :]), S("b_ready"), c + 1)
            v.wait_ge(S("ccol_mm"), 1)
            cc = ps[:, 7, 0:384].rearrange("p (q u h) -> p q u h", q=2, u=6)
            step.done(V.tensor_copy(dtc, cc[:, 0, :, :]), S("ccol_ready"), 1)
            step.done(V.tensor_copy(cumc, cc[:, 1, :, :]), S("ccol_ready"), 2)
            v.wait_ge(S("last_mm"), 1)
            lastp = ps[:, 4, 0:6 * HC].rearrange("p (u h) -> p u h", u=6)
            step(V.tensor_tensor(wsc, lastp, cumc, ALU.subtract))
            step(V.tensor_copy(elast[:, 0, :], lastp[:, 1, :]))
            step.done(V.tensor_copy(elast[:, 1, :], lastp[:, 5, :]), S("last_ready"), 1)

            def heads(ap):
                return ap.rearrange("p (h d) -> p h d", d=HD)

            def close_group(g):
                for c in range(C):
                    v.wait_ge(S("zg_ready"), C * g + c + 1)
                    step(V.tensor_tensor(zg[:, g % 2, c, :], yacc[:, c, :], zg[:, g % 2, c, :], ALU.mult))
                step.done(V.memset(inter1[:, 0:1], 0.0), S("yg_ready"), g + 1)
                v.wait_ge(S("yg_std"), g + 1)
                step(V.reciprocal(gsd, gsd))
                for c in range(C):
                    k = V.tensor_scalar(zg[:, g % 2, c, :], zg[:, g % 2, c, :], gsd[:, c:c + 1], None, ALU.mult)
                    if c < C - 1:
                        step(k)
                    else:
                        step.done(k, S("yn_ready"), g + 1)

            def group_out(g):
                for c in range(C):
                    v.wait_ge(S("yT_mm"), C * g + c + 1)
                    norm = pvec[:, PV["ssdn"][0] + 4 * g:PV["ssdn"][0] + 4 * g + 4]
                    step.done(V.tensor_tensor(yT[:, 4 * g:4 * g + 4, c * P:(c + 1) * P],
                                              ps[:, 5 + c, :].rearrange("p (j t) -> p j t", j=4),
                                              wide(norm, 2, P), ALU.mult), S("yT_ready"), C * g + c + 1)

            for g in range(NG):
                if g:
                    close_group(g - 1)
                    group_out(g - 1)
                hs = slice(g * HPG, (g + 1) * HPG)
                v.wait_ge(S("sini_in"), 16 * (g + 1))
                for e in range(2):
                    step(V.tensor_tensor(heads(sec[:, e, :]), heads(sini[:, e, :]), wide(elast[:, e, hs], 2, HD),
                                         ALU.mult))
                    v.wait_ge(S("upd_mm"), 2 * g + e + 1)
                    step.done(V.tensor_tensor(sec[:, e, :], ps[:, 6 + e, :], sec[:, e, :], ALU.add),
                              S("sec_ready"), 2 * g + e + 1)
                v.wait_ge(S("cb_ready"), g + 1)
                for r in range(HPG):
                    h = g * HPG + r
                    for e in range(2):
                        v.wait_ge(S("s_e_ready"), 2 * h + e + 1)
                        if h >= 2:
                            v.wait_ge(S("ysum_mm"), h - 1)
                        step.done(V.tensor_tensor(wdec[:, r % 2, e, :], edec[:, e, :], cb, ALU.mult),
                                  S("s_w_ready"), 2 * h + e + 1)
                    if r == 0:
                        v.wait_ge(S("yd_ready"), C * (g + 1))
                    for n in {3: (0,), 6: (1,), 7: (2, 3)}.get(r, ()):
                        e, c = n // 2, 1 + n % 2
                        v.wait_ge(S("inter_mm"), 4 * g + n + 1)
                        step(V.tensor_tensor(heads(inter1), heads(ps[:, (7, 5, 6, 7)[n], :]),
                                             wide(ecumc[:, 3 * e + c, hs], 2, HD), ALU.mult))
                        step.done(V.tensor_tensor(yacc[:, c, :], yacc[:, c, :], inter1, ALU.add),
                                  S("inter_ready"), 4 * g + n + 1)
                v.wait_ge(S("ysum_mm"), HPG * (g + 1))
                for c in range(C):
                    step.done(V.tensor_tensor(yacc[:, c, :], ps[:, c, :], yacc[:, c, :], ALU.add),
                              S("ybank_ready"), C * g + c + 1)
            close_group(NG - 1)
            group_out(NG - 1)
            layer_norm(1, 0, 2, lambda b: b % 4)
            modulate(1, 1, 3)
            v.wait_ge(S("ssd_stored"), 16 * NG)
            v.wait_ge(S("route_mm"), 1)
            step(V.tensor_tensor(logit, ps[:, 0, 0:C * NE].rearrange("p (c e) -> p c e", c=C),
                                      wide(routb, 1, C), ALU.add))

            def table(ap, n):
                return ap.rearrange("p (c e f) -> p c e f", c=C, e=n)

            mine, other = wide(logit, 3, NE), wide(logit, 2, NE)
            step(V.tensor_tensor(table(cmp1, NE), other, mine, ALU.is_gt))
            step(V.tensor_tensor(table(cmp2, NE), other, mine, ALU.is_equal))
            step(V.tensor_tensor(cmp2.rearrange("p (c n) -> p c n", c=C), cmp2.rearrange("p (c n) -> p c n", c=C),
                                 wide(con("tie"), 1, C), ALU.mult))
            step(V.tensor_tensor(cmp1, cmp1, cmp2, ALU.add))
            step(V.tensor_reduce(rank, table(cmp1, NE), X, ALU.add))
            step.done(V.tensor_scalar(sel, rank, 2.0, None, ALU.is_lt), S("sel_ready"), 1)
            step(V.tensor_reduce(vmax, logit, X, ALU.max))
            step.done(V.tensor_tensor(expl, logit, wide(vmax, 2, NE), ALU.subtract), S("sel_ready"), 2)
            v.wait_ge(S("expl_ready"), 1)
            step(V.tensor_tensor(expl, expl, sel, ALU.mult))
            step(V.tensor_reduce(gsum, expl, X, ALU.add))
            step(V.reciprocal(gsum, gsum))
            step(V.tensor_tensor(gate, expl, wide(gsum, 2, NE), ALU.mult))
            v.wait_ge(S("route_mm"), 2)
            step(V.tensor_scalar_add(ppos, ps[:, 1, 0:C * NE].rearrange("p (c e) -> p c e", c=C), 1.0))
            step(V.tensor_tensor(ppos, ppos, sel, ALU.mult))
            step(V.tensor_scalar_add(ppos, ppos, -1.0))
            step(V.tensor_copy(cnt, ps[:, 1, C * NE:(C + 1) * NE]))
            step(V.tensor_copy(posi[:, :, 0:NE], ppos))
            step(V.tensor_copy(gatei[:, :, 0:NE], gate))
            for j in range(2):
                step(V.tensor_scalar(have[:, NE * j:NE * j + NE], cnt, float(P * (j + 1)), None, ALU.is_gt))
                step(V.tensor_copy(pp2.rearrange("p (c n) -> p c n", c=C)[:, :, NE * j:NE * j + NE], ppos))
                step(V.tensor_copy(gg2.rearrange("p (c n) -> p c n", c=C)[:, :, NE * j:NE * j + NE], gate))
            step(V.tensor_tensor_scan(order, onesf[:, 0:16], have, 0.0, ALU.mult, ALU.add))
            step(V.tensor_scalar_add(listf[:, ITEMS:ITEMS + 1], order[:, 15:16], float(NE)))
            step(V.tensor_tensor(order, order, have, ALU.subtract))
            hot2 = hot.rearrange("p (i n) -> p i n", i=OVER)
            step(V.tensor_tensor(hot2, wide(order, 1, OVER), wide(con("irow"), 2, 16), ALU.is_equal))
            step(V.tensor_tensor(hot2, hot2, wide(have, 1, OVER), ALU.mult))
            big2 = big[:, 0:OVER * 16].rearrange("p (i n) -> p i n", i=OVER)
            step(V.tensor_tensor(big2, hot2, wide(con("jrow"), 1, OVER), ALU.mult))
            step(V.tensor_reduce(jover, big2, X, ALU.add))
            step(V.tensor_scalar_mul(jover, jover, float(P)))
            step(V.tensor_tensor(big2, hot2, wide(con("erow"), 1, OVER), ALU.mult))
            step(V.tensor_reduce(eover, big2, X, ALU.add))
            step(V.tensor_copy(listf[:, NE:ITEMS], eover))
            step(V.tensor_copy(listf[:, 0:NE], con("erow")[:, 0:NE]))
            step(V.memset(listf[:, ITEMS + 1:16], 0.0))
            for src, dst in ((pp2, posi), (gg2, gatei)):
                for c in range(C):
                    step(V.tensor_tensor(big2, hot2, wide(src[:, 16 * c:16 * c + 16], 1, OVER), ALU.mult))
                    step(V.tensor_reduce(dst[:, c, NE:ITEMS], big2, X, ALU.add))
            step(V.tensor_tensor(posi[:, :, NE:ITEMS], posi[:, :, NE:ITEMS], wide(jover, 1, C), ALU.subtract))
            step.done(V.tensor_copy(lists[:, :], listf[0:1, :]), S("routed"), 1)
            for n in range(3):
                v.wait_ge(S("utok_mm"), 2 * n + 1)
                step.done(V.tensor_copy(utok[:, n, 0:512], ps[:, 2 + 2 * (n % 2), :]), S("utok_dve"), n + 1)
            v.wait_ge(S("utok_mm"), 6)
            step(V.memset(acc[:, :, :], 0.0))
            n_items = v.value_load(lists[0:1, ITEMS:ITEMS + 1], min_val=NE, max_val=ITEMS)
            with v.Fori(0, n_items) as it:
                for c in range(C):
                    V.tensor_scalar(disp[:, c, :], con("iota"), posi[:, c, ds(it, 1)], None, ALU.is_equal) \
                        .then_inc(S("disp_ready"), 1)
                for c in range(C):
                    V.tensor_scalar(gdisp[:, c, :], con("iota"), posi[:, c, ds(it, 1)], gatei[:, c, ds(it, 1)],
                                    ALU.is_equal, ALU.mult).then_inc(S("disp_ready"), 1)
                v.wait_ge(S("xe_mm"), it * 2 + 2)
                V.tensor_copy(xe[:, 4:8, :], ps[:, 5, :].rearrange("p (k s) -> p k s", k=4)).then_inc(S("xe_dve"), 1)
                v.wait_ge(S("comb_mm"), it + 1)
                V.tensor_copy(comb, ps[:, 6, 0:T]).then_inc(S("comb_ready"), 1)
                for f in range(4):
                    v.wait_ge(S("msilu_ready"), it * 4 + f + 1)
                    V.tensor_tensor(he[:, f * (FE // 4):(f + 1) * (FE // 4)], ps[:, 2 * (f % 2) + 1, 0:FE // 4],
                                    sige[:, f % 2, :], ALU.mult).then_inc(S("mh_ready"), 1)
                v.wait_ge(S("mhT_mm"), it * 3 + 2)
                V.tensor_copy(heT[:, 4:8, :], ps[:, 5, :].rearrange("p (f s) -> p f s", s=P)) \
                    .then_inc(S("mhT_dve"), 1)
                for b in range(KB):
                    v.wait_ge(S("madd_mm"), it * KB + b + 1)
                    V.tensor_tensor(acc[:, b, :], ps[:, 5 + b % 2, 0:T], acc[:, b, :], ALU.add) \
                        .then_inc(S("macc_ready"), 1)
                v.wait_ge(S("macc_ready"), it * KB + KB)
            v.wait_ge(S("ax_ready"), 4)
            for b in range(KB):
                for grp, t0, t1 in GROUPS:
                    z = V.scalar_tensor_tensor(zT[:, b, t0:t1], acc[:, b, t0:t1], mod(1, 5, b, grp), xT[:, b, t0:t1],
                                               ALU.mult, ALU.add)
                    if grp == 0:
                        step(z)
                step.done(z, S("z_ready"), KB * 3 + b + 1)
            norm_steps(3)

        @block.tensor
        def _(pe):
            M = nc.tensor

            def ada(bank, name, t0, n, c0):
                first = FIRST[name] + t0
                with pe.Fori(0, n // RING) as it:
                    for j in range(RING):
                        g = first + j
                        pe.wait_ge(ready[g % RING], it * 16 + 16 * (g // RING + 1))
                        w = slot(g % RING)
                        for b in range(2):
                            for k in range(KB):
                                m = M.matmul(ps[:, bank, ds(it * 16 + (c0 + 4 * j + 2 * b), 2)],
                                             w[:, k * 256 + b * P:k * 256 + (b + 1) * P], cact[:, k, :],
                                             start=k == 0, stop=k == KB - 1)
                        m.then_inc(S("ada_mm"), 1)

            def layer_norm(ln, between=None):
                for b in range(KB):
                    pe.wait_ge(S("z_ready"), KB * ln + b + 1)
                    m = M.matmul(ps[:, 6, 0:T], onesm[:, :], zT[:, b, :], start=b == 0, stop=b == KB - 1)
                m.then_inc(S("mean_mm"), 1)
                if between:
                    between()
                for b in range(KB):
                    pe.wait_ge(S("sq_ready"), 4 * ln + b // 2 + 1)
                    m = M.matmul(ps[:, 7, 0:T], onesm[:, :], sqT[:, b, :], start=b == 0, stop=b == KB - 1)
                m.then_inc(S("var_mm"), 1)

            def out_blocks(name, ln, src, per, kb):
                for b in range(KB):
                    g = FIRST[name] + b // per
                    pe.wait_ge(*tile_ready(g))
                    if b >= 4:
                        pe.wait_ge(S("z_ready"), KB * ln + b - 3)
                    w = slot(g % RING)
                    for k in range(kb):
                        m = M.matmul(ps[:, b % 4, 0:T], w[:, k * per * P + (b % per) * P:k * per * P + (b % per + 1) * P],
                                     src(k), start=k == 0, stop=k == kb - 1)
                    m.then_inc(S("y_mm"), 1)

            pe.wait_ge(S("cact_ready"), 1)
            ada(5, "ada0a", 0, ADA_PE, 0)
            pe.wait_ge(*tile_ready(FIRST["gate"]))
            w = slot(FIRST["gate"] % RING)
            for k in range(KB):
                pe.wait_ge(S("u_ready"), k + 1)
                m = M.matmul(ps[0:32, 2, 0:T], w[:, k * 32:(k + 1) * 32], uT[:, k, :], start=k == 0, stop=k == KB - 1)
            m.then_inc(S("gate_mm"), 1)
            for j in range(4):
                g = FIRST["qm"] + j // 2
                pe.wait_ge(*tile_ready(g))
                if j >= 2:
                    pe.wait_ge(S("qm_ready"), j - 1)
                for k in range(KB):
                    c0 = k * 256 + (j % 2) * P
                    m = M.matmul(ps[:, j % 2, 0:T], slot(g % RING)[:, c0:c0 + P], uT[:, k, :],
                                 start=k == 0, stop=k == KB - 1)
                m.then_inc(S("qm_mm"), 1)
            with pe.Fori(0, 2) as it:
                for j in range(4):
                    g = FIRST["tok"] + j
                    pe.wait_ge(ready[g % RING], it * 16 + 16 * (g // RING + 1))
                    pe.wait_ge(S("tok_free"), it * 4 + j + 1)
                    for c in range(C):
                        for k in range(KB):
                            m = M.matmul(ps[:, 3 * (j % 2) + c, 0:TOKW], uT[:, k, c * P:(c + 1) * P],
                                         slot(g % RING)[:, k * TOKW:(k + 1) * TOKW],
                                         start=k == 0, stop=k == KB - 1)
                    m.then_inc(S("tok_mm"), 1)
            pe.wait_ge(S("tok_free"), 10)
            pe.wait_ge(S("qk_ready"), 1)
            for c in range(C):
                for j in range(4):
                    m = M.transpose(ps[:, c, j * P:(j + 1) * P], qkr[:, c, j * P:(j + 1) * P], ident)
                m.then_inc(S("qkT_mm"), 1)
            for c, at in ((0, 0), (1, 2), (2, 3)):
                m = M.transpose(ps[:, 3, at * P:(at + 1) * P], qkr[:, c, 512:640], ident)
            m.then_inc(S("qkT_mm"), 1)
            pe.wait_ge(S("mods_ready"), 2)
            for c in range(C):
                for j in range(4):
                    m = M.transpose(ps[:, 4 + c, j * P:(j + 1) * P], tok0[:, c, KM + j * P:KM + (j + 1) * P], ident)
                m.then_inc(S("tr_mm"), 1)
            pe.wait_ge(S("qkT_ready"), 1)
            pe.wait_ge(S("kmT_ready"), 3)
            pe.wait_ge(S("misc_in"), 16 * 7)

            def scores(h):
                a, j = h % 2, h % 4
                r = slice(HD * (h // 4), HD * (h // 4) + HD)
                if h >= 2:
                    pe.wait_ge(S("exp_ready"), 3 * (h - 1))
                M.matmul(ps[:, 2 * a, 384:512], qaT[r, j, 0:P], kaT[r, 0:P], start=True, stop=True)
                M.matmul(ps[:, 2 * a, 0:384], qaT[r, j, P:2 * P], kaT[r, P:4 * P], start=True, stop=True)
                M.matmul(ps[:, 2 * a + 1, 0:384], qaT[r, j, 2 * P:3 * P], kaT[r, P:4 * P],
                         start=True, stop=True).then_inc(S("att_mm"), 1)

            def turn(h):
                pe.wait_ge(S("exp_ready"), 3 * h + 3)
                if h >= 1:
                    pe.wait_ge(S("attT_dve"), h)
                    pe.wait_ge(S("attT_act"), h)
                for n in range(7):
                    m = M.transpose(ps[:, 4 + n // 4, (n % 4) * P:(n % 4 + 1) * P],
                                    pexp[:, h % 2, n * P:(n + 1) * P], ident)
                m.then_inc(S("attT_mm"), 1)

            def values(h):
                pe.wait_ge(S("attT_dve"), h + 1)
                pe.wait_ge(S("attT_act"), h + 1)
                if h >= 2:
                    pe.wait_ge(S("att_ready"), h - 1)
                kv = (h // 4) * HD
                out = ps[:, 6 + h % 2, 0:C * HD]
                keys = (vcache[:, kv:kv + HD], tok0[:, 1, VAT + kv:VAT + kv + HD], tok0[:, 2, VAT + kv:VAT + kv + HD])
                M.matmul(out[:, 0:HD], pexpT[:, h % 2, 0:P], tok0[:, 0, VAT + kv:VAT + kv + HD], start=True, stop=True)
                for q in range(2):
                    for n in range(3):
                        c0 = P + (3 * q + n) * P
                        m = M.matmul(out[:, (q + 1) * HD:(q + 2) * HD], pexpT[:, h % 2, c0:c0 + P], keys[n],
                                     start=n == 0, stop=n == 2)
                m.then_inc(S("pv_mm"), 1)

            scores(0)
            for h in range(H_ATT):
                if h + 1 < H_ATT:
                    scores(h + 1)
                turn(h)
                values(h)
            pe.wait_ge(S("rows_ready"), 1)
            pe.wait_ge(S("att_ready"), H_ATT)
            for q in range(4):
                for u in range(6):
                    src = gli if q == 0 else rows[:, q - 1, :, :]
                    m = M.transpose(ps[:, 7, (6 * q + u) * HA:(6 * q + u + 1) * HA],
                                    src[:, u // 3, (u % 3) * P:(u % 3 + 1) * P], ident[0:HA, 0:HA])
            m.then_inc(S("cols_mm"), 1)
            pe.wait_ge(S("dspread_ready"), 2)
            M.matmul(ps[:, 7, 192:200], con("selp", HA), dspread.rearrange("p e j -> p (e j)"),
                     start=True, stop=True).then_inc(S("dcol_mm"), 1)
            pe.wait_ge(S("dspread_ready"), 3)
            for u, c in enumerate((0, 0, 1, 2)):
                pe.wait_ge(S("kw_ready"), u + 1)
                for j in range(4):
                    m = M.matmul(ps[:, 2 * u + j // 2, (j % 2) * 2 * VA:(j % 2 + 1) * 2 * VA],
                                 kw[:, u, 2 * j:2 * j + 2, :].rearrange("p h d -> p (h d)"),
                                 vaug[:, c, 2 * j:2 * j + 2, :].rearrange("p h v -> p (h v)"), start=True, stop=True)
                m.then_inc(S("state_mm"), 1)
            pe.wait_ge(S("state_ready"), 2)
            pe.wait_ge(S("b16_ready"), 1)

            def pair(h):
                return slice(HD * (h % 2), HD * (h % 2) + HD)

            def mlstm_scores(h):
                r, j = pair(h), h // 2
                if h >= 2:
                    pe.wait_ge(S("pt_ready"), 2 * (h - 2) + 2)
                for c in range(C):
                    t = slice(c * P, (c + 1) * P)
                    m = M.matmul(ps[:, h % 2, t], kmT[r, j, t], qmT[r, j, t], start=True, stop=True)
                m.then_inc(S("sc_mm"), 1)
                for e in range(2):
                    if h >= 1:
                        pe.wait_ge(S("e_ready"), 2 * (h - 1) + e + 1)
                    M.matmul(ps[:, 2 + e, 0:T], ident[0:HA, h:h + 1].broadcast_to([HA, P]), gtmp[:, e, :],
                             start=True, stop=False)
                    M.matmul(ps[:, 2 + e, 0:T], identb16[:, :], wide(maskb16[:, e, :], 1, C),
                             start=False, stop=True).then_inc(S("bc_mm"), 1)

            def mlstm_values(h):
                r, j = pair(h), h // 2
                pe.wait_ge(S("pt_ready"), 2 * h + 2)
                if h >= 2:
                    pe.wait_ge(S("num_ready"), 2 * (h - 2) + 2)
                for e in range(2):
                    for c in range(C):
                        u = 3 * e + c
                        M.matmul(ps[:, 4 + h % 2, u * VA:(u + 1) * VA], pwt[:, h % 2, e, c * P:(c + 1) * P],
                                 vaug[:, c, h, :], start=True, stop=True)
                for e in range(2):
                    for c in (1, 2):
                        u = 2 * e + c - 1
                        which = (c - 1) if e == 0 else (2 - c)
                        m = M.matmul(ps[:, 6 + h % 2, u * VA:(u + 1) * VA], qmT[r, j, c * P:(c + 1) * P],
                                     cst[r, which, e, j, :], start=True, stop=True)
                m.then_inc(S("num_mm"), 1)

            mlstm_scores(0)
            for h in range(HA):
                if h + 1 < HA:
                    mlstm_scores(h + 1)
                mlstm_values(h)
            pe.wait_ge(S("num_ready"), 2 * HA)
            for c in range(C):
                for j in range(4):
                    m = None
                pass
            for b in range(6):
                half, c = b // 3, b % 3
                pe.wait_ge(S("hcat_ready"), c + 1 if half == 0 else 3)
                for j in range(4):
                    m = M.transpose(ps[:, b, j * P:(j + 1) * P],
                                    hcat[:, c, half * 512 + j * P:half * 512 + (j + 1) * P], ident)
                m.then_inc(S("hcatT_mm"), 1)
            pe.wait_ge(S("hT_ready"), 3)
            pe.wait_ge(S("hT_act"), 3)
            out_blocks("mixo", 0, lambda k: hT0[:, k, :], 2, KB)
            layer_norm(0)
            pe.wait_ge(S("u_ready"), 2 * KB)

            def up_tile(g, sem_base, t):
                w = slot(g % RING)
                for n in range(2):
                    for k in range(KB):
                        m = M.matmul(ps[:, 2 * (t % 2) + n, 0:T], w[:, (n * KB + k) * P:(n * KB + k + 1) * P],
                                     uT[:, k, :], start=k == 0, stop=k == KB - 1)
                m.then_inc(S("up_mm"), 1)

            loops = FFB // RING
            with pe.Fori(0, loops) as it:
                for j in range(RING):
                    g = FIRST["up"] + j
                    pe.wait_ge(ready[g % RING], it * 16 + 16 * (g // RING + 1))
                    pe.wait_ge(S("h_ready"), it * RING + j + 1)
                    up_tile(g, 0, j)
            for t in range(loops * RING, FFB):
                g = FIRST["up"] + t
                pe.wait_ge(*tile_ready(g))
                pe.wait_ge(S("h_ready"), t + 1)
                up_tile(g, 0, t)
            pe.wait_ge(S("h_ready"), FFB + 2)
            out_blocks("down", 1, lambda k: ffh[:, k, :], 1, FFB)
            layer_norm(1)
            g = FIRST["dt"]
            pe.wait_ge(*tile_ready(g))
            for e in range(2):
                for k in range(KB):
                    pe.wait_ge(S("u_ready"), 2 * KB + k + 1)
                    m = M.matmul(ps[0:HC, e, 0:T], slot(g % RING)[:, k * 64 + e * HC:k * 64 + (e + 1) * HC],
                                 uT[:, k, :], start=k == 0, stop=k == KB - 1)
            m.then_inc(S("dt_mm"), 1)

            def xbc_block(g, j, n):
                pe.wait_ge(S("bc_free"), n + 1)
                for k in range(KB):
                    c0 = k * 256 + (j % 2) * P
                    m = M.matmul(ps[:, 2 + j % 2, 0:T], slot(g % RING)[:, c0:c0 + P], uT[:, k, :],
                                 start=k == 0, stop=k == KB - 1)
                m.then_inc(S("xbc_mm"), 1)

            def turn_x(it, j):
                pe.wait_ge(S("xfeat_ready"), it * 8 + (j + 1))
                for c in range(C):
                    m = M.transpose(ps[:, 4 + j % 2, c * P:(c + 1) * P], xfeat[:, j % 2, c * P:(c + 1) * P], ident)
                m.then_inc(S("xT_mm"), 1)

            pe.wait_ge(S("mods_ready"), 3)
            pe.wait_ge(*tile_ready(FIRST["xbc"]))
            for n in range(2):
                xbc_block(FIRST["xbc"], n, n)
            with pe.Fori(0, 2) as it:
                for j in range(8):
                    g = FIRST["xbc"] + (j + 2) // 2
                    if j % 2 == 0:
                        pe.wait_ge(ready[g % RING], it * 16 + 16 * (g // RING + 1))
                    xbc_block(g, j, it * 8 + (j + 2))
                    turn_x(it, j)
            for n in range(18, 24):
                g = FIRST["xbc"] + n // 2
                pe.wait_ge(*tile_ready(g))
                xbc_block(g, n, n)
            pe.wait_ge(S("cum_ready"), 1)
            for q, src in ((0, rdt), (1, rcum)):
                for u in range(6):
                    m = M.transpose(ps[:, 7, (6 * q + u) * HC:(6 * q + u + 1) * HC],
                                    src[:, u // 3, (u % 3) * P:(u % 3 + 1) * P], ident[0:HC, 0:HC])
            m.then_inc(S("ccol_mm"), 1)
            pe.wait_ge(S("xg_ready"), 16)
            for c in range(C):
                for g in range(NG):
                    pe.wait_ge(S("bcT_ready"), g + 1)
                    m = M.transpose(ps[:, 4 + c, g * P:(g + 1) * P], bcT[:, g, c * P:(c + 1) * P], ident)
                m.then_inc(S("b_mm"), 1)
            pe.wait_ge(S("ccol_ready"), 2)
            pe.wait_ge(S("b_ready"), 3)
            for e in range(2):
                t = (P - 1, 0)[e]
                m = M.matmul(ps[:, 4, e * 3 * HC:(e + 1) * 3 * HC], ident[:, t:t + 1].broadcast_to([P, P]),
                             cumc[:, 3 * e:3 * e + 3, :].rearrange("p u h -> p (u h)"), start=True, stop=True)
            m.then_inc(S("last_mm"), 1)

            def gate_cols(g):
                for n in range(2):
                    t = FIRST["z"] + 2 * g + n
                    pe.wait_ge(*tile_ready(t))
                    for c in range(C):
                        for k in range(KB):
                            m = M.matmul(ps[:, 5 + c, n * 256:(n + 1) * 256], uT[:, k, c * P:(c + 1) * P],
                                         slot(t % RING)[:, k * 256:(k + 1) * 256], start=k == 0, stop=k == KB - 1)
                    m.then_inc(S("z_mm"), 1)

            def decay_rows(h):
                for e in range(2):
                    if h:
                        pe.wait_ge(S("s_e_ready"), 2 * (h - 1) + e + 1)
                    M.matmul(ps[:, 3 + e, 0:T], ident[0:HC, h:h + 1].broadcast_to([HC, P]), rcum[:, e, :],
                             start=True, stop=False)
                    M.matmul(ps[:, 3 + e, 0:T], identb16[:, :], wide(maskb16[:, e, :], 1, C),
                             start=False, stop=True).then_inc(S("s_bc_mm"), 1)

            def head_sums(g, r):
                h = g * HPG + r
                pe.wait_ge(S("s_w_ready"), 2 * h + 2)
                if r == 0:
                    pe.wait_ge(S("xdt_ready"), 2 * g + 2)
                    if g:
                        pe.wait_ge(S("ybank_ready"), C * g)
                for c in range(C):
                    for e in range(2):
                        m = M.matmul(ps[:, c, r * HD:(r + 1) * HD], wdec[:, r % 2, e, c * P:(c + 1) * P],
                                     xdt[:, e, c, r * HD:(r + 1) * HD], start=e == 0, stop=e == 1)
                m.then_inc(S("ysum_mm"), 1)

            def turn_y(g):
                pe.wait_ge(S("yn_ready"), g + 1)
                for c in range(C):
                    for j in range(4):
                        m = M.transpose(ps[:, 5 + c, j * P:(j + 1) * P], zg[:, g % 2, c, j * P:(j + 1) * P], ident)
                    m.then_inc(S("yT_mm"), 1)

            def extra(g, r):
                if r == 0:
                    for e in range(2):
                        pe.wait_ge(S("xw_ready"), 4 * g + 3 + e)
                        M.matmul(ps[:, 6 + e, :], btok[:, 1 + e, g * P:(g + 1) * P], xw[:, 2 + e, :],
                                 start=True, stop=True).then_inc(S("upd_mm"), 1)
                elif r in (1, 3):
                    e = r // 2
                    if e:
                        pe.wait_ge(S("sec_ready"), 2 * g + 1)
                    for j in range(4):
                        m = M.matmul(ps[:, 5 + e, j * P:(j + 1) * P], xw[:, e, j * P:(j + 1) * P],
                                     btok[:, 0, g * P:(g + 1) * P], start=True, stop=True)
                    m.then_inc(S("out_mm"), 1)

            def inter(g, n):
                e, c = n // 2, 1 + n % 2
                if n == 0:
                    pe.wait_ge(S("sec_ready"), 2 * g + 2)
                elif n < 3:
                    pe.wait_ge(S("snew_half"), 2 * g + n)
                else:
                    pe.wait_ge(S("inter_ready"), 4 * g + 1)
                state = sini[:, e, :] if (c == 1) == (e == 0) else sec[:, e, :]
                M.matmul(ps[:, (7, 5, 6, 7)[n], :], bcT[:, NG + g, c * P:(c + 1) * P], state,
                         start=True, stop=True).then_inc(S("inter_mm"), 1)

            pe.wait_ge(S("cumc_ready"), 1)
            pe.wait_ge(S("wexp_ready"), 1)
            for g in range(NG):
                gate_cols(g)
                if g:
                    pe.wait_ge(S("zg_ready"), C * (g + 1))
                    turn_y(g - 1)
                if g:
                    pe.wait_ge(S("s_e_ready"), 2 * HPG * g)
                for c in range(C):
                    t = slice(c * P, (c + 1) * P)
                    pe.wait_ge(S("bcT_ready"), 8)
                    m = M.matmul(ps[:, 3, t], bcT[:, g, t], bcT[:, NG + g, t], start=True, stop=True)
                m.then_inc(S("cb_mm"), 1)
                pe.wait_ge(S("cb_ready"), g + 1)
                pe.wait_ge(S("zg_ready"), C * (g + 1))
                if g:
                    pe.wait_ge(S("yT_ready"), C * g)
                decay_rows(g * HPG)
                extra(g, 0)
                for r in range(HPG):
                    if r + 1 < HPG:
                        decay_rows(g * HPG + r + 1)
                    head_sums(g, r)
                    if r >= 1:
                        extra(g, r)
                    if r == 1:
                        inter(g, 0)
                    elif r in (4, 5, 6):
                        inter(g, r - 3)
                if g < NG - 1:
                    pe.wait_ge(S("inter_ready"), 4 * (g + 1))
            pe.wait_ge(S("inter_ready"), 4 * NG)
            turn_y(NG - 1)
            pe.wait_ge(S("yT_ready"), C * NG)
            out_blocks("ssdo", 2, lambda k: yT[:, k, :], 1, 16)
            layer_norm(2)
            for c in range(C):
                for k in range(KB):
                    pe.wait_ge(S("u_ready"), 3 * KB + k + 1)
                    m = M.matmul(ps[:, 0, c * NE:(c + 1) * NE], uT[:, k, c * P:(c + 1) * P], routw[:, k, :],
                                 start=k == 0, stop=k == KB - 1)
            m.then_inc(S("route_mm"), 1)
            for c in range(C):
                for half in range(2):
                    if c == 2:
                        pe.wait_ge((S("utok_dve"), S("utok_act"))[half], 1)
                    for j in range(4):
                        k = 4 * half + j
                        m = M.transpose(ps[:, 2 + 2 * (c % 2) + half, j * P:(j + 1) * P],
                                        uT[:, k, c * P:(c + 1) * P], ident)
                    m.then_inc(S("utok_mm"), 1)
                if c == 1:
                    pe.wait_ge(S("sel_ready"), 1)
                    for c1 in range(C):
                        for c0 in range(c1 + 1):
                            M.matmul(ps[:, 1, c1 * NE:(c1 + 1) * NE], con("tri") if c0 == c1 else onesf[:, :],
                                     sel[:, c0, :], start=c0 == 0, stop=c0 == c1)
                    for c0 in range(C):
                        m = M.matmul(ps[:, 1, C * NE:(C + 1) * NE], onesf[:, :], sel[:, c0, :],
                                     start=c0 == 0, stop=c0 == C - 1)
                    m.then_inc(S("route_mm"), 1)
            pe.wait_ge(S("routed"), 1)
            pe.wait_ge(S("utok_dve"), 3)
            pe.wait_ge(S("utok_act"), 3)
            n_items = pe.value_load(lists[0:1, ITEMS:ITEMS + 1], min_val=NE, max_val=ITEMS)
            with pe.Fori(0, n_items) as it:
                pe.wait_ge(S("disp_ready"), it * (2 * C) + C)
                for b in range(KB):
                    for c in range(C):
                        m = M.matmul(ps[:, 4 + b // 4, (b % 4) * P:(b % 4 + 1) * P], utok[:, c, b * P:(b + 1) * P],
                                     disp[:, c, :], start=c == 0, stop=c == C - 1)
                    if b % 4 == 3:
                        m.then_inc(S("xe_mm"), 1)
                pe.wait_ge(S("disp_ready"), it * (2 * C) + 2 * C)
                for c in range(C):
                    m = M.transpose(ps[:, 6, c * P:(c + 1) * P], gdisp[:, c, :], ident)
                m.then_inc(S("comb_mm"), 1)
                pe.wait_ge(S("xe_act"), it + 1)
                pe.wait_ge(S("xe_dve"), it + 1)

                def turn_h(n, need):
                    pe.wait_ge(S("mh_ready"), it * 4 + need)
                    if n == 2:
                        pe.wait_ge(S("comb_ready"), it + 1)
                    for f in range(4 * n, min(4 * n + 4, FEB)):
                        m = M.transpose(ps[:, 4 + n, (f % 4) * P:(f % 4 + 1) * P], he[:, f * P:(f + 1) * P], ident)
                    m.then_inc(S("mhT_mm"), 1)

                W = FE // 4
                for f in range(4):
                    if f >= 2:
                        pe.wait_ge(S("mh_ready"), it * 4 + (f - 1))
                    for n in range(2):
                        pe.wait_ge(ready[2 * f + n], it * 16 + (moe_base[2 * f + n] + 16))
                    for k in range(KB):
                        for n in range(2):
                            m = M.matmul(ps[:, 2 * (f % 2) + n, 0:W], xe[:, k, :],
                                         slot(2 * f + n)[:, k * W:(k + 1) * W], start=k == 0, stop=k == KB - 1)
                    m.then_inc(S("mup_mm"), 1)
                    if f == 3:
                        turn_h(0, 2)
                        turn_h(1, 3)
                turn_h(2, 4)
                pe.wait_ge(S("mhT_act"), it * 2 + 2)
                pe.wait_ge(S("mhT_dve"), it + 1)
                for n in range(4):
                    pe.wait_ge(ready[8 + n], it * 16 + 16)
                    for f in range(FEB):
                        m = M.matmul(ps[:, (7, 4)[n // 2], (n % 2) * 256:(n % 2 + 1) * 256], heT[:, f, :],
                                     slot(8 + n)[:, f * 256:(f + 1) * 256], start=f == 0, stop=f == FEB - 1)
                    m.then_inc(S("my_mm"), 1)
                for b in range(KB):
                    pe.wait_ge(S("ye_ready"), it * 2 + 1 + b // 4)
                    if b >= 2:
                        pe.wait_ge(S("macc_ready"), it * KB + b - 1)
                    M.matmul(ps[:, 5 + b % 2, 0:T], ye[:, b * P:(b + 1) * P], comb,
                             start=True, stop=True).then_inc(S("madd_mm"), 1)
                pe.wait_ge(S("macc_ready"), it * KB + KB)
            layer_norm(3)


def blocks(w, n):
    w = np.asarray(w)
    k, m = w.shape
    return np.ascontiguousarray(w.reshape(k // P, P, m // n, n).transpose(2, 1, 0, 3)).reshape(m // n, P, -1)


def columns(v):
    return np.asarray(v).reshape(-1, P).T


def constants():
    c = np.zeros((P, NCONST), np.float32)

    def put(name, a):
        c[0:a.shape[0], CI[name][0]:CI[name][0] + a.shape[1]] = a

    put("ident", np.eye(P, dtype=np.float32))
    nf = HD // 4
    inv = (10000.0 ** (-np.arange(nf, dtype=np.float32) / nf)).astype(np.float32)
    t = np.arange(TS)
    row, col = (t // 64).astype(np.float32), (t % 64).astype(np.float32)
    cr, sr = np.cos(row[:, None] * inv), np.sin(row[:, None] * inv)
    cc, sc = np.cos(col[:, None] * inv), np.sin(col[:, None] * inv)
    cos = np.concatenate([cr, cr, cc, cc], 1)
    sin = np.concatenate([-sr, sr, -sc, sc], 1)
    put("ropec", np.concatenate([cos[:P], cos[P:]], 1))
    put("ropes", np.concatenate([sin[:P], sin[P:]], 1))
    put("iota", np.broadcast_to(np.arange(P, dtype=np.float32), (P, P)))
    a = np.arange(P)
    put("tri", (a[:, None] < a[None, :]).astype(np.float32))
    e = np.arange(NE)
    put("tie", np.broadcast_to((e[None, :] < e[:, None]).astype(np.float32).reshape(1, -1), (P, 64)))
    put("selp", ((np.arange(HA) % 2)[:, None] == (a // HD)[None, :]).astype(np.float32))
    put("pm", ((np.arange(HA) // 2)[:, None] == np.arange(4)[None, :]).astype(np.float32))
    put("jrow", np.broadcast_to(np.repeat(np.float32([1, 2]), NE), (P, 16)))
    put("erow", np.broadcast_to(np.tile(np.arange(NE, dtype=np.float32), 2), (P, 16)))
    put("irow", np.broadcast_to(np.arange(OVER, dtype=np.float32), (P, OVER)))
    return c


def kernel(**inputs):
    from concourse import bacc
    from concourse.bass_utils import run_bass_kernel_spmd

    a = {k: np.asarray(v) for k, v in inputs.items()}
    x = np.concatenate([a["x_prompt"][0], a["x_sample"][0]], 0)
    t = np.arange(P)
    arr = {
        "consts": constants(),
        "masks": np.ascontiguousarray(np.stack([np.where(t[None, :] >= t[:, None], 0, -1e30),
                                                np.where(t[None, :] <= t[:, None], 0, -1e30)], 1), np.float32),
        "pvec": np.concatenate([columns(a["ada_b_l0"]), columns(a["ada_b_l1"])]
                               + [columns(a[f"ln{n}_{p}_l{l}"]) for l in (0, 1) for n in (1, 2) for p in "gb"]
                               + [columns(a["ssd_conv_w_l1"]), columns(a["ssd_conv_b_l1"]),
                                  columns(a["ssd_norm_g_l1"])], 1),
        "cvec": np.ascontiguousarray(np.stack([a["c_ctx"], a["c"][0]], 1).reshape(KB, P, 2).transpose(1, 0, 2)),
        "xT": np.ascontiguousarray(x.T.reshape(KB, P, T).transpose(1, 0, 2)),
    }
    wi = a["mix_w_in_l0"]
    arr["w_ada0a"] = blocks(a["ada_w_l0"][:, :256 * ADA_PE], 256)
    arr["w_adav0"], arr["w_adav1"] = (a[f"ada_w_l{l}"].T.reshape(ADA, 2, P, D).transpose(0, 2, 1, 3)
                                      .reshape(ADA, P, 2 * D)[ADA_PE * (1 - l):] for l in range(2))
    arr["cond"] = np.concatenate([a["c_ctx"], a["c"][0]])
    o = np.cumsum([0, 512, 512, 512, 512, 32, 512, 128, 128])
    arr["w_gate"] = blocks(wi[:, o[4]:o[5]], 32)
    arr["w_qm"] = blocks(wi[:, o[0]:o[1]], 256)
    arr["w_tok"] = blocks(np.concatenate([wi[:, o[5]:o[8]], wi[:, o[1]:o[4]]], 1), TOKW)
    arr["w_mixo"] = blocks(a["mix_w_out_l0"], 256)
    arr["w_up"] = np.concatenate([blocks(a["ffn_w1_l0"], P), blocks(a["ffn_w3_l0"], P)], 2)
    arr["w_down"] = blocks(a["ffn_w2_l0"], P)
    sw = a["ssd_w_in_l1"]
    arr["w_z"] = blocks(sw[:, :2048], 256)
    arr["w_xbc"] = blocks(sw[:, 2048:5120], 256)
    arr["w_dt"] = blocks(sw[:, 5120:], 64)
    arr["w_ssdo"] = blocks(a["ssd_w_out_l1"], P)
    up = [a["moe_w1_l1"].reshape(NE, KB, P, 4, FE // 4), a["moe_w3_l1"].reshape(NE, KB, P, 4, FE // 4)]
    moe = np.empty((NE, MOE_SLOTS, P, SLOT), np.float32)
    for n in range(2):
        moe[:, n:8:2] = up[n].transpose(0, 3, 2, 1, 4).reshape(NE, 4, P, SLOT)
    moe[:, 8:] = a["moe_w2_l1"].reshape(NE, FEB, P, 4, 256).transpose(0, 3, 2, 1, 4).reshape(NE, 4, P, SLOT)
    arr["w_moe"] = moe
    arr["dt_bias"], arr["a_log"] = a["ssd_dt_bias_l1"].T, a["ssd_a_log_l1"].T
    arr["d_skip"], arr["router_b"] = a["ssd_d_l1"], a["router_b_l1"]
    arr["router_w"] = a["router_w_l1"].reshape(KB, P, NE).transpose(1, 0, 2)
    arr["ssd0"] = a["state_ssd_l1"][0].reshape(2, NG, HPG * HD, NS).transpose(1, 3, 0, 2)
    arr["gate_b"] = a["mlstm_gate_b_l0"].reshape(32, 1)
    arr["cache_kT"] = a["cache_k_l0"][0].reshape(P, P).T
    arr["cache_v"] = a["cache_v_l0"][0].reshape(P, P)
    cn = np.concatenate([a["state_mlstm_c_l0"][0], a["state_mlstm_n_l0"][0][..., None]], -1)
    arr["c0n0"] = cn.reshape(2, 4, P, VA).transpose(2, 0, 1, 3)
    arr["m0"] = a["state_mlstm_m_l0"][0].T
    arr["qk_g"] = np.concatenate([np.tile(a["q_norm_g_l0"], 8), np.tile(a["k_norm_g_l0"], 2)])
    arr["mlstm_g"] = a["mlstm_norm_g_l0"]
    arr = {k: np.ascontiguousarray(v) for k, v in arr.items()}
    outs = {"yT": (P, KB, T), "new_k": (P, P), "new_v": (P, P), "new_m": (HA, 2, C), "new_cn": (P, 2, 4, VA),
            "new_ssd": (NG, P, 2, 4, NS)}
    nc = bacc.Bacc("TRN2", target_bir_lowering=False, num_devices=1)
    i = {k: nc.dram_tensor("in_" + k, v.shape, F32, kind="ExternalInput").ap() for k, v in arr.items()}
    od = {k: nc.dram_tensor("out_" + k, s, F32, kind="ExternalOutput").ap() for k, s in outs.items()}
    build(nc, i, od)
    r = run_bass_kernel_spmd(nc, [{"in_" + k: v for k, v in arr.items()}], core_ids=[0]).results[0]
    y = r["out_yT"].transpose(2, 1, 0).reshape(T, D)
    cn = r["out_new_cn"].transpose(1, 2, 0, 3).reshape(1, 2, HA, HD, VA)
    ssd = r["out_new_ssd"].transpose(2, 0, 3, 1, 4).reshape(1, 2, HC, HD, NS)
    return (y[None, :TP], y[None, TP:], r["out_new_k"].reshape(1, TP, KV, HD), r["out_new_v"].reshape(1, TP, KV, HD),
            np.ascontiguousarray(cn[..., :HD]), np.ascontiguousarray(cn[..., HD]),
            np.ascontiguousarray(r["out_new_m"][:, :, 0].T)[None], ssd)
```

```python
from contextlib import ExitStack

import numpy as np
import concourse.bass as bass
from concourse import mybir

F32 = mybir.dt.float32
BF16 = mybir.dt.bfloat16
F32R = mybir.dt.float32r
I32 = mybir.dt.int32
ALU = mybir.AluOpType
ACT = mybir.ActivationFunctionType
X = mybir.AxisListType.X

P = 128
D = 1024
KB = D // P
TP, TS = 128, 256
T = TP + TS
C = T // P
ALPHA = 4 ** 0.25
EPS = 1e-6
HD = 64
HA = 8
VA = HD + 1
H_ATT, KV = 8, 2
HC, NG, HPG, NS = 32, 4, 8, 128
FF, FE, NE = 2816, 1408, 8
FFB, FEB = FF // P, FE // P
XBCB = 24
SCALE = HD ** -0.5
GROUPS = ((0, 0, TP), (1, TP, T))

SLOT = 2816
RING = 4
MOE_TILES = 12
PAIRS = 3
TOKW = 288
TOKN = 2304
ITEMS = 13
OVER = ITEMS - NE

QA, KA, VAT, KM, VM, OM = 0, 512, 640, 768, 1280, 1792

CI = {}
_at = 0
for _n, _w in (("ident", 128), ("ropec", 128), ("ropes", 128),
               ("iota", 128), ("tri", 128), ("tie", 64), ("selp", 128), ("pm", 4), ("jrow", 16),
               ("erow", 16), ("irow", OVER)):
    CI[_n] = (_at, _at + _w)
    _at += _w
NCONST = _at

PV = {}
_at = 0
for _n, _w in (("adab0", 48), ("adab1", 48), ("ln", 64), ("convw", 72), ("convb", 24), ("ssdn", 16)):
    PV[_n] = (_at, _at + _w)
    _at += _w
NPV = _at

ADA, ADA_PE = 24, 4
ADA_DVE = ADA - ADA_PE

STAGES = (
    ("ada0a", ADA_PE, 2048, 1), ("gate", 1, 256, 1), ("qm", 2, 2048, 2), ("tok", 8, 8 * TOKW, 1),
    ("mixo", 4, 2048, 2), ("up", 22, 2048, 1), ("down", 8, 2816, 1),
    ("dt", 1, 512, 1), ("xbc", 12, 2048, 2), ("z", 8, 2048, 1),
    ("ssdo", 8, 2048, 1),
)
FIRST, _t = {}, 0
for _n, _k, _w, _s in STAGES:
    FIRST[_n] = _t
    _t += _k


def ds(start, size):
    return bass.ds(start, size)


def wide(ap, axis, n):
    u = ap.unsqueeze(axis)
    shape = list(u.shape)
    shape[axis] = n
    return u.broadcast_to(shape)


def build(nc, i, o):
    ctx = ExitStack()
    with ctx:
        def sb(name, shape, dt=F32):
            return ctx.enter_context(nc.sbuf_tensor(name, shape, dt))

        places_of = {}

        def placed(name, shape):
            places_of[name] = (nc.sbuf_base + 31) // 32 * 32
            return sb(name, shape)

        def rounded(name, at, n):
            return nc.alloc_sbuf_tensor_at(f"{name}_r{at}", [P, n], F32R, offset=places_of[name] + 4 * at)[:, :]

        def rounded_blocks(name):
            return rounded(name, 0, KB * T).rearrange("p (b t) -> p b t", b=KB)

        arena = placed("arena", [P, 12 * SLOT])
        spare = placed("spare", [P, 3900])
        cons = sb("cons", [P, NCONST])
        pvec = sb("pvec", [P, NPV])
        mods = sb("mods", [P, 192])
        xT = sb("xT", [P, KB, T])
        uT = placed("uT", [P, KB, T])
        zT = placed("zT", [P, KB, T])
        sqT = placed("sqT", [P, KB, T])
        uT_r, sqT_r = rounded_blocks("uT"), rounded_blocks("sqT")
        ring_r = rounded("arena", 0, RING * SLOT)
        onesm = sb("onesm", [P, P])
        onesf = sb("onesf", [P, P])
        maskb16 = sb("maskb16", [P, 2, P], BF16)
        identb16 = sb("identb16", [P, P], BF16)
        small = sb("small", [P, 640])
        ps = ctx.enter_context(nc.psum_tensor("ps", [P, 8, 512], F32))

        ident = cons[:, CI["ident"][0]:CI["ident"][1]]

        def con(name, rows=P):
            return cons[0:rows, CI[name][0]:CI[name][1]]

        def pv(name, j):
            return pvec[:, PV[name][0] + j:PV[name][0] + j + 1]

        def mod(layer, which, b, grp):
            c = layer * 96 + (which * KB + b) * 2 + grp
            return mods[:, c:c + 1]

        def slot(s):
            return arena[:, s * SLOT:(s + 1) * SLOT]

        def slot_r(s):
            return ring_r[:, s * SLOT:(s + 1) * SLOT]

        class Region:
            def __init__(self, ap, at=0):
                self.ap, self.at, self.end = ap, at, ap.shape[1]

            def take(self, n, rows=P):
                assert self.at + n <= self.end, (self.at, n, self.end)
                self.at += n
                return self.ap[0:rows, self.at - n:self.at]

        class Rounded:
            def __init__(self, name, at):
                self.name, self.at = name, at

            def take(self, n):
                self.at += n
                return rounded(self.name, self.at - n, n)

        wa = Region(arena[:, :], RING * SLOT)
        sa = Region(spare[:, :])
        tok0 = wa.take(C * TOKN).rearrange("p (c n) -> p c n", c=C)
        qmT = wa.take(4 * T).rearrange("p (j t) -> p j t", j=4)
        ada_at0 = wa.at
        qkr = wa.take(C * 640).rearrange("p (c n) -> p c n", c=C)
        vaug = wa.take(C * HA * VA).rearrange("p (c h v) -> p c h v", c=C, h=HA)
        kmT = wa.take(4 * T).rearrange("p (j t) -> p j t", j=4)
        qaT = wa.take(4 * T).rearrange("p (j t) -> p j t", j=4)
        kaT = wa.take(4 * P)
        vcache = wa.take(P)
        cst = wa.take(4 * 4 * VA).rearrange("p (w e j v) -> p w e j v", w=2, e=2, j=4)
        cnew = wa.take(2 * 4 * VA).rearrange("p (e j v) -> p e j v", e=2, j=4)
        ewt = wa.take(2 * T).rearrange("p (e t) -> p e t", e=2)
        pwt = wa.take(4 * T).rearrange("p (b e t) -> p b e t", b=2, e=2)
        rope1 = sa.take(C * 640).rearrange("p (c n) -> p c n", c=C)
        rope2 = sa.take(C * 640).rearrange("p (c n) -> p c n", c=C)
        sa.at = 0
        pexp = sa.take(2 * 896).rearrange("p (b n) -> p b n", b=2)
        pexpT = sa.take(2 * 896).rearrange("p (b n) -> p b n", b=2)
        sa.at = 0
        kw = sa.take(4 * 512).rearrange("p (u h d) -> p u h d", u=4, h=HA)
        sa.at = 0
        num = sa.take(HA * 6 * VA).rearrange("p (h u v) -> p h u v", h=HA, u=6)
        itmp = sa.take(4 * VA).rearrange("p (u v) -> p u v", u=4)
        qkg = wa.take(640)
        normg = wa.take(512)
        hsum = wa.take(C * HA * HD).rearrange("p (h c d) -> p h c d", h=HA, c=C)
        ga = Region(zT[:, :, :].rearrange("p a b -> p (a b)"))
        gates32 = ga.take(T, 32)
        gli = ga.take(2 * T, HA).rearrange("p (e t) -> p e t", e=2)
        glf = ga.take(2 * T, HA).rearrange("p (e t) -> p e t", e=2)
        gtmp = ga.take(2 * T, HA).rearrange("p (e t) -> p e t", e=2)
        gb = Region(sqT[:, :, :].rearrange("p a b -> p (a b)"))
        gb1 = gb.take(2 * T, HA).rearrange("p (e t) -> p e t", e=2)
        rows = gb.take(4 * 2 * T - 2 * T, HA)
        rows = rows.rearrange("p (q e t) -> p q e t", q=3, e=2)
        gmax = glf
        hcat = uT[:, :, :].rearrange("p a b -> p (a b)").rearrange("p (c n) -> p c n", c=C)
        hT0 = arena[:, RING * SLOT:RING * SLOT + KB * T].rearrange("p (b t) -> p b t", b=KB)
        sm = Region(small[:, :])
        cvec = sm.take(2 * KB).rearrange("p (k v) -> p k v", k=KB)
        cact = sm.take(2 * KB).rearrange("p (k v) -> p k v", k=KB)
        gbias = sm.take(1, 32)
        mrow = sm.take(2, HA)
        mprev = sm.take(6, HA).rearrange("p (e c) -> p e c", e=2)
        mlast = sm.take(6, HA).rearrange("p (e c) -> p e c", e=2)
        mnew = sm.take(6, HA).rearrange("p (e c) -> p e c", e=2)
        decay = sm.take(6, HA).rearrange("p (e c) -> p e c", e=2)
        dspread = sm.take(8, HA).rearrange("p (e j) -> p e j", e=2)
        dcol = sm.take(8).rearrange("p (e j) -> p e j", e=2)
        cols = sm.take(4 * 6 * HA).rearrange("p (q u h) -> p q u h", q=4, u=6)
        rstat = sm.take(30)
        rstat2 = sm.take(30)
        negmax = sm.take(6).rearrange("p (b u) -> p b u", b=2)
        rsum = sm.take(24).rearrange("p (h u) -> p h u", h=H_ATT)
        rrec = sm.take(24).rearrange("p (h u) -> p h u", h=H_ATT)
        den = sm.take(48)
        den2 = sm.take(48)
        hmean = sm.take(24).rearrange("p (h c) -> p h c", h=HA)
        hvar = sm.take(24).rearrange("p (h c) -> p h c", h=HA)
        epsc = sm.take(1)
        hsq = qkr.rearrange("p c n -> p (c n)")[:, 0:HA * C * HD].rearrange("p (h c d) -> p h c d", h=HA, c=C)
        knew_v = wa.take(P)
        stdr = sb("stdr", [P, T])
        masks = stdr[:, 0:2 * P].rearrange("p (e t) -> p e t", e=2)

        fr = Rounded("arena", RING * SLOT)
        ffhi, fflo = (fr.take(FFB * T).rearrange("p (f t) -> p f t", f=FFB) for _ in range(2))
        fwhi = [fr.take(SLOT) for _ in range(2)]
        fh = Region(zT[:, :, :].rearrange("p a b -> p (a b)"))
        silu2 = fh.take(2 * T).rearrange("p (b t) -> p b t", b=2)
        htmp = fh.take(2 * T).rearrange("p (b t) -> p b t", b=2)
        fh.at = 2 * D

        adaw = [[arena[:, ada_at0 + 2 * D * b:ada_at0 + 2 * D * (b + 1)] for b in range(2)],
                [spare[:, 2 * D:3 * D], fh.take(D)]]
        crow = [spare[:, 0:2 * D], spare[:, 0:2 * D]]
        junk = [spare[:, 2 * D:3 * D], ps[:, 4:6, :].rearrange("p a b -> p (a b)")]

        wb = Region(arena[:, :], RING * SLOT)
        bcT = wb.take(2 * NG * T).rearrange("p (n t) -> p n t", n=2 * NG)
        btok = wb.take(C * 512).rearrange("p (c n) -> p c n", c=C)
        xg_flat = wb.take(NG * C * 512)
        xg = xg_flat.rearrange("p (g c n) -> p g c n", g=NG, c=C)
        yT = xg_flat.rearrange("p (k t) -> p k t", t=T)
        zg = wb.take(2 * C * 512).rearrange("p (b c n) -> p b c n", b=2, c=C)
        xdt_at = wb.at
        xdt = wb.take(2 * C * 512).rearrange("p (e c n) -> p e c n", e=2, c=C)
        xdt_end, wb.at = wb.at, xdt_at
        PAD = T + 3
        raw = wb.take(2 * PAD).rearrange("p (b t) -> p b t", b=2)
        conv = wb.take(2 * PAD).rearrange("p (b t) -> p b t", b=2)
        xfeat = wb.take(2 * T).rearrange("p (b t) -> p b t", b=2)
        wb.at = xdt_end
        cb = wb.take(T)
        edec = wb.take(2 * T).rearrange("p (e t) -> p e t", e=2)
        wdec = wb.take(4 * T).rearrange("p (b e t) -> p b e t", b=2, e=2)
        sec = wb.take(2 * 512).rearrange("p (e n) -> p e n", e=2)
        yacc = wb.take(C * 512).rearrange("p (c n) -> p c n", c=C)
        sc_ = Region(spare[:, :])
        sini = sc_.take(2 * 512).rearrange("p (e n) -> p e n", e=2)
        snew = sc_.take(2 * 4 * P).rearrange("p (e j n) -> p e j n", e=2, j=4)
        dtc = sc_.take(6 * HC).rearrange("p (u h) -> p u h", u=6)
        cumc = sc_.take(6 * HC).rearrange("p (u h) -> p u h", u=6)
        ncumc = sc_.take(6 * HC).rearrange("p (u h) -> p u h", u=6)
        ecumc = sc_.take(6 * HC).rearrange("p (u h) -> p u h", u=6)
        wsc = sc_.take(6 * HC).rearrange("p (u h) -> p u h", u=6)
        dskip = sc_.take(HC)
        inter1 = sc_.take(512)
        elast = sm.take(2 * HC).rearrange("p (e h) -> p e h", e=2)
        dtb = sm.take(2, HC)
        acoef = sm.take(2, HC)
        gss = sm.take(C)
        gsd = sm.take(C)
        ra = Region(zT[:, :, :].rearrange("p a b -> p (a b)"))
        rx, rz, ru, rd = (ra.take(2 * T, HC).rearrange("p (e t) -> p e t", e=2) for _ in range(4))
        rb = Region(sqT[:, :, :].rearrange("p a b -> p (a b)"))
        rdt, rda, rcum = (rb.take(2 * T, HC).rearrange("p (e t) -> p e t", e=2) for _ in range(3))
        ra.at = 0
        xw = ra.take(4 * 512).rearrange("p (u n) -> p u n", u=4)
        ysq = ra.take(512)

        utok = sqT_r.rearrange("p a b -> p (a b)").rearrange("p (c n) -> p c n", c=C)
        rc = Region(zT[:, :, :].rearrange("p a b -> p (a b)"))
        rcr = Rounded("zT", 0)
        xe = rcr.take(D).rearrange("p (k s) -> p k s", k=KB)
        disp = rcr.take(C * P).rearrange("p (c s) -> p c s", c=C)
        rc.at = rcr.at
        ye = rc.take(D)
        comb = rc.take(T)
        gdisp = stdr[:, :].rearrange("p (c s) -> p c s", c=C)
        acc = uT
        rl = Rounded("arena", RING * SLOT)
        whi, wlo = [], []
        for _ in range(PAIRS):
            whi.append(rl.take(SLOT))
            wlo.append(rl.take(SLOT))
        xelo = rl.take(D).rearrange("p (k s) -> p k s", k=KB)
        heTlo = rl.take(FEB * P).rearrange("p (f s) -> p f s", f=FEB)
        utoklo = rl.take(C * D).rearrange("p (c n) -> p c n", c=C)
        re_ = Region(spare[:, :])
        he = re_.take(FE)
        sige = re_.take(2 * (FE // 4)).rearrange("p (b n) -> p b n", b=2)
        heT = Rounded("spare", re_.at).take(FEB * P).rearrange("p (f s) -> p f s", f=FEB)
        re_.at += FEB * P
        posi = re_.take(C * ITEMS).rearrange("p (c i) -> p c i", c=C)
        gatei = re_.take(C * ITEMS).rearrange("p (c i) -> p c i", c=C)
        listf = re_.take(16)
        routw = re_.take(KB * NE).rearrange("p (k e) -> p k e", k=KB)
        routb = re_.take(NE)
        rt = Region(spare[:, :])
        logit, sel, ppos, gate, rank, expl = (rt.take(C * NE).rearrange("p (c e) -> p c e", c=C) for _ in range(6))
        vmax, gsum = rt.take(C), rt.take(C)
        cnt = rt.take(NE)
        cmp1, cmp2 = (rt.take(C * NE * NE) for _ in range(2))
        have, order = rt.take(16), rt.take(16)
        hot = rt.take(OVER * 16)
        pp2, gg2 = (rt.take(C * 16) for _ in range(2))
        big = rt.take(C * OVER * 16)
        jover, eover = rt.take(OVER), rt.take(OVER)
        lists = sb("lists", [1, 16], I32)

        sems = {}

        def S(name):
            if name not in sems:
                sems[name] = ctx.enter_context(nc.semaphore(name))
            return sems[name]

        ready = [S(f"slot_ready{s}") for s in range(RING)]
        TILES = FIRST["ssdo"] + 8
        moe_base = [16 * sum(t % RING == s for t in range(TILES)) for s in range(RING)]

        def tile_done(t):
            for name, n, _, per in STAGES:
                if t < FIRST[name] + n:
                    k = t - FIRST[name]
                    if name == "ada0a":
                        return S("ada_mm"), k + 1
                    return S({"mixo": "y_mm", "down": "y_mm", "ssdo": "y_mm"}.get(name, name + "_mm")), \
                        {"mixo": 0, "down": KB, "ssdo": 2 * KB}.get(name, 0) + per * (k + 1)

        def tile_ready(t):
            return ready[t % RING], 16 * (t // RING + 1)

        class Serial:
            def __init__(self, eng, sem):
                self.eng, self.sem, self.n = eng, sem, 0

            def __call__(self, ins):
                self.n += 1
                ins.then_inc(self.sem, 1)
                self.eng.wait_ge(self.sem, self.n)

            def done(self, ins, sem, count):
                ins.then_inc(sem, 1)
                self.eng.wait_ge(sem, count)

            def ready(self, ins, sem, count):
                ins.then_inc(sem, 1)
                self.eng.wait_ge(sem, count)

        block = ctx.enter_context(nc.Block())

        @block.sync
        def _(sp):
            sp.dma_start(cons[:, :], i["consts"]).then_inc(S("consts_in"), 16)
            sp.dma_start(pvec[:, :], i["pvec"]).then_inc(S("consts_in"), 16)
            sp.dma_start(masks, i["masks"]).then_inc(S("consts_in"), 16)
            sp.dma_start(cvec, i["cvec"]).then_inc(S("consts_in"), 16)

            def load(name, width, t, k):
                g = FIRST[name] + t
                sp.dma_start(slot(g % RING)[:, 0:width], i["w_" + name][k]).then_inc(ready[g % RING], 16)

            def stream(name):
                _, n, width, per = [x for x in STAGES if x[0] == name][0]
                first = FIRST[name]
                head = min(n, RING)
                for t in range(head):
                    if first + t >= RING:
                        sp.wait_ge(*tile_done(first + t - RING))
                    load(name, width, t, t)
                loops = (n - head) // RING
                if loops:
                    with sp.Fori(0, loops) as it:
                        for j in range(RING):
                            sem, count = tile_done(first + j)
                            sp.wait_ge(sem, it * (RING * per) + count)
                            load(name, width, head + j, it * RING + head + j)
                for t in range(head + loops * RING, n):
                    sp.wait_ge(*tile_done(first + t - RING))
                    load(name, width, t, t)

            sp.dma_start(xT[:, :, :], i["xT"]).then_inc(S("x_in"), 16)
            for name, *_ in STAGES:
                stream(name)

            def load_expert(e, s):
                sp.dma_start(slot(s % RING), i["w_moe"][e, s] if isinstance(e, int) else
                             i["w_moe"][ds(e, 1), s].rearrange("a p n -> (a p) n")).then_inc(ready[s % RING], 16)

            for s in range(MOE_TILES):
                if s < RING:
                    sp.wait_ge(*tile_done(max(t for t in range(TILES) if t % RING == s)))
                else:
                    sp.wait_ge(S("split_lo"), s - RING + 1)
                load_expert(0, s)
            with sp.Fori(1, NE) as it:
                for s in range(MOE_TILES):
                    sp.wait_ge(S("split_lo"), it * MOE_TILES + (s - RING + 1))
                    load_expert(it, s)
            sp.wait_ge(S("routed"), 1)
            n_items = sp.value_load(lists[0:1, ITEMS:ITEMS + 1], min_val=NE, max_val=ITEMS)
            with sp.If(n_items > NE):
                with sp.Fori(NE, n_items) as it:
                    e = sp.value_load(lists[0:1, ds(it, 1)], min_val=0, max_val=NE - 1)
                    for s in range(MOE_TILES):
                        sp.wait_ge(S("split_lo"), it * MOE_TILES + (s - RING + 1))
                        load_expert(e, s)
            for half in range(2):
                b = slice(half * KB // 2, (half + 1) * KB // 2)
                sp.wait_ge(S("x_ready"), 3 * KB + (half + 1) * KB // 2)
                sp.dma_start(o["yT"][:, b], xT[:, b, :]).then_inc(S("stored"), 16)
            sp.wait_ge(S("stored"), 32)
            sp.wait_ge(S("ctx_stored"), 16 * 4)
            sp.wait_ge(S("ssd_stored"), 16 * NG)

        @block.gpsimd
        def _(gp):
            step = Serial(gp, S("pool_step"))

            def ada_tile(layer, n, b):
                src = i[f"w_adav{layer}"]
                gp.dma_start(adaw[layer][b], src[n] if isinstance(n, int) else
                             src[ds(n, 1)].rearrange("a p n -> (a p) n")).then_inc(S(f"ada_in{b}"), 16)

            def ada_tiles(layer, n):
                base = (0, ADA_DVE)[layer]
                with gp.Fori(0, n // 2 - 1) as it:
                    for b in range(2):
                        gp.wait_ge(S("ada_used"), it * 2 + (base + b + 1))
                        ada_tile(layer, it * 2 + (b + 2), b)

            gp.dma_start(crow[0], i["cond"].partition_broadcast(P)).then_inc(S("cond_in"), 16)
            for b in range(2):
                ada_tile(0, b, b)
            gp.dma_start(gbias, i["gate_b"]).then_inc(S("misc_in"), 16)
            gp.dma_start(kaT[:, P:2 * P], i["cache_kT"]).then_inc(S("misc_in"), 16)
            gp.dma_start(vcache, i["cache_v"]).then_inc(S("misc_in"), 16)
            gp.dma_start(cst[:, 0, :, :, :], i["c0n0"]).then_inc(S("misc_in"), 16)
            gp.dma_start(mrow, i["m0"]).then_inc(S("misc_in"), 16)
            gp.dma_start(qkg, i["qk_g"].partition_broadcast(P)).then_inc(S("misc_in"), 16)
            gp.dma_start(normg, i["mlstm_g"].partition_broadcast(P)).then_inc(S("misc_in"), 16)
            ada_tiles(0, ADA_DVE)

            def scale_x(n):
                gp.wait_ge(S("u_ready"), KB * (n + 1))
                step.done(nc.gpsimd.tensor_scalar_mul(xT[:, :, :], xT[:, :, :], ALPHA), S("ax_ready"), n + 1)

            scale_x(0)
            gp.wait_ge(S("qk_ready"), 1)
            gp.dma_start(o["new_k"], knew_v).then_inc(S("ctx_stored"), 16)
            gp.dma_start(o["new_v"], tok0[:, 0, VAT:VAT + P]).then_inc(S("ctx_stored"), 16)
            gp.wait_ge(S("exp_in"), 1)
            gp.dma_start(o["new_m"], mnew).then_inc(S("ctx_stored"), 16)
            gp.wait_ge(S("state_ready"), 1)
            gp.dma_start(o["new_cn"], cnew).then_inc(S("ctx_stored"), 16)
            gp.wait_ge(S("z_ready"), 1)
            gp.dma_start(crow[1], i["cond"].partition_broadcast(P)).then_inc(S("cond_in"), 16)
            gp.wait_ge(S("x_ready"), KB)
            for b in range(2):
                ada_tile(1, b, b)
            scale_x(1)
            ada_tiles(1, 2 * ADA)
            gp.dma_start(dtb, i["dt_bias"]).then_inc(S("misc1_in"), 16)
            gp.dma_start(acoef, i["a_log"]).then_inc(S("misc1_in"), 16)
            gp.wait_ge(S("z_ready"), 2 * KB)
            gp.dma_start(routw, i["router_w"]).then_inc(S("misc1_in"), 16)
            gp.dma_start(routb, i["router_b"].partition_broadcast(P)).then_inc(S("misc1_in"), 16)
            gp.dma_start(dskip, i["d_skip"].partition_broadcast(P)).then_inc(S("misc1_in"), 16)
            scale_x(2)
            step.done(nc.gpsimd.memset(raw, 0.0), S("raw_zero"), 1)
            for g in range(NG):
                def heads(ap):
                    return ap.rearrange("p (h d) -> p h d", d=HD)

                hs = slice(g * HPG, (g + 1) * HPG)
                gp.wait_ge(S("wexp_ready"), 1)
                if g:
                    gp.wait_ge(S("inter_mm"), 4 * g)
                    gp.wait_ge(S("inter_ready"), 4 * g)
                    gp.wait_ge(S("sec_ready"), 2 * g)
                    gp.wait_ge(S("ysum_mm"), HPG * g)
                gp.dma_start(sini, i["ssd0"][g]).then_inc(S("sini_in"), 16)
                for e in range(2):
                    for c in range(C):
                        k = nc.gpsimd.tensor_tensor(heads(xdt[:, e, c, :]), heads(xg[:, g, c, :]),
                                                    wide(dtc[:, 3 * e + c, hs], 2, HD), ALU.mult)
                        step(k)
                    step.done(nc.gpsimd.memset(listf[0:1, 14:15], 0.0), S("xdt_ready"), 2 * g + e + 1)
                for u, (c, e) in enumerate(((0, 0), (0, 1), (1, 0), (2, 1))):
                    step.done(nc.gpsimd.tensor_tensor(heads(xw[:, u, :]), heads(xdt[:, e, c, :]),
                                                      wide(wsc[:, 3 * e + c, hs], 2, HD), ALU.mult),
                              S("xw_ready"), 4 * g + u + 1)
                if g:
                    gp.wait_ge(S("yn_ready"), g)
                for c in range(C):
                    step.done(nc.gpsimd.tensor_tensor(heads(yacc[:, c, :]), heads(xg[:, g, c, :]),
                                                      wide(dskip[:, hs], 2, HD), ALU.mult),
                              S("yd_ready"), C * g + c + 1)
                gp.wait_ge(S("snew_half"), 2 * g + 2)
                gp.dma_start(o["new_ssd"][g], snew).then_inc(S("ssd_stored"), 16)
            scale_x(3)

        @block.scalar
        def _(act):
            step = Serial(act, S("act_step"))

            def layer_norm(ln):
                for q in range(4):
                    act.wait_ge(S("dev_ready"), 4 * ln + q + 1)
                    nc.scalar.activation(sqT[:, 2 * q:2 * q + 2, :], zT[:, 2 * q:2 * q + 2, :], ACT.Square) \
                        .then_inc(S("sq_ready"), 1)
                act.wait_ge(S("var_mm"), ln + 1)
                nc.scalar.activation(stdr[:, :], ps[:, 7, 0:T], ACT.Sqrt, bias=epsc).then_inc(S("std_ready"), 1)
                for b in range(KB):
                    act.wait_ge(S("norm_ready"), 4 * ln + b // 2 + 1)
                    nc.scalar.activation(xT[:, b, :], zT[:, b, :], ACT.Identity,
                                         bias=pv("ln", (2 * ln + 1) * KB + b),
                                         scale=pv("ln", 2 * ln * KB + b)).then_inc(S("x_ready"), 1)

            act.wait_ge(S("consts_in"), 64)
            nc.scalar.activation(cact, cvec, ACT.Silu).then_inc(S("cact_ready"), 1)
            act.wait_ge(S("cond_in"), 16)
            nc.scalar.activation(crow[0], crow[0], ACT.Silu).then_inc(S("cond_ready"), 1)
            act.wait_ge(S("gate_mm"), 1)
            act.wait_ge(S("misc_in"), 16 * 7)
            step.done(nc.scalar.activation(gates32, ps[0:32, 2, 0:T], ACT.Identity, bias=gbias),
                      S("gates_ready"), 1)
            for q in range(4):
                act.dma_start((gli, glf)[q % 2][:, q // 2, :], gates32[HA * q:HA * q + HA, :]) \
                    .then_inc(S("gates_moved"), 16)
            for j in range(4):
                act.wait_ge(S("qm_mm"), j + 1)
                step.done(nc.scalar.activation(qmT[:, j, :], ps[:, j % 2, 0:T], ACT.Copy, scale=SCALE),
                          S("qm_ready"), j + 1)
            act.wait_ge(S("gates_moved"), 64)
            step(nc.scalar.activation(gtmp, glf, ACT.Abs))
            step(nc.scalar.activation(gtmp, gtmp, ACT.Exp, scale=-1.0))
            step.done(nc.scalar.activation(gtmp, gtmp, ACT.Ln, bias=1.0), S("soft_log"), 1)
            act.sem_inc(S("tok_free"), 2)
            with act.Fori(0, 2) as it:
                for j in range(4):
                    act.wait_ge(S("tok_mm"), it * 4 + j + 1)
                    for c in range(C):
                        e = nc.scalar.activation(tok0[:, c, ds(it * (4 * TOKW) + j * TOKW, TOKW)],
                                                 ps[:, 3 * (j % 2) + c, 0:TOKW], ACT.Copy)
                    e.then_inc(S("tok_free"), 1)
            act.wait_ge(S("tok_free"), 10)
            act.wait_ge(S("ada_used"), ADA_DVE)
            step.done(nc.scalar.activation(rope1, tok0[:, :, 0:640], ACT.Square), S("qk_moments"), 1)
            act.wait_ge(S("qk_var"), 1)
            step.done(nc.scalar.activation(rstat2, rstat, ACT.Sqrt, bias=epsc, scale=1.0 / HD), S("qk_moments"), 2)
            act.wait_ge(S("exp_in"), 1)
            step(nc.scalar.activation(rows[:, 0:2, :, :], rows[:, 0:2, :, :], ACT.Exp, scale=-1.0))
            step(nc.scalar.activation(rows[:, 2, :, :], rows[:, 2, :, :], ACT.Exp))
            step.done(nc.scalar.activation(decay, decay, ACT.Exp), S("rows_ready"), 1)
            for c in range(C):
                act.wait_ge(S("tr_mm"), c + 1)
                nc.scalar.activation(kmT[:, :, c * P:(c + 1) * P],
                                     ps[:, 4 + c, :].rearrange("p (j t) -> p j t", j=4), ACT.Copy) \
                    .then_inc(S("kmT_ready"), 1)
            for h in range(H_ATT):
                act.wait_ge(S("max_ready"), h + 1)
                a = h % 2
                if h >= 2:
                    act.wait_ge(S("attT_mm"), h - 1)
                src = (ps[:, 2 * a, 384:512], ps[:, 2 * a, 0:384], ps[:, 2 * a + 1, 0:384])
                dst = (pexp[:, a, 0:128], pexp[:, a, 128:512], pexp[:, a, 512:896])
                for u in range(3):
                    nc.scalar.activation(dst[u], src[u], ACT.Exp, bias=negmax[:, a, u:u + 1], scale=SCALE,
                                         accum_out=rsum[:, h, u:u + 1]).then_inc(S("exp_ready"), 1)
                act.wait_ge(S("attT_mm"), h + 1)
                if h >= 2:
                    act.wait_ge(S("pv_mm"), h - 1)
                nc.scalar.activation(pexpT[:, a, 512:896], ps[:, 5, 0:384], ACT.Copy).then_inc(S("attT_act"), 1)
            act.wait_ge(S("att_ready"), 1)
            nc.scalar.activation(tok0[:, :, OM:OM + 512], tok0[:, :, OM:OM + 512], ACT.Sigmoid) \
                .then_inc(S("om_ready"), 1)
            for h in range(HA):
                for e in range(2):
                    act.wait_ge(S("bc_mm"), 2 * h + e + 1)
                    if h == 0:
                        act.wait_ge(S("cols_ready"), 1)
                        act.wait_ge(S("pv_mm"), H_ATT)
                    else:
                        act.wait_ge(S("pt_ready"), 2 * (h - 1) + e + 1)
                    for c in range(C):
                        k = nc.scalar.activation(ewt[:, e, c * P:(c + 1) * P], ps[:, 2 + e, c * P:(c + 1) * P],
                                                 ACT.Exp, bias=cols[:, 0, 3 * e + c, h:h + 1])
                    k.then_inc(S("e_ready"), 1)
            act.wait_ge(S("h_moments"), 1)
            nc.scalar.activation(hsq, hsum, ACT.Square).then_inc(S("h_moments_act"), 1)
            act.wait_ge(S("h_moments"), 2)
            nc.scalar.activation(hvar, hvar, ACT.Sqrt, bias=epsc, scale=1.0 / HD).then_inc(S("h_moments_act"), 1)
            def ffn_split(it, n):
                g = FIRST["up"] + n
                act.wait_ge(ready[g % RING], it * 16 + 16 * (g // RING + 1))
                width = 2048 if n < FFB and not (isinstance(it, int) and it * RING + n >= FFB) else SLOT
                nc.scalar.activation(fwhi[n % 2][:, 0:width], slot(g % RING)[:, 0:width], ACT.Copy) \
                    .then_inc(S("ffw_hi"), 1)

            for b in range(3, 6):
                act.wait_ge(S("hcatT_mm"), b + 1)
                nc.scalar.activation(hT0[:, 4:8, (b - 3) * P:(b - 2) * P],
                                     ps[:, b, :].rearrange("p (j t) -> p j t", j=4), ACT.Copy) \
                    .then_inc(S("hT_act"), 1)
            for n in range(2):
                ffn_split(0, n)
            layer_norm(0)
            act.wait_ge(S("cond_in"), 32)
            nc.scalar.activation(crow[1], crow[1], ACT.Silu).then_inc(S("cond_ready"), 1)
            for b in range(KB):
                act.wait_ge(S("u_ready"), KB + b + 1)
                nc.scalar.activation(sqT_r[:, b, :], uT[:, b, :], ACT.Copy).then_inc(S("u_hi"), 1)

            def hidden(it, j):
                t = it * RING + j
                b = j % 2
                act.wait_ge(S("up_mm"), t + 1)
                act.wait_ge(S("h_ready"), t + 1)
                nc.scalar.activation(silu2[:, b, :], ps[:, 2 * b, 0:T], ACT.Silu).then_inc(S("silu_ready"), 1)
                ffn_split(it, j + 2)
                act.wait_ge(S("h_ready"), t + 3)
                nc.scalar.activation(ffhi[:, ds(t, 1), :].rearrange("p a t -> p (a t)"), htmp[:, b, :], ACT.Copy) \
                    .then_inc(S("h_hi"), 1)

            with act.Fori(0, FFB // RING) as it:
                for j in range(RING):
                    hidden(it, j)
            for j in range(FFB % RING):
                hidden(FFB // RING, j)
            for d in range(2, KB):
                act.wait_ge(S("y_mm"), KB + d - 1)
                ffn_split(0, FFB + d)
            layer_norm(1)
            act.wait_ge(S("misc1_in"), 16 * 5)
            step(nc.scalar.activation(acoef, acoef, ACT.Exp))
            act.wait_ge(S("dt_mm"), 1)
            for e in range(2):
                step(nc.scalar.activation(rx[:, e, :], ps[0:HC, e, 0:T], ACT.Identity, bias=dtb[:, e:e + 1]))
            step(nc.scalar.activation(rz, rx, ACT.Abs))
            step.done(nc.scalar.activation(rz, rz, ACT.Exp, scale=-1.0), S("soft_log"), 2)
            act.wait_ge(S("dt_u"), 1)
            step.done(nc.scalar.activation(rdt, ru, ACT.Ln), S("soft_log"), 3)
            act.sem_inc(S("bc_free"), 2)

            def conv_in(n, j, first):
                act.wait_ge(S("xbc_mm"), n + 1)
                b = j % 2
                if not first:
                    act.wait_ge(S("conv_ready"), n - 1)
                nc.scalar.activation(raw[:, b, 1:1 + TP], ps[:, 2 + b, 0:TP], ACT.Copy)
                nc.scalar.activation(raw[:, b, 2 + TP:2 + T], ps[:, 2 + b, TP:T], ACT.Copy) \
                    .then_inc(S("bc_free"), 1)

            def conv_out(n, j, dst, sem):
                act.wait_ge(S("conv_ready"), n + 1)
                b = j % 2
                nc.scalar.activation(dst[:, 0:TP], conv[:, b, 0:TP], ACT.Silu)
                nc.scalar.activation(dst[:, TP:T], conv[:, b, TP + 1:T + 1], ACT.Silu).then_inc(sem, 1)

            act.wait_ge(S("raw_zero"), 1)
            for n in range(2):
                conv_in(n, n, True)
            with act.Fori(0, 2) as it:
                for j in range(8):
                    n = it * 8 + j
                    conv_out(n, j, xfeat[:, j % 2, :], S("xfeat_ready"))
                    conv_in(n + 2, j, False)
            for n in range(16, 24):
                conv_out(n, n, bcT[:, n - 16, :], S("bcT_ready"))
                if n + 2 < 24:
                    conv_in(n + 2, n, False)
            act.wait_ge(S("ccol_ready"), 2)
            step(nc.scalar.activation(ecumc, cumc, ACT.Exp))
            step.done(nc.scalar.activation(ncumc, cumc, ACT.Copy, scale=-1.0), S("cumc_ready"), 1)
            act.wait_ge(S("last_ready"), 1)
            step(nc.scalar.activation(elast, elast, ACT.Exp))
            step.done(nc.scalar.activation(wsc, wsc, ACT.Exp), S("wexp_ready"), 1)
            for g in range(NG):
                act.wait_ge(S("z_mm"), 2 * g + 2)
                if g >= 2:
                    act.wait_ge(S("yT_mm"), C * (g - 1))
                for c in range(C):
                    nc.scalar.activation(zg[:, g % 2, c, :], ps[:, 5 + c, :], ACT.Silu).then_inc(S("zg_ready"), 1)
                if g:
                    act.wait_ge(S("yg_ready"), g)
                    for c in range(C):
                        step(nc.scalar.activation(ysq, zg[:, (g - 1) % 2, c, :], ACT.Square,
                                                  accum_out=gss[:, c:c + 1]))
                    step.done(nc.scalar.activation(gsd, gss, ACT.Sqrt, bias=epsc, scale=1.0 / 512),
                              S("yg_std"), g)
                act.wait_ge(S("cb_mm"), g + 1)
                if g:
                    act.wait_ge(S("s_w_ready"), 2 * HPG * g)
                nc.scalar.activation(cb, ps[:, 3, 0:T], ACT.Copy).then_inc(S("cb_ready"), 1)
                for r in range(HPG):
                    h = g * HPG + r
                    for e in range(2):
                        act.wait_ge(S("s_bc_mm"), 2 * h + e + 1)
                        if h:
                            act.wait_ge(S("s_w_ready"), 2 * (h - 1) + e + 1)
                        for c in range(C):
                            k = nc.scalar.activation(edec[:, e, c * P:(c + 1) * P],
                                                     ps[:, 3 + e, c * P:(c + 1) * P], ACT.Exp,
                                                     bias=ncumc[:, 3 * e + c, h:h + 1])
                        k.then_inc(S("s_e_ready"), 1)
                    if r in (2, 4):
                        e = r // 2 - 1
                        act.wait_ge(S("out_mm"), 2 * g + e + 1)
                        if g and e == 0:
                            act.wait_ge(S("ssd_stored"), 16 * g)
                        k = nc.scalar.activation(snew[:, e, :, :],
                                                 ps[:, 5 + e, :].rearrange("p (j n) -> p j n", j=4), ACT.Copy)
                        step.done(k, S("snew_half"), 2 * g + e + 1)
            act.wait_ge(S("yg_ready"), NG)
            for c in range(C):
                step(nc.scalar.activation(ysq, zg[:, (NG - 1) % 2, c, :], ACT.Square, accum_out=gss[:, c:c + 1]))
            step.done(nc.scalar.activation(gsd, gss, ACT.Sqrt, bias=epsc, scale=1.0 / 512), S("yg_std"), NG)
            layer_norm(2)
            act.wait_ge(S("ssd_stored"), 16 * NG)
            act.wait_ge(S("sel_ready"), 2)
            step.done(nc.scalar.activation(expl, expl, ACT.Exp), S("expl_ready"), 1)
            for n in range(3):
                for half in range(2):
                    act.wait_ge(S("utok_mm"), 2 * n + half + 1)
                    nc.scalar.activation(utok[:, n, half * 512:(half + 1) * 512],
                                         ps[:, 2 + half + 2 * (n % 2), :], ACT.Copy).then_inc(S("utok_act"), 1)

            def split(it, s):
                act.wait_ge(ready[s % RING], it * (16 * MOE_TILES // RING) + (moe_base[s % RING] + 16 * (s // RING + 1)))
                if s >= PAIRS or not isinstance(it, int):
                    act.wait_ge(S("w_used"), it * MOE_TILES + (s - PAIRS + 1))
                nc.scalar.activation(whi[s % PAIRS], slot(s % RING), ACT.Copy) \
                    .then_inc(S("split_hi"), 1)

            for s in range(PAIRS):
                split(0, s)
            act.wait_ge(S("routed"), 1)
            n_last = act.value_load(lists[0:1, ITEMS + 1:ITEMS + 2], min_val=NE - 1, max_val=ITEMS - 1)

            def item(it, last):
                for n in range(2):
                    act.wait_ge(S("xe_mm"), it * 2 + (n + 1))
                    nc.scalar.activation(xe[:, 4 * n:4 * n + 4, :],
                                         ps[:, 4 + n, :].rearrange("p (k s) -> p k s", k=4), ACT.Copy) \
                        .then_inc(S("xe_hi"), 1)

                def silu(f):
                    act.wait_ge(S("w_used"), it * MOE_TILES + (2 * f + 1))
                    if f >= 2:
                        act.wait_ge(S("mh_ready"), it * 4 + (f - 1))
                    nc.scalar.activation(sige[:, f % 2, :], ps[:, 2 * (f % 2), 0:FE // 4], ACT.Silu) \
                        .then_inc(S("msilu_ready"), 1)

                def hidden_hi(n):
                    f0, f1 = 4 * n, min(4 * n + 4, FEB)
                    act.wait_ge(S("mhT_mm"), it * 3 + (n + 1))
                    nc.scalar.activation(heT[:, f0:f1, :],
                                         ps[:, 4 + n, 0:(f1 - f0) * P].rearrange("p (f s) -> p f s", s=P),
                                         ACT.Copy).then_inc(S("mhT_hi"), 1)

                def out(n):
                    act.wait_ge(S("w_used"), it * MOE_TILES + (8 + 2 * n + 2))
                    nc.scalar.activation(ye[:, n * 512:(n + 1) * 512], ps[:, (7, 4)[n], :], ACT.Copy) \
                        .then_inc(S("ye_ready"), 1)

                silu(0)
                split(it, 3)
                split(it, 4)
                silu(1)
                split(it, 5)
                split(it, 6)
                silu(2)
                split(it, 7)
                split(it, 8)
                hidden_hi(0)
                silu(3)
                split(it, 9)
                hidden_hi(1)
                hidden_hi(2)
                split(it, 10)
                split(it, 11)
                out(0)
                if not last:
                    split(it, MOE_TILES)
                    split(it, MOE_TILES + 1)
                out(1)
                if not last:
                    split(it, MOE_TILES + 2)

            with act.Fori(0, n_last) as it:
                item(it, False)
            item(n_last, True)
            layer_norm(3)

        @block.vector
        def _(v):
            step = Serial(v, S("dve_step"))
            V = nc.vector

            def ada_rows(layer, n, b, seen, used, blocks=2):
                v.wait_ge(S(f"ada_in{b}"), seen)
                for blk in range(blocks):
                    for grp in range(2):
                        c = n * (2 * blocks) + (layer * 96 + 2 * blk + grp)
                        k = V.scalar_tensor_tensor(junk[layer], adaw[layer][b][:, blk * D:(blk + 1) * D], 1.0,
                                                   crow[layer][:, grp * D:(grp + 1) * D], ALU.mult, ALU.mult,
                                                   accum_out=mods[:, ds(c, 1)])
                        if (blk, grp) != (blocks - 1, 1):
                            step(k)
                step.done(k, S("ada_used"), used)

            def ada_loop(n0, n1):
                at = step.n
                with v.Fori(0, (n1 - n0) // 2) as it:
                    for b in range(2):
                        step.n = it * 6 + (at + 3 * b)
                        ada_rows(0, it * 2 + (n0 + b + ADA_PE), b, it * 16 + 8 * (n0 + 2), it * 2 + (n0 + b + 1))
                step.n = at + 3 * (n1 - n0)

            def ada1_block(it, per, n):
                b = n % 2
                ada_rows(1, it * per + n, b, it * (8 * per) + 8 * ADA_DVE + 16 * (n // 2 + 1),
                         it * per + (ADA_DVE + n + 1), 1)

            def modulations(layer, b0, b1, count):
                for lo, hi, src in ((b0, 2 * ADA_PE, ps[:, 5, :]), (2 * ADA_PE, b1, mods)) \
                        if layer == 0 and b0 == 0 else ((b0, b1, mods),):
                    c0, c1 = layer * 96 + 2 * lo, layer * 96 + 2 * hi
                    bias = pvec[:, PV[f"adab{layer}"][0] + lo:PV[f"adab{layer}"][0] + hi]
                    step(V.tensor_tensor(mods[:, c0:c1].rearrange("p (b g) -> p b g", g=2),
                                         src[:, c0:c1].rearrange("p (b g) -> p b g", g=2),
                                         wide(bias, 2, 2), ALU.add))
                for s in (2 * KB, 8 * KB):
                    if 2 * b0 <= s < 2 * b1:
                        s += layer * 96
                        step(V.tensor_scalar_add(mods[:, s:s + 2 * KB], mods[:, s:s + 2 * KB], 1.0))
                step.done(V.memset(epsc, EPS), S("mods_ready"), count)

            def modulate(layer, half, n, after=None):
                for b in range(KB):
                    if n:
                        v.wait_ge(S("x_ready"), KB * n + b + 1 - (KB if n else 0))
                    for _, t0, t1 in GROUPS:
                        grp = 0 if t0 == 0 else 1
                        u = V.tensor_scalar(uT[:, b, t0:t1], xT[:, b, t0:t1], mod(layer, 3 * half + 1, b, grp),
                                            mod(layer, 3 * half, b, grp), ALU.mult, ALU.add)
                        if grp == 0:
                            step(u)
                    step.done(u, S("u_ready"), KB * n + b + 1)
                    if after:
                        after(b)

            def layer_norm(layer, half, ln, bank, after=None):
                v.wait_ge(S("ax_ready"), ln + 1)
                for b in range(KB):
                    v.wait_ge(S("y_mm"), KB * ln + b + 1)
                    for grp, t0, t1 in GROUPS:
                        z = V.scalar_tensor_tensor(zT[:, b, t0:t1], ps[:, bank(b), t0:t1],
                                                   mod(layer, 3 * half + 2, b, grp), xT[:, b, t0:t1],
                                                   ALU.mult, ALU.add)
                        if grp == 0:
                            step(z)
                    step.done(z, S("z_ready"), KB * ln + b + 1)
                    if after:
                        after(b)
                norm_steps(ln)

            def norm_steps(ln):
                v.wait_ge(S("mean_mm"), ln + 1)
                for q in range(4):
                    step.done(V.tensor_tensor(zT[:, 2 * q:2 * q + 2, :], zT[:, 2 * q:2 * q + 2, :],
                                              wide(ps[:, 6, 0:T], 1, 2), ALU.subtract),
                              S("dev_ready"), 4 * ln + q + 1)
                v.wait_ge(S("std_ready"), ln + 1)
                step(V.reciprocal(stdr[:, :], stdr[:, :]))
                for q in range(4):
                    step.done(V.tensor_tensor(zT[:, 2 * q:2 * q + 2, :], zT[:, 2 * q:2 * q + 2, :],
                                              wide(stdr[:, :], 1, 2), ALU.mult), S("norm_ready"), 4 * ln + q + 1)

            step(V.memset(onesf[:, :], 1.0))
            step(V.memset(epsc, EPS))
            step(V.memset(onesm[:, :], 1.0 / D))
            v.wait_ge(S("consts_in"), 64)
            step(V.tensor_copy(maskb16[:, :, :], masks))
            step.done(V.tensor_copy(identb16[:, :], ident), S("b16_ready"), 1)
            v.wait_ge(S("cond_ready"), 1)
            ada_loop(0, KB - ADA_PE)
            v.wait_ge(S("ada_mm"), ADA_PE)
            modulations(0, 0, 2 * KB, 1)
            v.wait_ge(S("x_in"), 16)
            modulate(0, 0, 0)
            ada_loop(KB - ADA_PE, KB)
            v.wait_ge(S("soft_log"), 1)
            step(V.scalar_tensor_tensor(glf, glf, 0.0, gtmp, ALU.min, ALU.subtract))

            def span(ap, e, c):
                if e == 0:
                    return ap[:, 0, c * P:(c + 1) * P]
                return ap[:, 1, (c + 1) * P - 1:(c * P - 1 if c else None):-1]

            for e in range(2):
                for c in range(C):
                    step(V.tensor_tensor_scan(span(gb1, e, c), onesf[0:HA, :], span(glf, e, c), 0.0,
                                              ALU.mult, ALU.add))
            step(V.tensor_tensor(gli, gli, gb1, ALU.subtract))

            def running_max(e, c, initial):
                step(V.tensor_tensor_scan(span(gmax, e, c), span(gli, e, c), span(gli, e, c), initial,
                                          ALU.max, ALU.max))
                last = c * P + (P - 1 if e == 0 else 0)
                step(V.tensor_copy(mlast[:, e, c:c + 1], gmax[:, e, last:last + 1]))
                step(V.tensor_tensor(mnew[:, e, c:c + 1], mlast[:, e, c:c + 1], gb1[:, e, last:last + 1], ALU.add))

            step(V.memset(mprev, 0.0))
            v.wait_ge(S("misc_in"), 16 * 7)
            for e in range(2):
                running_max(e, 0, 0.0)
                first, second = (1, 2) if e == 0 else (2, 1)
                step(V.tensor_copy(mprev[:, e, first:first + 1], mrow[:, e:e + 1]))
                running_max(e, first, mrow[:, e:e + 1])
                step(V.tensor_copy(mprev[:, e, second:second + 1], mnew[:, e, first:first + 1]))
                running_max(e, second, mnew[:, e, first:first + 1])
            step(V.tensor_scalar_mul(gtmp, gmax, -1.0))

            def chunks(ap):
                return ap.rearrange("p e (c t) -> p (e c) t", c=C)

            def per_chunk(ap):
                return wide(ap.rearrange("p e c -> p (e c)"), 2, P)

            step(V.tensor_tensor(chunks(rows[:, 0, :, :]), chunks(gmax), per_chunk(mprev), ALU.subtract))
            step(V.tensor_tensor(rows[:, 1, :, :], gmax, gb1, ALU.add))
            step(V.tensor_tensor(chunks(rows[:, 2, :, :]), chunks(gli), per_chunk(mlast), ALU.subtract))
            step.done(V.tensor_tensor(decay, mprev, mlast, ALU.subtract), S("exp_in"), 1)
            ada_loop(KB, ADA_DVE)
            modulations(0, 2 * KB, 6 * KB, 2)

            v.wait_ge(S("qk_moments"), 1)
            sq30 = rope1.rearrange("p c (h d) -> p (c h) d", d=HD)
            qk = tok0[:, :, 0:640]
            step.done(V.tensor_reduce(rstat, sq30, X, ALU.add), S("qk_var"), 1)
            v.wait_ge(S("qk_moments"), 2)
            step(V.reciprocal(rstat, rstat2))
            for c in range(C):
                qc = tok0[:, c, 0:640].rearrange("p (h d) -> p h d", d=HD)
                step(V.tensor_tensor(qc, qc, wide(rstat[:, 10 * c:10 * c + 10], 2, HD), ALU.mult))
            step(V.tensor_tensor(qk, qk, wide(qkg, 1, C), ALU.mult))
            step(V.tensor_copy(knew_v, tok0[:, 0, KA:KA + P]))

            def paired(ap):
                return ap.rearrange("p (j w d) -> p w j d", w=2, d=HD)

            def plain(ap):
                return ap.rearrange("p (w j d) -> p w j d", w=2, d=HD)

            step(V.tensor_copy(paired(qkr[:, 0, 0:512]), plain(tok0[:, 0, 0:512])))
            step(V.tensor_copy(qkr[:, 0, 512:640], tok0[:, 0, 512:640]))
            for c in (1, 2):
                cosr = con("ropec")[:, (c - 1) * HD:c * HD]
                sinr = con("ropes")[:, (c - 1) * HD:c * HD].rearrange("p (a b f) -> p a b f", a=2, b=2)
                step(V.tensor_tensor(rope1[:, c, :].rearrange("p (h d) -> p h d", d=HD),
                                     tok0[:, c, 0:640].rearrange("p (h d) -> p h d", d=HD),
                                     wide(cosr, 1, 10), ALU.mult))
                x4 = tok0[:, c, 0:640].rearrange("p (h a b f) -> p h a b f", a=2, b=2, f=16)
                y4 = rope2[:, c, :].rearrange("p (h a b f) -> p h a b f", a=2, b=2, f=16)
                for b in range(2):
                    step(V.tensor_tensor(y4[:, :, :, b, :], x4[:, :, :, 1 - b, :],
                                         wide(sinr[:, :, b, :], 1, 10), ALU.mult))
                step(V.tensor_tensor(paired(qkr[:, c, 0:512]), plain(rope1[:, c, 0:512]),
                                     plain(rope2[:, c, 0:512]), ALU.add))
                step(V.tensor_tensor(qkr[:, c, 512:640], rope1[:, c, 512:640], rope2[:, c, 512:640], ALU.add))
            step.done(V.memset(vaug[:, :, :, HD:VA], 1.0), S("qk_ready"), 1)
            step(V.tensor_copy(vaug[:, :, :, 0:HD].rearrange("p c h d -> p (c h) d"),
                                    tok0[:, :, VM:VM + 512].rearrange("p c (h d) -> p c h d", d=HD)
                                    .rearrange("p c h d -> p c h d")) if False else
                      V.tensor_copy(vaug[:, :, :, 0:HD], tok0[:, :, VM:VM + 512]
                                    .rearrange("p c (h d) -> p c h d", d=HD)))
            for c in range(C):
                v.wait_ge(S("qkT_mm"), c + 1)
                step(V.tensor_copy(qaT[:, :, c * P:(c + 1) * P], ps[:, c, :].rearrange("p (j t) -> p j t", j=4)))
            v.wait_ge(S("qkT_mm"), 4)
            step(V.tensor_copy(kaT[:, 0:P], ps[:, 3, 0:P]))
            step.done(V.tensor_copy(kaT[:, 2 * P:4 * P], ps[:, 3, 2 * P:4 * P]), S("qkT_ready"), 1)
            for h in range(H_ATT + 1):
                if h < H_ATT:
                    a = h % 2
                    v.wait_ge(S("att_mm"), h + 1)
                    if h >= 2:
                        v.wait_ge(S("exp_ready"), 3 * (h - 1))
                    src = (ps[:, 2 * a, 384:512], ps[:, 2 * a, 0:384], ps[:, 2 * a + 1, 0:384])
                    for u in range(3):
                        step(V.tensor_reduce(negmax[:, a, u:u + 1], src[u], X, ALU.max))
                    step.done(V.tensor_scalar_mul(negmax[:, a, :], negmax[:, a, :], -SCALE),
                              S("max_ready"), h + 1)
                    v.wait_ge(S("attT_mm"), h + 1)
                    if h >= 2:
                        v.wait_ge(S("pv_mm"), h - 1)
                    step.done(V.tensor_copy(pexpT[:, a, 0:512], ps[:, 4, :]), S("attT_dve"), h + 1)
                if h >= 1:
                    g = h - 1
                    v.wait_ge(S("pv_mm"), h)
                    step(V.reciprocal(rrec[:, g, :], rsum[:, g, :]))
                    step.done(V.tensor_tensor(hcat[:, :, 512 + g * HD:512 + (g + 1) * HD],
                                              ps[:, 6 + g % 2, 0:C * HD].rearrange("p (c d) -> p c d", c=C),
                                              wide(rrec[:, g, :], 2, HD), ALU.mult), S("att_ready"), h)
            v.wait_ge(S("cols_mm"), 1)
            step.done(V.tensor_copy(cols, ps[:, 7, 0:192].rearrange("p (q u h) -> p q u h", q=4, u=6)),
                      S("cols_ready"), 1)
            UNITS = ((0, 0), (0, 1), (1, 0), (2, 1))
            for u, (c, e) in enumerate(UNITS):
                step.done(V.tensor_tensor(kw[:, u, :, :],
                                          tok0[:, c, KM:KM + 512].rearrange("p (h d) -> p h d", d=HD),
                                          wide(cols[:, 3, 3 * e + c, :], 2, HD), ALU.mult), S("kw_ready"), u + 1)
            for e, c in ((0, 1), (1, 2)):
                step.done(V.tensor_scalar(dspread[:, e, :], con("pm", HA), decay[:, e, c:c + 1], None, ALU.mult),
                          S("dspread_ready"), e + 1)
            v.wait_ge(S("dcol_mm"), 1)
            step.done(V.tensor_copy(dcol, ps[:, 7, 192:200].rearrange("p (e j) -> p e j", e=2)), S("dspread_ready"), 3)
            for u, (c, e) in enumerate(UNITS):
                v.wait_ge(S("state_mm"), u + 1)
                if u >= 2:
                    step(V.tensor_tensor(cst[:, 1, e, :, :], cst[:, 0, e, :, :], wide(dcol[:, e, :], 2, VA),
                                         ALU.mult))
                for half in range(2):
                    part = ps[:, 2 * u + half, 0:4 * VA].rearrange("p (j w v) -> p j w v", j=2, w=2)
                    for w in range(2):
                        r = slice(HD * w, HD * w + HD)
                        j2 = slice(2 * half, 2 * half + 2)
                        if u < 2:
                            step(V.tensor_copy(cnew[r, e, j2, :], part[r, :, w, :]))
                        else:
                            step(V.tensor_tensor(cst[r, 1, e, j2, :], part[r, :, w, :], cst[r, 1, e, j2, :],
                                                 ALU.add))
                if u % 2 == 1:
                    step.done(V.memset(itmp[:, 0:1, 0:1], 0.0), S("state_ready"), u // 2 + 1)
            for h in range(HA + 1):
                if h < HA:
                    for e in range(2):
                        v.wait_ge(S("e_ready"), 2 * h + e + 1)
                        if e == 0:
                            v.wait_ge(S("sc_mm"), h + 1)
                            if h >= 2:
                                v.wait_ge(S("num_mm"), h - 1)
                        step.done(V.tensor_tensor(pwt[:, h % 2, e, :], ps[:, h % 2, 0:T], ewt[:, e, :], ALU.mult),
                                  S("pt_ready"), 2 * h + e + 1)
                if h >= 1:
                    g = h - 1
                    v.wait_ge(S("num_mm"), h)
                    inter = ps[:, 6 + g % 2, 0:4 * VA].rearrange("p (u v) -> p u v", u=4)
                    intra = ps[:, 4 + g % 2, 0:6 * VA].rearrange("p (u v) -> p u v", u=6)
                    for e in range(2):
                        step(V.tensor_tensor(itmp[:, 2 * e:2 * e + 2, :], inter[:, 2 * e:2 * e + 2, :],
                                             wide(cols[:, 1, 3 * e + 1:3 * e + 3, g], 2, VA), ALU.mult))
                        step(V.tensor_tensor(num[:, g, 3 * e + 1:3 * e + 3, :], intra[:, 3 * e + 1:3 * e + 3, :],
                                             itmp[:, 2 * e:2 * e + 2, :], ALU.add))
                        step.done(V.tensor_copy(num[:, g, 3 * e, :], intra[:, 3 * e, :]),
                                  S("num_ready"), 2 * g + e + 1)
            den3 = den.rearrange("p (h u) -> p h u", h=HA)
            step(V.tensor_copy(den3, num[:, :, :, HD]))
            step(V.scalar_tensor_tensor(den2, den, -1.0, den, ALU.mult, ALU.max))
            step(V.tensor_tensor(den2.rearrange("p (h u) -> p u h", h=HA), den2.rearrange("p (h u) -> p u h", h=HA),
                                 cols[:, 2, :, :], ALU.max))
            step(V.reciprocal(den, den2))
            numf = num.rearrange("p h u v -> p (h u) v")[:, :, 0:HD]
            step(V.tensor_tensor(numf, numf, wide(den, 2, HD), ALU.mult))
            for e in range(1):
                step(V.tensor_tensor(hsum, num[:, :, 0:3, 0:HD], num[:, :, 3:6, 0:HD], ALU.add))
            hf = hsum.rearrange("p h c d -> p (h c) d")
            hm = hmean.rearrange("p h c -> p (h c)")
            step(V.tensor_reduce(hm, hf, X, ALU.add))
            step(V.tensor_scalar_mul(hm, hm, 1.0 / HD))
            step.done(V.tensor_tensor(hf, hf, wide(hm, 2, HD), ALU.subtract), S("h_moments"), 1)
            v.wait_ge(S("h_moments_act"), 1)
            hv = hvar.rearrange("p h c -> p (h c)")
            step.done(V.tensor_reduce(hv, hsq.rearrange("p h c d -> p (h c) d"), X, ALU.add), S("h_moments"), 2)
            v.wait_ge(S("h_moments_act"), 2)
            step(V.reciprocal(hm, hv))
            step(V.tensor_tensor(hf, hf, wide(hm, 2, HD), ALU.mult))
            v.wait_ge(S("om_ready"), 1)
            step(V.tensor_tensor(tok0[:, :, OM:OM + 512], tok0[:, :, OM:OM + 512], wide(normg, 1, C), ALU.mult))
            for c in range(C):
                step.done(V.tensor_tensor(hcat[:, c, 0:512].rearrange("p (h d) -> p h d", d=HD), hsum[:, :, c, :],
                                          tok0[:, c, OM:OM + 512].rearrange("p (h d) -> p h d", d=HD), ALU.mult),
                          S("hcat_ready"), c + 1)
            for b in range(3):
                v.wait_ge(S("hcatT_mm"), b + 1)
                if b == 0:
                    v.wait_ge(S("ctx_stored"), 16 * 4)
                step.done(V.tensor_copy(hT0[:, 0:4, b * P:(b + 1) * P],
                                        ps[:, b, :].rearrange("p (j t) -> p j t", j=4)), S("hT_ready"), b + 1)

            def ffn_split(it, n):
                g = FIRST["up"] + n
                v.wait_ge(S("ffw_hi"), it * RING + (n + 1))
                width = 2048 if n < FFB and not (isinstance(it, int) and it * RING + n >= FFB) else SLOT
                V.tensor_tensor(slot_r(g % RING)[:, 0:width], slot(g % RING)[:, 0:width],
                                fwhi[n % 2][:, 0:width].bitcast(F32), ALU.subtract).then_inc(S("ffw_lo"), 1)

            layer_norm(0, 0, 0, lambda b: b % 4, lambda b: ffn_split(0, b - 4) if b in (4, 5) else None)

            def u_low(b):
                v.wait_ge(S("u_hi"), b + 1)
                V.tensor_tensor(uT_r[:, b, :], uT[:, b, :], sqT_r[:, b, :].bitcast(F32), ALU.subtract) \
                    .then_inc(S("u_lo"), 1)

            modulate(0, 1, 1, lambda b: u_low(b - 1) if b else None)
            u_low(KB - 1)
            v.sem_inc(S("h_ready"), 2)

            def hidden(it, j):
                t = it * RING + j
                b = j % 2
                v.wait_ge(S("silu_ready"), t + 1)
                V.tensor_tensor(htmp[:, b, :], ps[:, 2 * b + 1, 0:T], silu2[:, b, :], ALU.mult) \
                    .then_inc(S("h_ready"), 1)
                ffn_split(it, j + 2)
                v.wait_ge(S("h_hi"), t + 1)
                V.tensor_tensor(fflo[:, ds(t, 1), :].rearrange("p a t -> p (a t)"), htmp[:, b, :],
                                ffhi[:, ds(t, 1), :].rearrange("p a t -> p (a t)").bitcast(F32), ALU.subtract) \
                    .then_inc(S("h_lo"), 1)

            v.wait_ge(S("cond_ready"), 2)
            at = step.n
            with v.Fori(0, FFB // RING) as it:
                for j in range(RING):
                    hidden(it, j)
                    for n in ((0,), (1, 2), (3,), (4, 5))[j]:
                        step.n = it * 6 + (at + n)
                        ada1_block(it, 6, n)
            done = 6 * (FFB // RING)
            step.n = at + done
            for j in range(FFB % RING):
                hidden(FFB // RING, j)
                ada1_block(0, 6, done)
                done += 1

            def after(b):
                nonlocal done
                if b + 2 < KB:
                    ffn_split(0, FFB + b + 2)
                if b < 5:
                    for _ in range((3, 3, 3, 3, 4)[b]):
                        ada1_block(0, 6, done)
                        done += 1

            layer_norm(0, 1, 1, lambda b: b % 4, after)
            assert done == 2 * ADA
            modulations(1, 0, 6 * KB, 3)
            modulate(1, 0, 2)
            v.wait_ge(S("soft_log"), 2)
            step(V.tensor_scalar_mul(acoef, acoef, -1.0))
            step.done(V.tensor_scalar_add(ru, rz, 1.0), S("dt_u"), 1)
            step(V.tensor_scalar_add(rd, ru, -1.0))
            step(V.tensor_tensor(rd, rz, rd, ALU.subtract))
            v.wait_ge(S("soft_log"), 3)
            step(V.reciprocal(ru, ru))
            step(V.tensor_tensor(rd, rd, ru, ALU.mult))
            step(V.tensor_tensor(rdt, rdt, rd, ALU.add))
            step(V.scalar_tensor_tensor(rdt, rx, 0.0, rdt, ALU.max, ALU.add))
            for e in range(2):
                step(V.tensor_scalar(rda[:, e, :], rdt[:, e, :], acoef[:, e:e + 1], None, ALU.mult))
            for e in range(2):
                for c in range(C):
                    step(V.tensor_tensor_scan(span(rcum, e, c), onesf[0:HC, :], span(rda, e, c), 0.0,
                                              ALU.mult, ALU.add))
            step.done(V.memset(gsd[0:1, 0:1], 0.0), S("cum_ready"), 1)

            def convolve(n, j):
                b = j % 2
                v.wait_ge(S("bc_free"), n + 3)
                w0 = PV["convw"][0]
                full = slice(0, PAD - 2)

                def col(k):
                    return pvec[:, ds(n + k, 1)]

                step(V.tensor_scalar(conv[:, b, full], raw[:, b, 1:PAD - 1], col(w0 + XBCB), col(PV["convb"][0]),
                                     ALU.mult, ALU.add))
                step(V.scalar_tensor_tensor(conv[:, b, full], raw[:, b, 0:PAD - 2], col(w0), conv[:, b, full],
                                            ALU.mult, ALU.add))
                step.ready(V.scalar_tensor_tensor(conv[:, b, full], raw[:, b, 2:PAD], col(w0 + 2 * XBCB),
                                                  conv[:, b, full], ALU.mult, ALU.add), S("conv_ready"), n + 1)

            def xg_out(it, j):
                v.wait_ge(S("xT_mm"), it * 8 + (j + 1))
                g = it * 2 + j // 4
                for c in range(C):
                    k = V.tensor_copy(xg_flat[:, ds(g * (C * 512) + (c * 512 + (j % 4) * P), P)],
                                      ps[:, 4 + j % 2, c * P:(c + 1) * P])
                k.then_inc(S("xg_ready"), 1)

            convolve(0, 0)
            at = step.n
            per = 2 * 8
            with v.Fori(0, 2) as it:
                for j in range(8):
                    step.n = it * per + (at + 2 * j)
                    convolve(it * 8 + (j + 1), j + 1)
                    xg_out(it, j)
            step.n = at + 2 * per
            v.wait_ge(S("xg_ready"), 16)
            for n in range(17, 24):
                if n == 17:
                    v.wait_ge(S("xfeat_ready"), 16)
                else:
                    v.wait_ge(S("bcT_ready"), n - 17)
                convolve(n, n)
            for c in range(C):
                v.wait_ge(S("b_mm"), c + 1)
                step.done(V.tensor_copy(btok[:, c, :], ps[:, 4 + c, :]), S("b_ready"), c + 1)
            v.wait_ge(S("ccol_mm"), 1)
            cc = ps[:, 7, 0:384].rearrange("p (q u h) -> p q u h", q=2, u=6)
            step.done(V.tensor_copy(dtc, cc[:, 0, :, :]), S("ccol_ready"), 1)
            step.done(V.tensor_copy(cumc, cc[:, 1, :, :]), S("ccol_ready"), 2)
            v.wait_ge(S("last_mm"), 1)
            lastp = ps[:, 4, 0:6 * HC].rearrange("p (u h) -> p u h", u=6)
            step(V.tensor_tensor(wsc, lastp, cumc, ALU.subtract))
            step(V.tensor_copy(elast[:, 0, :], lastp[:, 1, :]))
            step.done(V.tensor_copy(elast[:, 1, :], lastp[:, 5, :]), S("last_ready"), 1)

            def heads(ap):
                return ap.rearrange("p (h d) -> p h d", d=HD)

            def close_group(g):
                for c in range(C):
                    v.wait_ge(S("zg_ready"), C * g + c + 1)
                    step(V.tensor_tensor(zg[:, g % 2, c, :], yacc[:, c, :], zg[:, g % 2, c, :], ALU.mult))
                step.done(V.memset(inter1[:, 0:1], 0.0), S("yg_ready"), g + 1)
                v.wait_ge(S("yg_std"), g + 1)
                step(V.reciprocal(gsd, gsd))
                for c in range(C):
                    k = V.tensor_scalar(zg[:, g % 2, c, :], zg[:, g % 2, c, :], gsd[:, c:c + 1], None, ALU.mult)
                    if c < C - 1:
                        step(k)
                    else:
                        step.done(k, S("yn_ready"), g + 1)

            def group_out(g):
                for c in range(C):
                    v.wait_ge(S("yT_mm"), C * g + c + 1)
                    norm = pvec[:, PV["ssdn"][0] + 4 * g:PV["ssdn"][0] + 4 * g + 4]
                    step.done(V.tensor_tensor(yT[:, 4 * g:4 * g + 4, c * P:(c + 1) * P],
                                              ps[:, 5 + c, :].rearrange("p (j t) -> p j t", j=4),
                                              wide(norm, 2, P), ALU.mult), S("yT_ready"), C * g + c + 1)

            for g in range(NG):
                if g:
                    close_group(g - 1)
                    group_out(g - 1)
                hs = slice(g * HPG, (g + 1) * HPG)
                v.wait_ge(S("sini_in"), 16 * (g + 1))
                for e in range(2):
                    step(V.tensor_tensor(heads(sec[:, e, :]), heads(sini[:, e, :]), wide(elast[:, e, hs], 2, HD),
                                         ALU.mult))
                    v.wait_ge(S("upd_mm"), 2 * g + e + 1)
                    step.done(V.tensor_tensor(sec[:, e, :], ps[:, 6 + e, :], sec[:, e, :], ALU.add),
                              S("sec_ready"), 2 * g + e + 1)
                v.wait_ge(S("cb_ready"), g + 1)
                for r in range(HPG):
                    h = g * HPG + r
                    for e in range(2):
                        v.wait_ge(S("s_e_ready"), 2 * h + e + 1)
                        if h >= 2:
                            v.wait_ge(S("ysum_mm"), h - 1)
                        step.done(V.tensor_tensor(wdec[:, r % 2, e, :], edec[:, e, :], cb, ALU.mult),
                                  S("s_w_ready"), 2 * h + e + 1)
                    if r == 0:
                        v.wait_ge(S("yd_ready"), C * (g + 1))
                    for n in {3: (0,), 6: (1,), 7: (2, 3)}.get(r, ()):
                        e, c = n // 2, 1 + n % 2
                        v.wait_ge(S("inter_mm"), 4 * g + n + 1)
                        step(V.tensor_tensor(heads(inter1), heads(ps[:, (7, 5, 6, 7)[n], :]),
                                             wide(ecumc[:, 3 * e + c, hs], 2, HD), ALU.mult))
                        step.done(V.tensor_tensor(yacc[:, c, :], yacc[:, c, :], inter1, ALU.add),
                                  S("inter_ready"), 4 * g + n + 1)
                v.wait_ge(S("ysum_mm"), HPG * (g + 1))
                for c in range(C):
                    step.done(V.tensor_tensor(yacc[:, c, :], ps[:, c, :], yacc[:, c, :], ALU.add),
                              S("ybank_ready"), C * g + c + 1)
            close_group(NG - 1)
            group_out(NG - 1)
            layer_norm(1, 0, 2, lambda b: b % 4)
            modulate(1, 1, 3)
            v.wait_ge(S("ssd_stored"), 16 * NG)
            v.wait_ge(S("route_mm"), 1)
            step(V.tensor_tensor(logit, ps[:, 0, 0:C * NE].rearrange("p (c e) -> p c e", c=C),
                                      wide(routb, 1, C), ALU.add))

            def table(ap, n):
                return ap.rearrange("p (c e f) -> p c e f", c=C, e=n)

            mine, other = wide(logit, 3, NE), wide(logit, 2, NE)
            step(V.tensor_tensor(table(cmp1, NE), other, mine, ALU.is_gt))
            step(V.tensor_tensor(table(cmp2, NE), other, mine, ALU.is_equal))
            step(V.tensor_tensor(cmp2.rearrange("p (c n) -> p c n", c=C), cmp2.rearrange("p (c n) -> p c n", c=C),
                                 wide(con("tie"), 1, C), ALU.mult))
            step(V.tensor_tensor(cmp1, cmp1, cmp2, ALU.add))
            step(V.tensor_reduce(rank, table(cmp1, NE), X, ALU.add))
            step.done(V.tensor_scalar(sel, rank, 2.0, None, ALU.is_lt), S("sel_ready"), 1)
            step(V.tensor_reduce(vmax, logit, X, ALU.max))
            step.done(V.tensor_tensor(expl, logit, wide(vmax, 2, NE), ALU.subtract), S("sel_ready"), 2)
            v.wait_ge(S("expl_ready"), 1)
            step(V.tensor_tensor(expl, expl, sel, ALU.mult))
            step(V.tensor_reduce(gsum, expl, X, ALU.add))
            step(V.reciprocal(gsum, gsum))
            step(V.tensor_tensor(gate, expl, wide(gsum, 2, NE), ALU.mult))
            v.wait_ge(S("route_mm"), 2)
            step(V.tensor_scalar_add(ppos, ps[:, 1, 0:C * NE].rearrange("p (c e) -> p c e", c=C), 1.0))
            step(V.tensor_tensor(ppos, ppos, sel, ALU.mult))
            step(V.tensor_scalar_add(ppos, ppos, -1.0))
            step(V.tensor_copy(cnt, ps[:, 1, C * NE:(C + 1) * NE]))
            step(V.tensor_copy(posi[:, :, 0:NE], ppos))
            step(V.tensor_copy(gatei[:, :, 0:NE], gate))
            for j in range(2):
                step(V.tensor_scalar(have[:, NE * j:NE * j + NE], cnt, float(P * (j + 1)), None, ALU.is_gt))
                step(V.tensor_copy(pp2.rearrange("p (c n) -> p c n", c=C)[:, :, NE * j:NE * j + NE], ppos))
                step(V.tensor_copy(gg2.rearrange("p (c n) -> p c n", c=C)[:, :, NE * j:NE * j + NE], gate))
            step(V.tensor_tensor_scan(order, onesf[:, 0:16], have, 0.0, ALU.mult, ALU.add))
            step(V.tensor_scalar_add(listf[:, ITEMS:ITEMS + 1], order[:, 15:16], float(NE)))
            step(V.tensor_scalar_add(listf[:, ITEMS + 1:ITEMS + 2], order[:, 15:16], float(NE - 1)))
            step(V.tensor_tensor(order, order, have, ALU.subtract))
            hot2 = hot.rearrange("p (i n) -> p i n", i=OVER)
            step(V.tensor_tensor(hot2, wide(order, 1, OVER), wide(con("irow"), 2, 16), ALU.is_equal))
            step(V.tensor_tensor(hot2, hot2, wide(have, 1, OVER), ALU.mult))
            big2 = big[:, 0:OVER * 16].rearrange("p (i n) -> p i n", i=OVER)
            step(V.tensor_tensor(big2, hot2, wide(con("jrow"), 1, OVER), ALU.mult))
            step(V.tensor_reduce(jover, big2, X, ALU.add))
            step(V.tensor_scalar_mul(jover, jover, float(P)))
            step(V.tensor_tensor(big2, hot2, wide(con("erow"), 1, OVER), ALU.mult))
            step(V.tensor_reduce(eover, big2, X, ALU.add))
            step(V.tensor_copy(listf[:, NE:ITEMS], eover))
            step(V.tensor_copy(listf[:, 0:NE], con("erow")[:, 0:NE]))
            step(V.memset(listf[:, ITEMS + 2:16], 0.0))
            for src, dst in ((pp2, posi), (gg2, gatei)):
                for c in range(C):
                    step(V.tensor_tensor(big2, hot2, wide(src[:, 16 * c:16 * c + 16], 1, OVER), ALU.mult))
                    step(V.tensor_reduce(dst[:, c, NE:ITEMS], big2, X, ALU.add))
            step(V.tensor_tensor(posi[:, :, NE:ITEMS], posi[:, :, NE:ITEMS], wide(jover, 1, C), ALU.subtract))
            step.done(V.tensor_copy(lists[:, :], listf[0:1, :]), S("routed"), 1)
            for n in range(3):
                for half in range(2):
                    part = slice(half * 512, (half + 1) * 512)
                    v.wait_ge(S("utok_act"), 2 * n + half + 1)
                    V.tensor_tensor(utoklo[:, n, part], ps[:, 2 + half + 2 * (n % 2), :],
                                    utok[:, n, part].bitcast(F32), ALU.subtract).then_inc(S("utok_dve"), 1)
            step(V.memset(acc[:, :, :], 0.0))
            n_last = v.value_load(lists[0:1, ITEMS + 1:ITEMS + 2], min_val=NE - 1, max_val=ITEMS - 1)

            def split(it, s):
                v.wait_ge(S("split_hi"), it * MOE_TILES + (s + 1))
                V.tensor_tensor(wlo[s % PAIRS], slot(s % RING), whi[s % PAIRS].bitcast(F32), ALU.subtract) \
                    .then_inc(S("split_lo"), 1)

            def places(it):
                for c in range(C):
                    V.tensor_scalar(disp[:, c, :], con("iota"), posi[:, c, ds(it, 1)], None,
                                    ALU.is_equal).then_inc(S("disp_ready"), 1)
                for c in range(C):
                    V.tensor_scalar(gdisp[:, c, :], con("iota"), posi[:, c, ds(it, 1)], gatei[:, c, ds(it, 1)],
                                    ALU.is_equal, ALU.mult).then_inc(S("disp_ready"), 1)

            def item(it, last):
                for n in range(2):
                    v.wait_ge(S("xe_hi"), it * 2 + (n + 1))
                    V.tensor_tensor(xelo[:, 4 * n:4 * n + 4, :],
                                    ps[:, 4 + n, :].rearrange("p (k s) -> p k s", k=4),
                                    xe[:, 4 * n:4 * n + 4, :].bitcast(F32),
                                    ALU.subtract).then_inc(S("xe_lo"), 1)

                def hidden(f):
                    v.wait_ge(S("msilu_ready"), it * 4 + (f + 1))
                    v.wait_ge(S("w_used"), it * MOE_TILES + (2 * f + 2))
                    V.tensor_tensor(he[:, f * (FE // 4):(f + 1) * (FE // 4)], ps[:, 2 * (f % 2) + 1, 0:FE // 4],
                                    sige[:, f % 2, :], ALU.mult).then_inc(S("mh_ready"), 1)

                def hidden_lo(n):
                    f0, f1 = 4 * n, min(4 * n + 4, FEB)
                    v.wait_ge(S("mhT_hi"), it * 3 + (n + 1))
                    V.tensor_tensor(heTlo[:, f0:f1, :],
                                    ps[:, 4 + n, 0:(f1 - f0) * P].rearrange("p (f s) -> p f s", s=P),
                                    heT[:, f0:f1, :].bitcast(F32), ALU.subtract).then_inc(S("mhT_lo"), 1)

                split(it, 3)
                hidden(0)
                split(it, 4)
                split(it, 5)
                hidden(1)
                split(it, 6)
                split(it, 7)
                hidden(2)
                split(it, 8)
                hidden_lo(0)
                split(it, 9)
                hidden(3)
                v.wait_ge(S("comb_mm"), it + 1)
                V.tensor_copy(comb, ps[:, 7, 0:T]).then_inc(S("comb_ready"), 1)
                hidden_lo(1)
                hidden_lo(2)
                split(it, 10)
                split(it, 11)
                if not last:
                    places(it + 1)
                    split(it, MOE_TILES)
                for b in range(KB):
                    v.wait_ge(S("madd_mm"), it * KB + (b + 1))
                    V.tensor_tensor(acc[:, b, :], ps[:, (5, 6, 0, 1)[b % 4], 0:T], acc[:, b, :], ALU.add) \
                        .then_inc(S("macc_ready"), 1)
                if not last:
                    split(it, MOE_TILES + 1)
                    split(it, MOE_TILES + 2)
                v.wait_ge(S("macc_ready"), it * KB + KB)

            places(0)
            for s in range(PAIRS):
                split(0, s)
            with v.Fori(0, n_last) as it:
                item(it, False)
            item(n_last, True)
            v.wait_ge(S("ax_ready"), 4)
            for b in range(KB):
                for grp, t0, t1 in GROUPS:
                    z = V.scalar_tensor_tensor(zT[:, b, t0:t1], acc[:, b, t0:t1], mod(1, 5, b, grp), xT[:, b, t0:t1],
                                               ALU.mult, ALU.add)
                    if grp == 0:
                        step(z)
                step.done(z, S("z_ready"), KB * 3 + b + 1)
            norm_steps(3)

        @block.tensor
        def _(pe):
            M = nc.tensor

            def ada(bank, name, t0, n, c0):
                first = FIRST[name] + t0
                with pe.Fori(0, n // RING) as it:
                    for j in range(RING):
                        g = first + j
                        pe.wait_ge(ready[g % RING], it * 16 + 16 * (g // RING + 1))
                        w = slot(g % RING)
                        for b in range(2):
                            for k in range(KB):
                                m = M.matmul(ps[:, bank, ds(it * 16 + (c0 + 4 * j + 2 * b), 2)],
                                             w[:, k * 256 + b * P:k * 256 + (b + 1) * P], cact[:, k, :],
                                             start=k == 0, stop=k == KB - 1)
                        m.then_inc(S("ada_mm"), 1)

            def layer_norm(ln, between=None):
                for b in range(KB):
                    pe.wait_ge(S("z_ready"), KB * ln + b + 1)
                    m = M.matmul(ps[:, 6, 0:T], onesm[:, :], zT[:, b, :], start=b == 0, stop=b == KB - 1)
                m.then_inc(S("mean_mm"), 1)
                if between:
                    between()
                for b in range(KB):
                    pe.wait_ge(S("sq_ready"), 4 * ln + b // 2 + 1)
                    m = M.matmul(ps[:, 7, 0:T], onesm[:, :], sqT[:, b, :], start=b == 0, stop=b == KB - 1)
                m.then_inc(S("var_mm"), 1)

            def out_blocks(name, ln, src, per, kb):
                for b in range(KB):
                    g = FIRST[name] + b // per
                    pe.wait_ge(*tile_ready(g))
                    if b >= 4:
                        pe.wait_ge(S("z_ready"), KB * ln + b - 3)
                    w = slot(g % RING)
                    for k in range(kb):
                        m = M.matmul(ps[:, b % 4, 0:T], w[:, k * per * P + (b % per) * P:k * per * P + (b % per + 1) * P],
                                     src(k), start=k == 0, stop=k == kb - 1)
                    m.then_inc(S("y_mm"), 1)

            pe.wait_ge(S("cact_ready"), 1)
            ada(5, "ada0a", 0, ADA_PE, 0)
            pe.wait_ge(*tile_ready(FIRST["gate"]))
            w = slot(FIRST["gate"] % RING)
            for k in range(KB):
                pe.wait_ge(S("u_ready"), k + 1)
                m = M.matmul(ps[0:32, 2, 0:T], w[:, k * 32:(k + 1) * 32], uT[:, k, :], start=k == 0, stop=k == KB - 1)
            m.then_inc(S("gate_mm"), 1)
            for j in range(4):
                g = FIRST["qm"] + j // 2
                pe.wait_ge(*tile_ready(g))
                if j >= 2:
                    pe.wait_ge(S("qm_ready"), j - 1)
                for k in range(KB):
                    c0 = k * 256 + (j % 2) * P
                    m = M.matmul(ps[:, j % 2, 0:T], slot(g % RING)[:, c0:c0 + P], uT[:, k, :],
                                 start=k == 0, stop=k == KB - 1)
                m.then_inc(S("qm_mm"), 1)
            with pe.Fori(0, 2) as it:
                for j in range(4):
                    g = FIRST["tok"] + j
                    pe.wait_ge(ready[g % RING], it * 16 + 16 * (g // RING + 1))
                    pe.wait_ge(S("tok_free"), it * 4 + j + 1)
                    for c in range(C):
                        for k in range(KB):
                            m = M.matmul(ps[:, 3 * (j % 2) + c, 0:TOKW], uT[:, k, c * P:(c + 1) * P],
                                         slot(g % RING)[:, k * TOKW:(k + 1) * TOKW],
                                         start=k == 0, stop=k == KB - 1)
                    m.then_inc(S("tok_mm"), 1)
            pe.wait_ge(S("tok_free"), 10)
            pe.wait_ge(S("mods_ready"), 2)
            for c in range(C):
                for j in range(4):
                    m = M.transpose(ps[:, 4 + c, j * P:(j + 1) * P], tok0[:, c, KM + j * P:KM + (j + 1) * P], ident)
                m.then_inc(S("tr_mm"), 1)
            pe.wait_ge(S("qk_ready"), 1)
            for c in range(C):
                for j in range(4):
                    m = M.transpose(ps[:, c, j * P:(j + 1) * P], qkr[:, c, j * P:(j + 1) * P], ident)
                m.then_inc(S("qkT_mm"), 1)
            for c, at in ((0, 0), (1, 2), (2, 3)):
                m = M.transpose(ps[:, 3, at * P:(at + 1) * P], qkr[:, c, 512:640], ident)
            m.then_inc(S("qkT_mm"), 1)
            pe.wait_ge(S("qkT_ready"), 1)
            pe.wait_ge(S("kmT_ready"), 3)
            pe.wait_ge(S("misc_in"), 16 * 7)

            def scores(h):
                a, j = h % 2, h % 4
                r = slice(HD * (h // 4), HD * (h // 4) + HD)
                if h >= 2:
                    pe.wait_ge(S("exp_ready"), 3 * (h - 1))
                M.matmul(ps[:, 2 * a, 384:512], qaT[r, j, 0:P], kaT[r, 0:P], start=True, stop=True)
                M.matmul(ps[:, 2 * a, 0:384], qaT[r, j, P:2 * P], kaT[r, P:4 * P], start=True, stop=True)
                M.matmul(ps[:, 2 * a + 1, 0:384], qaT[r, j, 2 * P:3 * P], kaT[r, P:4 * P],
                         start=True, stop=True).then_inc(S("att_mm"), 1)

            def turn(h):
                pe.wait_ge(S("exp_ready"), 3 * h + 3)
                if h >= 1:
                    pe.wait_ge(S("attT_dve"), h)
                    pe.wait_ge(S("attT_act"), h)
                for n in range(7):
                    m = M.transpose(ps[:, 4 + n // 4, (n % 4) * P:(n % 4 + 1) * P],
                                    pexp[:, h % 2, n * P:(n + 1) * P], ident)
                m.then_inc(S("attT_mm"), 1)

            def values(h):
                pe.wait_ge(S("attT_dve"), h + 1)
                pe.wait_ge(S("attT_act"), h + 1)
                if h >= 2:
                    pe.wait_ge(S("att_ready"), h - 1)
                kv = (h // 4) * HD
                out = ps[:, 6 + h % 2, 0:C * HD]
                keys = (vcache[:, kv:kv + HD], tok0[:, 1, VAT + kv:VAT + kv + HD], tok0[:, 2, VAT + kv:VAT + kv + HD])
                M.matmul(out[:, 0:HD], pexpT[:, h % 2, 0:P], tok0[:, 0, VAT + kv:VAT + kv + HD], start=True, stop=True)
                for q in range(2):
                    for n in range(3):
                        c0 = P + (3 * q + n) * P
                        m = M.matmul(out[:, (q + 1) * HD:(q + 2) * HD], pexpT[:, h % 2, c0:c0 + P], keys[n],
                                     start=n == 0, stop=n == 2)
                m.then_inc(S("pv_mm"), 1)

            scores(0)
            for h in range(H_ATT):
                if h + 1 < H_ATT:
                    scores(h + 1)
                turn(h)
                values(h)
            pe.wait_ge(S("rows_ready"), 1)
            pe.wait_ge(S("att_ready"), H_ATT)
            for q in range(4):
                for u in range(6):
                    src = gli if q == 0 else rows[:, q - 1, :, :]
                    m = M.transpose(ps[:, 7, (6 * q + u) * HA:(6 * q + u + 1) * HA],
                                    src[:, u // 3, (u % 3) * P:(u % 3 + 1) * P], ident[0:HA, 0:HA])
            m.then_inc(S("cols_mm"), 1)
            pe.wait_ge(S("dspread_ready"), 2)
            M.matmul(ps[:, 7, 192:200], con("selp", HA), dspread.rearrange("p e j -> p (e j)"),
                     start=True, stop=True).then_inc(S("dcol_mm"), 1)
            pe.wait_ge(S("dspread_ready"), 3)
            for u, c in enumerate((0, 0, 1, 2)):
                pe.wait_ge(S("kw_ready"), u + 1)
                for j in range(4):
                    m = M.matmul(ps[:, 2 * u + j // 2, (j % 2) * 2 * VA:(j % 2 + 1) * 2 * VA],
                                 kw[:, u, 2 * j:2 * j + 2, :].rearrange("p h d -> p (h d)"),
                                 vaug[:, c, 2 * j:2 * j + 2, :].rearrange("p h v -> p (h v)"), start=True, stop=True)
                m.then_inc(S("state_mm"), 1)
            pe.wait_ge(S("state_ready"), 2)
            pe.wait_ge(S("b16_ready"), 1)

            def pair(h):
                return slice(HD * (h % 2), HD * (h % 2) + HD)

            def mlstm_scores(h):
                r, j = pair(h), h // 2
                if h >= 2:
                    pe.wait_ge(S("pt_ready"), 2 * (h - 2) + 2)
                for c in range(C):
                    t = slice(c * P, (c + 1) * P)
                    m = M.matmul(ps[:, h % 2, t], kmT[r, j, t], qmT[r, j, t], start=True, stop=True)
                m.then_inc(S("sc_mm"), 1)
                for e in range(2):
                    if h >= 1:
                        pe.wait_ge(S("e_ready"), 2 * (h - 1) + e + 1)
                    M.matmul(ps[:, 2 + e, 0:T], ident[0:HA, h:h + 1].broadcast_to([HA, P]), gtmp[:, e, :],
                             start=True, stop=False)
                    M.matmul(ps[:, 2 + e, 0:T], identb16[:, :], wide(maskb16[:, e, :], 1, C),
                             start=False, stop=True).then_inc(S("bc_mm"), 1)

            def mlstm_values(h):
                r, j = pair(h), h // 2
                pe.wait_ge(S("pt_ready"), 2 * h + 2)
                if h >= 2:
                    pe.wait_ge(S("num_ready"), 2 * (h - 2) + 2)
                for e in range(2):
                    for c in range(C):
                        u = 3 * e + c
                        M.matmul(ps[:, 4 + h % 2, u * VA:(u + 1) * VA], pwt[:, h % 2, e, c * P:(c + 1) * P],
                                 vaug[:, c, h, :], start=True, stop=True)
                for e in range(2):
                    for c in (1, 2):
                        u = 2 * e + c - 1
                        which = (c - 1) if e == 0 else (2 - c)
                        m = M.matmul(ps[:, 6 + h % 2, u * VA:(u + 1) * VA], qmT[r, j, c * P:(c + 1) * P],
                                     cst[r, which, e, j, :], start=True, stop=True)
                m.then_inc(S("num_mm"), 1)

            mlstm_scores(0)
            for h in range(HA):
                if h + 1 < HA:
                    mlstm_scores(h + 1)
                mlstm_values(h)
            pe.wait_ge(S("num_ready"), 2 * HA)
            for c in range(C):
                for j in range(4):
                    m = None
                pass
            for b in range(6):
                half, c = b // 3, b % 3
                pe.wait_ge(S("hcat_ready"), c + 1 if half == 0 else 3)
                for j in range(4):
                    m = M.transpose(ps[:, b, j * P:(j + 1) * P],
                                    hcat[:, c, half * 512 + j * P:half * 512 + (j + 1) * P], ident)
                m.then_inc(S("hcatT_mm"), 1)
            pe.wait_ge(S("hT_ready"), 3)
            pe.wait_ge(S("hT_act"), 3)
            out_blocks("mixo", 0, lambda k: hT0[:, k, :], 2, KB)
            layer_norm(0)
            def three(out, ah, al, bh, bl, first, last):
                for n, (a, b) in enumerate(((ah, bh), (ah, bl), (al, bh))):
                    m = M.matmul(out, a, b, start=first and n == 0, stop=last and n == 2)
                return m

            def up_tile(it, j):
                t = it * RING + j
                g = FIRST["up"] + j
                hi, lo = fwhi[j % 2], slot_r(g % RING)
                pe.wait_ge(S("ffw_lo"), t + 1)
                pe.wait_ge(S("h_ready"), t + 1)
                for k, n in [(k, n) for k in range(KB) for n in range(2)]:
                        if j == 0:
                            pe.wait_ge(S("u_lo"), k + 1)
                        w = slice((n * KB + k) * P, (n * KB + k + 1) * P)
                        m = three(ps[:, 2 * (j % 2) + n, 0:T], hi[:, w], lo[:, w], sqT_r[:, k, :], uT_r[:, k, :],
                                  k == 0, k == KB - 1)
                m.then_inc(S("up_mm"), 1)

            with pe.Fori(0, FFB // RING) as it:
                for j in range(RING):
                    up_tile(it, j)
            for j in range(FFB % RING):
                up_tile(FFB // RING, j)
            pe.wait_ge(S("h_ready"), FFB + 2)
            for b in range(KB):
                g = FIRST["down"] + b
                hi, lo = fwhi[b % 2], slot_r(g % RING)
                pe.wait_ge(S("ffw_lo"), FFB + b + 1)
                if b >= 4:
                    pe.wait_ge(S("z_ready"), KB + b - 3)
                for k in range(FFB):
                    if b == 0:
                        pe.wait_ge(S("h_lo"), k + 1)
                    w = slice(k * P, (k + 1) * P)
                    m = three(ps[:, b % 4, 0:T], hi[:, w], lo[:, w], ffhi[:, k, :], fflo[:, k, :],
                              k == 0, k == FFB - 1)
                m.then_inc(S("y_mm"), 1)
            layer_norm(1)
            g = FIRST["dt"]
            pe.wait_ge(*tile_ready(g))
            for e in range(2):
                for k in range(KB):
                    pe.wait_ge(S("u_ready"), 2 * KB + k + 1)
                    m = M.matmul(ps[0:HC, e, 0:T], slot(g % RING)[:, k * 64 + e * HC:k * 64 + (e + 1) * HC],
                                 uT[:, k, :], start=k == 0, stop=k == KB - 1)
            m.then_inc(S("dt_mm"), 1)

            def xbc_block(g, j, n):
                pe.wait_ge(S("bc_free"), n + 1)
                for k in range(KB):
                    c0 = k * 256 + (j % 2) * P
                    m = M.matmul(ps[:, 2 + j % 2, 0:T], slot(g % RING)[:, c0:c0 + P], uT[:, k, :],
                                 start=k == 0, stop=k == KB - 1)
                m.then_inc(S("xbc_mm"), 1)

            def turn_x(it, j):
                pe.wait_ge(S("xfeat_ready"), it * 8 + (j + 1))
                for c in range(C):
                    m = M.transpose(ps[:, 4 + j % 2, c * P:(c + 1) * P], xfeat[:, j % 2, c * P:(c + 1) * P], ident)
                m.then_inc(S("xT_mm"), 1)

            pe.wait_ge(S("mods_ready"), 3)
            pe.wait_ge(*tile_ready(FIRST["xbc"]))
            for n in range(2):
                xbc_block(FIRST["xbc"], n, n)
            with pe.Fori(0, 2) as it:
                for j in range(8):
                    g = FIRST["xbc"] + (j + 2) // 2
                    if j % 2 == 0:
                        pe.wait_ge(ready[g % RING], it * 16 + 16 * (g // RING + 1))
                    xbc_block(g, j, it * 8 + (j + 2))
                    turn_x(it, j)
            for n in range(18, 24):
                g = FIRST["xbc"] + n // 2
                pe.wait_ge(*tile_ready(g))
                xbc_block(g, n, n)
            pe.wait_ge(S("cum_ready"), 1)
            for q, src in ((0, rdt), (1, rcum)):
                for u in range(6):
                    m = M.transpose(ps[:, 7, (6 * q + u) * HC:(6 * q + u + 1) * HC],
                                    src[:, u // 3, (u % 3) * P:(u % 3 + 1) * P], ident[0:HC, 0:HC])
            m.then_inc(S("ccol_mm"), 1)
            pe.wait_ge(S("xg_ready"), 16)
            for c in range(C):
                for g in range(NG):
                    pe.wait_ge(S("bcT_ready"), g + 1)
                    m = M.transpose(ps[:, 4 + c, g * P:(g + 1) * P], bcT[:, g, c * P:(c + 1) * P], ident)
                m.then_inc(S("b_mm"), 1)
            pe.wait_ge(S("ccol_ready"), 2)
            pe.wait_ge(S("b_ready"), 3)
            for e in range(2):
                t = (P - 1, 0)[e]
                m = M.matmul(ps[:, 4, e * 3 * HC:(e + 1) * 3 * HC], ident[:, t:t + 1].broadcast_to([P, P]),
                             cumc[:, 3 * e:3 * e + 3, :].rearrange("p u h -> p (u h)"), start=True, stop=True)
            m.then_inc(S("last_mm"), 1)

            def gate_cols(g):
                for n in range(2):
                    t = FIRST["z"] + 2 * g + n
                    pe.wait_ge(*tile_ready(t))
                    for c in range(C):
                        for k in range(KB):
                            m = M.matmul(ps[:, 5 + c, n * 256:(n + 1) * 256], uT[:, k, c * P:(c + 1) * P],
                                         slot(t % RING)[:, k * 256:(k + 1) * 256], start=k == 0, stop=k == KB - 1)
                    m.then_inc(S("z_mm"), 1)

            def decay_rows(h):
                for e in range(2):
                    if h:
                        pe.wait_ge(S("s_e_ready"), 2 * (h - 1) + e + 1)
                    M.matmul(ps[:, 3 + e, 0:T], ident[0:HC, h:h + 1].broadcast_to([HC, P]), rcum[:, e, :],
                             start=True, stop=False)
                    M.matmul(ps[:, 3 + e, 0:T], identb16[:, :], wide(maskb16[:, e, :], 1, C),
                             start=False, stop=True).then_inc(S("s_bc_mm"), 1)

            def head_sums(g, r):
                h = g * HPG + r
                pe.wait_ge(S("s_w_ready"), 2 * h + 2)
                if r == 0:
                    pe.wait_ge(S("xdt_ready"), 2 * g + 2)
                    if g:
                        pe.wait_ge(S("ybank_ready"), C * g)
                for c in range(C):
                    for e in range(2):
                        m = M.matmul(ps[:, c, r * HD:(r + 1) * HD], wdec[:, r % 2, e, c * P:(c + 1) * P],
                                     xdt[:, e, c, r * HD:(r + 1) * HD], start=e == 0, stop=e == 1)
                m.then_inc(S("ysum_mm"), 1)

            def turn_y(g):
                pe.wait_ge(S("yn_ready"), g + 1)
                for c in range(C):
                    for j in range(4):
                        m = M.transpose(ps[:, 5 + c, j * P:(j + 1) * P], zg[:, g % 2, c, j * P:(j + 1) * P], ident)
                    m.then_inc(S("yT_mm"), 1)

            def extra(g, r):
                if r == 0:
                    for e in range(2):
                        pe.wait_ge(S("xw_ready"), 4 * g + 3 + e)
                        M.matmul(ps[:, 6 + e, :], btok[:, 1 + e, g * P:(g + 1) * P], xw[:, 2 + e, :],
                                 start=True, stop=True).then_inc(S("upd_mm"), 1)
                elif r in (1, 3):
                    e = r // 2
                    if e:
                        pe.wait_ge(S("sec_ready"), 2 * g + 1)
                    for j in range(4):
                        m = M.matmul(ps[:, 5 + e, j * P:(j + 1) * P], xw[:, e, j * P:(j + 1) * P],
                                     btok[:, 0, g * P:(g + 1) * P], start=True, stop=True)
                    m.then_inc(S("out_mm"), 1)

            def inter(g, n):
                e, c = n // 2, 1 + n % 2
                if n == 0:
                    pe.wait_ge(S("sec_ready"), 2 * g + 2)
                elif n < 3:
                    pe.wait_ge(S("snew_half"), 2 * g + n)
                else:
                    pe.wait_ge(S("inter_ready"), 4 * g + 1)
                state = sini[:, e, :] if (c == 1) == (e == 0) else sec[:, e, :]
                M.matmul(ps[:, (7, 5, 6, 7)[n], :], bcT[:, NG + g, c * P:(c + 1) * P], state,
                         start=True, stop=True).then_inc(S("inter_mm"), 1)

            pe.wait_ge(S("cumc_ready"), 1)
            pe.wait_ge(S("wexp_ready"), 1)
            for g in range(NG):
                gate_cols(g)
                if g:
                    pe.wait_ge(S("zg_ready"), C * (g + 1))
                    turn_y(g - 1)
                if g:
                    pe.wait_ge(S("s_e_ready"), 2 * HPG * g)
                for c in range(C):
                    t = slice(c * P, (c + 1) * P)
                    pe.wait_ge(S("bcT_ready"), 8)
                    m = M.matmul(ps[:, 3, t], bcT[:, g, t], bcT[:, NG + g, t], start=True, stop=True)
                m.then_inc(S("cb_mm"), 1)
                pe.wait_ge(S("cb_ready"), g + 1)
                pe.wait_ge(S("zg_ready"), C * (g + 1))
                if g:
                    pe.wait_ge(S("yT_ready"), C * g)
                decay_rows(g * HPG)
                extra(g, 0)
                for r in range(HPG):
                    if r + 1 < HPG:
                        decay_rows(g * HPG + r + 1)
                    head_sums(g, r)
                    if r >= 1:
                        extra(g, r)
                    if r == 1:
                        inter(g, 0)
                    elif r in (4, 5, 6):
                        inter(g, r - 3)
                if g < NG - 1:
                    pe.wait_ge(S("inter_ready"), 4 * (g + 1))
            pe.wait_ge(S("inter_ready"), 4 * NG)
            turn_y(NG - 1)
            pe.wait_ge(S("yT_ready"), C * NG)
            out_blocks("ssdo", 2, lambda k: yT[:, k, :], 1, 16)
            layer_norm(2)
            for c in range(C):
                for k in range(KB):
                    pe.wait_ge(S("u_ready"), 3 * KB + k + 1)
                    m = M.matmul(ps[:, 0, c * NE:(c + 1) * NE], uT[:, k, c * P:(c + 1) * P], routw[:, k, :],
                                 start=k == 0, stop=k == KB - 1)
            m.then_inc(S("route_mm"), 1)
            for c in range(C):
                for half in range(2):
                    if c == 2:
                        pe.wait_ge(S("utok_dve"), half + 1)
                    for j in range(4):
                        k = 4 * half + j
                        m = M.transpose(ps[:, 2 + 2 * (c % 2) + half, j * P:(j + 1) * P],
                                        uT[:, k, c * P:(c + 1) * P], ident)
                    m.then_inc(S("utok_mm"), 1)
                if c == 1:
                    pe.wait_ge(S("sel_ready"), 1)
                    for c1 in range(C):
                        for c0 in range(c1 + 1):
                            M.matmul(ps[:, 1, c1 * NE:(c1 + 1) * NE], con("tri") if c0 == c1 else onesf[:, :],
                                     sel[:, c0, :], start=c0 == 0, stop=c0 == c1)
                    for c0 in range(C):
                        m = M.matmul(ps[:, 1, C * NE:(C + 1) * NE], onesf[:, :], sel[:, c0, :],
                                     start=c0 == 0, stop=c0 == C - 1)
                    m.then_inc(S("route_mm"), 1)
            pe.wait_ge(S("routed"), 1)
            pe.wait_ge(S("utok_dve"), 6)
            n_last = pe.value_load(lists[0:1, ITEMS + 1:ITEMS + 2], min_val=NE - 1, max_val=ITEMS - 1)

            def item(it, last):
                pe.wait_ge(S("disp_ready"), it * (2 * C) + C)
                for b in range(KB):
                    for c in range(C):
                        for n, u in enumerate((utok, utoklo)):
                            m = M.matmul(ps[:, 4 + b // 4, (b % 4) * P:(b % 4 + 1) * P],
                                         u[:, c, b * P:(b + 1) * P], disp[:, c, :],
                                         start=c == 0 and n == 0, stop=c == C - 1 and n == 1)
                    if b % 4 == 3:
                        m.then_inc(S("xe_mm"), 1)

                def three(out, xh, xl, wh, wl, first, last):
                    for n, (a, b) in enumerate(((xh, wh), (xh, wl), (xl, wh))):
                        m = M.matmul(out, a, b, start=first and n == 0,
                                     stop=last and n == 2)
                    return m

                def up(s):
                    f, n = s // 2, s % 2
                    pe.wait_ge(S("split_lo"), it * MOE_TILES + (s + 1))
                    if f >= 2:
                        pe.wait_ge(S("mh_ready"), it * 4 + (f - 1))
                    W = FE // 4
                    for k in range(KB):
                        if s == 0 and k % 4 == 0:
                            pe.wait_ge(S("xe_lo"), it * 2 + (k // 4 + 1))
                        w = slice(k * W, (k + 1) * W)
                        m = three(ps[:, 2 * (f % 2) + n, 0:W], xe[:, k, :], xelo[:, k, :], whi[s % PAIRS][:, w],
                                  wlo[s % PAIRS][:, w], k == 0, k == KB - 1)
                    m.then_inc(S("w_used"), 1)

                def turn_h(n, need):
                    pe.wait_ge(S("mh_ready"), it * 4 + need)
                    for f in range(4 * n, min(4 * n + 4, FEB)):
                        m = M.transpose(ps[:, 4 + n, (f % 4) * P:(f % 4 + 1) * P], he[:, f * P:(f + 1) * P], ident)
                    m.then_inc(S("mhT_mm"), 1)

                for s in range(6):
                    up(s)
                turn_h(0, 2)
                up(6)
                up(7)
                turn_h(1, 3)
                pe.wait_ge(S("disp_ready"), it * (2 * C) + 2 * C)
                for c in range(C):
                    m = M.transpose(ps[:, 7, c * P:(c + 1) * P], gdisp[:, c, :], ident)
                m.then_inc(S("comb_mm"), 1)
                turn_h(2, 4)
                pe.wait_ge(S("comb_ready"), it + 1)
                for n in range(4):
                    s = 8 + n
                    pe.wait_ge(S("split_lo"), it * MOE_TILES + (s + 1))
                    for f in range(FEB):
                        if n == 0 and f % 4 == 0:
                            pe.wait_ge(S("mhT_lo"), it * 3 + (f // 4 + 1))
                        w = slice(f * 256, (f + 1) * 256)
                        m = three(ps[:, (7, 4)[n // 2], (n % 2) * 256:(n % 2 + 1) * 256], heT[:, f, :],
                                  heTlo[:, f, :], whi[s % PAIRS][:, w], wlo[s % PAIRS][:, w], f == 0, f == FEB - 1)
                    m.then_inc(S("w_used"), 1)
                for b in range(KB):
                    pe.wait_ge(S("ye_ready"), it * 2 + (1 + b // 4))
                    if b >= 4:
                        pe.wait_ge(S("macc_ready"), it * KB + (b - 3))
                    M.matmul(ps[:, (5, 6, 0, 1)[b % 4], 0:T], ye[:, b * P:(b + 1) * P], comb,
                             start=True, stop=True).then_inc(S("madd_mm"), 1)
                pe.wait_ge(S("macc_ready"), it * KB + KB)

            with pe.Fori(0, n_last) as it:
                item(it, False)
            item(n_last, True)
            layer_norm(3)


def blocks(w, n):
    w = np.asarray(w)
    k, m = w.shape
    return np.ascontiguousarray(w.reshape(k // P, P, m // n, n).transpose(2, 1, 0, 3)).reshape(m // n, P, -1)


def columns(v):
    return np.asarray(v).reshape(-1, P).T


def constants():
    c = np.zeros((P, NCONST), np.float32)

    def put(name, a):
        c[0:a.shape[0], CI[name][0]:CI[name][0] + a.shape[1]] = a

    put("ident", np.eye(P, dtype=np.float32))
    nf = HD // 4
    inv = (10000.0 ** (-np.arange(nf, dtype=np.float32) / nf)).astype(np.float32)
    t = np.arange(TS)
    row, col = (t // 64).astype(np.float32), (t % 64).astype(np.float32)
    cr, sr = np.cos(row[:, None] * inv), np.sin(row[:, None] * inv)
    cc, sc = np.cos(col[:, None] * inv), np.sin(col[:, None] * inv)
    cos = np.concatenate([cr, cr, cc, cc], 1)
    sin = np.concatenate([-sr, sr, -sc, sc], 1)
    put("ropec", np.concatenate([cos[:P], cos[P:]], 1))
    put("ropes", np.concatenate([sin[:P], sin[P:]], 1))
    put("iota", np.broadcast_to(np.arange(P, dtype=np.float32), (P, P)))
    a = np.arange(P)
    put("tri", (a[:, None] < a[None, :]).astype(np.float32))
    e = np.arange(NE)
    put("tie", np.broadcast_to((e[None, :] < e[:, None]).astype(np.float32).reshape(1, -1), (P, 64)))
    put("selp", ((np.arange(HA) % 2)[:, None] == (a // HD)[None, :]).astype(np.float32))
    put("pm", ((np.arange(HA) // 2)[:, None] == np.arange(4)[None, :]).astype(np.float32))
    put("jrow", np.broadcast_to(np.repeat(np.float32([1, 2]), NE), (P, 16)))
    put("erow", np.broadcast_to(np.tile(np.arange(NE, dtype=np.float32), 2), (P, 16)))
    put("irow", np.broadcast_to(np.arange(OVER, dtype=np.float32), (P, OVER)))
    return c


def kernel(**inputs):
    from concourse import bacc
    from concourse.bass_utils import run_bass_kernel_spmd

    a = {k: np.asarray(v) for k, v in inputs.items()}
    x = np.concatenate([a["x_prompt"][0], a["x_sample"][0]], 0)
    t = np.arange(P)
    arr = {
        "consts": constants(),
        "masks": np.ascontiguousarray(np.stack([np.where(t[None, :] >= t[:, None], 0, -1e30),
                                                np.where(t[None, :] <= t[:, None], 0, -1e30)], 1), np.float32),
        "pvec": np.concatenate([columns(a["ada_b_l0"]), columns(a["ada_b_l1"])]
                               + [columns(a[f"ln{n}_{p}_l{l}"]) for l in (0, 1) for n in (1, 2) for p in "gb"]
                               + [columns(a["ssd_conv_w_l1"]), columns(a["ssd_conv_b_l1"]),
                                  columns(a["ssd_norm_g_l1"])], 1),
        "cvec": np.ascontiguousarray(np.stack([a["c_ctx"], a["c"][0]], 1).reshape(KB, P, 2).transpose(1, 0, 2)),
        "xT": np.ascontiguousarray(x.T.reshape(KB, P, T).transpose(1, 0, 2)),
    }
    wi = a["mix_w_in_l0"]
    arr["w_ada0a"] = blocks(a["ada_w_l0"][:, :256 * ADA_PE], 256)
    arr["w_adav0"] = (a["ada_w_l0"].T.reshape(ADA, 2, P, D).transpose(0, 2, 1, 3)
                      .reshape(ADA, P, 2 * D)[ADA_PE:])
    arr["w_adav1"] = a["ada_w_l1"].T.reshape(2 * ADA, P, D)
    arr["cond"] = np.concatenate([a["c_ctx"], a["c"][0]])
    o = np.cumsum([0, 512, 512, 512, 512, 32, 512, 128, 128])
    arr["w_gate"] = blocks(wi[:, o[4]:o[5]], 32)
    arr["w_qm"] = blocks(wi[:, o[0]:o[1]], 256)
    arr["w_tok"] = blocks(np.concatenate([wi[:, o[5]:o[8]], wi[:, o[1]:o[4]]], 1), TOKW)
    arr["w_mixo"] = blocks(a["mix_w_out_l0"], 256)
    arr["w_up"] = np.concatenate([blocks(a["ffn_w1_l0"], P), blocks(a["ffn_w3_l0"], P)], 2)
    arr["w_down"] = blocks(a["ffn_w2_l0"], P)
    sw = a["ssd_w_in_l1"]
    arr["w_z"] = blocks(sw[:, :2048], 256)
    arr["w_xbc"] = blocks(sw[:, 2048:5120], 256)
    arr["w_dt"] = blocks(sw[:, 5120:], 64)
    arr["w_ssdo"] = blocks(a["ssd_w_out_l1"], P)
    up = [a["moe_w1_l1"].reshape(NE, KB, P, 4, FE // 4), a["moe_w3_l1"].reshape(NE, KB, P, 4, FE // 4)]
    moe = np.empty((NE, MOE_TILES, P, SLOT), np.float32)
    for n in range(2):
        moe[:, n:8:2] = up[n].transpose(0, 3, 2, 1, 4).reshape(NE, 4, P, SLOT)
    moe[:, 8:] = a["moe_w2_l1"].reshape(NE, FEB, P, 4, 256).transpose(0, 3, 2, 1, 4).reshape(NE, 4, P, SLOT)
    arr["w_moe"] = moe
    arr["dt_bias"], arr["a_log"] = a["ssd_dt_bias_l1"].T, a["ssd_a_log_l1"].T
    arr["d_skip"], arr["router_b"] = a["ssd_d_l1"], a["router_b_l1"]
    arr["router_w"] = a["router_w_l1"].reshape(KB, P, NE).transpose(1, 0, 2)
    arr["ssd0"] = a["state_ssd_l1"][0].reshape(2, NG, HPG * HD, NS).transpose(1, 3, 0, 2)
    arr["gate_b"] = a["mlstm_gate_b_l0"].reshape(32, 1)
    arr["cache_kT"] = a["cache_k_l0"][0].reshape(P, P).T
    arr["cache_v"] = a["cache_v_l0"][0].reshape(P, P)
    cn = np.concatenate([a["state_mlstm_c_l0"][0], a["state_mlstm_n_l0"][0][..., None]], -1)
    arr["c0n0"] = cn.reshape(2, 4, P, VA).transpose(2, 0, 1, 3)
    arr["m0"] = a["state_mlstm_m_l0"][0].T
    arr["qk_g"] = np.concatenate([np.tile(a["q_norm_g_l0"], 8), np.tile(a["k_norm_g_l0"], 2)])
    arr["mlstm_g"] = a["mlstm_norm_g_l0"]
    arr = {k: np.ascontiguousarray(v) for k, v in arr.items()}
    outs = {"yT": (P, KB, T), "new_k": (P, P), "new_v": (P, P), "new_m": (HA, 2, C), "new_cn": (P, 2, 4, VA),
            "new_ssd": (NG, P, 2, 4, NS)}
    nc = bacc.Bacc("TRN2", target_bir_lowering=False, num_devices=1)
    i = {k: nc.dram_tensor("in_" + k, v.shape, F32, kind="ExternalInput").ap() for k, v in arr.items()}
    od = {k: nc.dram_tensor("out_" + k, s, F32, kind="ExternalOutput").ap() for k, s in outs.items()}
    build(nc, i, od)
    r = run_bass_kernel_spmd(nc, [{"in_" + k: v for k, v in arr.items()}], core_ids=[0]).results[0]
    y = r["out_yT"].transpose(2, 1, 0).reshape(T, D)
    cn = r["out_new_cn"].transpose(1, 2, 0, 3).reshape(1, 2, HA, HD, VA)
    ssd = r["out_new_ssd"].transpose(2, 0, 3, 1, 4).reshape(1, 2, HC, HD, NS)
    return (y[None, :TP], y[None, TP:], r["out_new_k"].reshape(1, TP, KV, HD), r["out_new_v"].reshape(1, TP, KV, HD),
            np.ascontiguousarray(cn[..., :HD]), np.ascontiguousarray(cn[..., HD]),
            np.ascontiguousarray(r["out_new_m"][:, :, 0].T)[None], ssd)
```
